# Optimizing a Trainium2 kernel written in Bass

```python
import math
import jax
import jax.numpy as jnp
from jax import lax
import numpy as np

D_MODEL = 1024
BATCH = 1
SEQ = 1024
DEPTH = 1

GRID_W = 64
N_META = 16
NA_HEADS = 8
NA_HEAD_DIM = 64
NA_W = NA_HEADS * NA_HEAD_DIM
NA_WIN_ROWS = 8
NA_WIN_COLS = 16
GDN_HEADS = 8
GDN_HEAD_DIM = 128
GDN_W = GDN_HEADS * GDN_HEAD_DIM
GDN_CONV = 5
GDN_CHUNK = 64
N_GROUPS = 4
EXPERTS_PER_GROUP = 8
N_EXPERTS = N_GROUPS * EXPERTS_PER_GROUP
TOP_K = 2
D_EXPERT = 256
EXPERT_BLOCK = 128
LN_EPS = 1e-5
NORM_EPS = 1e-6
DN_ALPHA = (2 * DEPTH) ** 0.25
DN_BETA = (8 * DEPTH) ** -0.25
IN_SPLITS = (NA_W, NA_W, NA_W, GDN_W, GDN_W, GDN_W, GDN_W, GDN_HEADS, GDN_HEADS, GDN_HEADS, GDN_HEADS, D_MODEL, D_MODEL)
D_IN = 3 * NA_W + 4 * GDN_W + 4 * GDN_HEADS + 2 * D_MODEL
VALUE_BLOCKS = (2, 5)

kernel_name = "hybrid_na_gdn_hmoe_encoder_block"

def layer_norm(x, g, b):
    xf = x.astype(jnp.float32)
    xc = xf - jnp.mean(xf, -1, keepdims=True)
    var = jnp.mean(xc * xc, -1, keepdims=True)
    y = xc * lax.rsqrt(var + LN_EPS) * g.astype(jnp.float32) + b.astype(jnp.float32)
    return y.astype(x.dtype)

def l2_normalize(t):
    return t * lax.rsqrt(jnp.sum(t * t, -1, keepdims=True) + NORM_EPS)

def neighbourhood_attention(q, k, v, rpb, keep_meta):
    B, L, H, dh = q.shape
    n = L - N_META
    rows = n // GRID_W
    kr = min(NA_WIN_ROWS, rows)
    kc = NA_WIN_COLS
    scale = dh ** -0.5
    qm, km, vm = q[:, :N_META], k[:, :N_META], v[:, :N_META]
    qg = q[:, N_META:].reshape(B, rows, GRID_W, H, dh)
    kg = k[:, N_META:].reshape(B, rows, GRID_W, H, dh)
    vg = v[:, N_META:].reshape(B, rows, GRID_W, H, dh)
    row_start = np.clip(np.arange(rows) - kr // 2, 0, rows - kr)
    col = np.arange(GRID_W)
    col_start = np.clip(col - kc // 2, 0, GRID_W - kc)
    col_mask = (col[None, :] >= col_start[:, None]) & (col[None, :] < col_start[:, None] + kc)
    dc_idx = np.clip(col[None, :] - col[:, None] + NA_WIN_COLS - 1, 0, 2 * NA_WIN_COLS - 2)

    def row_block(args):
        r, r0, q_r = args
        k_blk = lax.dynamic_slice_in_dim(kg, r0, kr, axis=1)
        v_blk = lax.dynamic_slice_in_dim(vg, r0, kr, axis=1)
        s_win = jnp.einsum('bqhd,bikhd->bhqik', q_r, k_blk, preferred_element_type=jnp.float32) * scale
        dr = r0 + jnp.arange(kr) - r + NA_WIN_ROWS - 1
        bias = rpb[:, dr][:, :, dc_idx].astype(jnp.float32)
        s_win = jnp.where(col_mask[None, None, :, None, :], s_win + bias.transpose(0, 2, 1, 3)[None], -jnp.inf)
        s_meta = jnp.einsum('bqhd,bmhd->bhqm', q_r, km, preferred_element_type=jnp.float32) * scale
        s = jnp.concatenate([s_meta, s_win.reshape(B, H, GRID_W, kr * GRID_W)], axis=-1)
        p = jax.nn.softmax(s, axis=-1).astype(v.dtype)
        p_win = p[..., N_META:].reshape(B, H, GRID_W, kr, GRID_W)
        return (jnp.einsum('bhqm,bmhd->bqhd', p[..., :N_META], vm)
                + jnp.einsum('bhqik,bikhd->bqhd', p_win, v_blk))

    o_rows = lax.map(row_block, (jnp.arange(rows), jnp.asarray(row_start, jnp.int32), qg.transpose(1, 0, 2, 3, 4)))
    o_real = o_rows.transpose(1, 0, 2, 3, 4).reshape(B, n, H, dh)
    if not keep_meta:
        return o_real
    s_mm = jnp.einsum('bqhd,bmhd->bhqm', qm, km, preferred_element_type=jnp.float32) * scale
    o_meta = jnp.einsum('bhqm,bmhd->bqhd', jax.nn.softmax(s_mm, axis=-1).astype(v.dtype), vm)
    return jnp.concatenate([o_meta, o_real], axis=1)

def centred_conv(x, w):
    pad = GDN_CONV // 2
    return lax.conv_general_dilated(x, w[:, None, :].astype(x.dtype), window_strides=(1,),
                                    padding=((pad, pad),), dimension_numbers=('NWC', 'WIO', 'NWC'),
                                    feature_group_count=x.shape[-1])

def chunk_gated_delta(q, k, v, g, beta):
    B, T, H, dk = q.shape
    dv = v.shape[-1]
    C = GDN_CHUNK
    nc = T // C

    def chunks(t):
        return jnp.moveaxis(t.reshape((B, nc, C, H) + t.shape[3:]), 3, 1)

    q, k, v, g, beta = chunks(q), chunks(k), chunks(v), chunks(g), chunks(beta)
    gc = jnp.cumsum(g, axis=-1)
    tri = np.tril(np.ones((C, C), bool))
    strict = np.tril(np.ones((C, C), bool), -1)
    decay = jnp.exp(jnp.where(tri, gc[..., :, None] - gc[..., None, :], -jnp.inf))
    kb = k * beta[..., None]
    m = jnp.where(strict, jnp.einsum('bhnid,bhnjd->bhnij', kb, k) * decay, 0.0)
    rhs = jnp.concatenate([v * beta[..., None], kb * jnp.exp(gc)[..., None]], axis=-1)
    sol = lax.linalg.triangular_solve(jnp.eye(C, dtype=q.dtype) + m, rhs, left_side=True,
                                      lower=True, unit_diagonal=True)
    u, w = sol[..., :dv], sol[..., dv:]
    a_qk = jnp.einsum('bhnid,bhnjd->bhnij', q, k) * decay
    q_dec = q * jnp.exp(gc)[..., None]
    k_dec = k * jnp.exp(gc[..., -1:] - gc)[..., None]
    g_last = jnp.exp(gc[..., -1])
    xs = tuple(jnp.moveaxis(t, 2, 0) for t in (u, w, a_qk, q_dec, k_dec, g_last))

    def step(S, inp):
        u_c, w_c, a_c, qd_c, kd_c, gl_c = inp
        v_new = u_c - jnp.einsum('bhcd,bhde->bhce', w_c, S)
        o_c = jnp.einsum('bhcd,bhde->bhce', qd_c, S) + jnp.einsum('bhij,bhje->bhie', a_c, v_new)
        S = S * gl_c[..., None, None] + jnp.einsum('bhcd,bhce->bhde', kd_c, v_new)
        return S, o_c

    _, o = lax.scan(step, jnp.zeros((B, H, dk, dv), q.dtype), xs)
    return jnp.transpose(o, (1, 0, 3, 2, 4)).reshape(B, T, H, dv)

def lead_meta(t, reverse):
    pad = (-N_META) % GDN_CHUNK
    real = t[:, N_META:]
    if reverse:
        real = jnp.flip(real, axis=1)
    zeros = jnp.zeros((t.shape[0], pad) + t.shape[2:], t.dtype)
    return jnp.concatenate([zeros, t[:, :N_META], real], axis=1)

def restore_order(o, reverse):
    o = o[:, (-N_META) % GDN_CHUNK:]
    if reverse:
        o = jnp.concatenate([o[:, :N_META], jnp.flip(o[:, N_META:], axis=1)], axis=1)
    return o

def gated_deltanet(q, k, v, z, a_f, a_b, b_f, b_b, conv_w, a_log, dt_bias, norm_w, keep_meta):
    B, L, _ = q.shape
    H, dh = GDN_HEADS, GDN_HEAD_DIM
    out_dtype = z.dtype
    qkv = jax.nn.silu(centred_conv(jnp.concatenate([q, k, v], axis=-1), conv_w)).astype(jnp.float32)
    q, k, v = jnp.split(qkv, 3, axis=-1)
    q = l2_normalize(q.reshape(B, L, H, dh)) * (dh ** -0.5)
    k = l2_normalize(k.reshape(B, L, H, dh))
    v = v.reshape(B, L, H, dh)
    o = None
    for d, (a_in, b_in, rev) in enumerate(((a_f, b_f, False), (a_b, b_b, True))):
        g = -jnp.exp(a_log[d].astype(jnp.float32)) * jax.nn.softplus(
            a_in.astype(jnp.float32) + dt_bias[d].astype(jnp.float32))
        beta = jax.nn.sigmoid(b_in.astype(jnp.float32))
        o_d = restore_order(chunk_gated_delta(*(lead_meta(t, rev) for t in (q, k, v, g, beta))), rev)
        o = o_d if o is None else o + o_d
    s = 0 if keep_meta else N_META
    o = o[:, s:]
    zh = z[:, s:].reshape(B, L - s, H, dh).astype(jnp.float32)
    o = o * lax.rsqrt(jnp.mean(o * o, -1, keepdims=True) + NORM_EPS) * norm_w.astype(jnp.float32)
    return (o * jax.nn.silu(zh)).reshape(B, L - s, GDN_W).astype(out_dtype)

def token_mixer(h, w_in, rpb, conv_w, a_log, dt_bias, norm_w, w_na, w_gdn, w_out, keep_meta):
    B, L, _ = h.shape
    offsets = np.cumsum(IN_SPLITS)[:-1].tolist()
    (na_q, na_k, na_v, g_q, g_k, g_v, g_z, a_f, a_b, b_f, b_b,
     gate_na, gate_gdn) = jnp.split(h @ w_in, offsets, axis=-1)
    heads = lambda t: t.reshape(B, L, NA_HEADS, NA_HEAD_DIM)
    o_na = neighbourhood_attention(heads(na_q), heads(na_k), heads(na_v), rpb, keep_meta)
    o_gdn = gated_deltanet(g_q, g_k, g_v, g_z, a_f, a_b, b_f, b_b, conv_w, a_log, dt_bias, norm_w, keep_meta)
    s = 0 if keep_meta else N_META
    y_na = o_na.reshape(B, L - s, NA_W) @ w_na
    y_gdn = o_gdn @ w_gdn
    merged = jax.nn.sigmoid(gate_na[:, s:]) * y_na + jax.nn.sigmoid(gate_gdn[:, s:]) * y_gdn
    return merged @ w_out

def expert_dispatch(xt, e_idx, weights, w_gate, w_up, w_down):
    T, D = xt.shape
    A = T * TOP_K
    flat_e = e_idx.reshape(-1)
    flat_tok = jnp.repeat(jnp.arange(T), TOP_K)
    order = jnp.argsort(flat_e)
    se, stok, sw = flat_e[order], flat_tok[order], weights.reshape(-1)[order]
    counts = jnp.bincount(flat_e, length=N_EXPERTS)
    padded = (counts + EXPERT_BLOCK - 1) // EXPERT_BLOCK * EXPERT_BLOCK
    pad_end = jnp.cumsum(padded)
    start = jnp.cumsum(counts) - counts
    dest = (pad_end - padded)[se] + jnp.arange(A) - start[se]
    n_blocks = -(-(A + N_EXPERTS * (EXPERT_BLOCK - 1)) // EXPERT_BLOCK)
    x_pad = jnp.zeros((n_blocks * EXPERT_BLOCK, D), xt.dtype).at[dest].set(xt[stok])
    block_e = jnp.minimum(jnp.searchsorted(pad_end, jnp.arange(n_blocks) * EXPERT_BLOCK, side='right'),
                          N_EXPERTS - 1)

    def run(args):
        xb, e = args
        hdn = jax.nn.silu(xb @ w_gate[e]) * (xb @ w_up[e])
        return hdn @ w_down[e]

    y_pad = lax.map(run, (x_pad.reshape(n_blocks, EXPERT_BLOCK, D), block_e)).reshape(-1, D)
    return jnp.zeros((T, D), jnp.float32).at[stok].add(y_pad[dest].astype(jnp.float32) * sw[:, None])

def hierarchical_moe(x, w_group, b_group, w_expert, b_expert, w_gate, w_up, w_down):
    B, L, D = x.shape
    xt = x.reshape(-1, D)
    gl = (xt @ w_group).astype(jnp.float32) + b_group.astype(jnp.float32)
    pg = jax.nn.softmax(gl, axis=-1)
    _, g_top = lax.top_k(gl, 1)
    g_idx = g_top[:, 0]
    g_w = jnp.take_along_axis(pg, g_top, axis=-1)[:, 0]
    el = ((xt @ w_expert).astype(jnp.float32) + b_expert.astype(jnp.float32)).reshape(-1, N_GROUPS, EXPERTS_PER_GROUP)
    el_sel = jnp.take_along_axis(el, g_idx[:, None, None], axis=1)[:, 0]
    top_l, top_i = lax.top_k(el_sel, TOP_K)
    top_w = jax.nn.softmax(top_l, axis=-1) * g_w[:, None]
    e_idx = g_idx[:, None] * EXPERTS_PER_GROUP + top_i
    y = expert_dispatch(xt, e_idx, top_w, w_gate, w_up, w_down)
    return y.astype(x.dtype).reshape(B, L, D)

def setup_inputs(seed: int = 0) -> dict:
    key = jax.random.key(seed)
    ks = jax.random.split(key, 24)
    f32 = jnp.float32
    D = D_MODEL
    nrm = lambda k, shape, s: jax.random.normal(k, shape, f32) * s
    col_scale = jnp.asarray(np.concatenate(
        [np.full((w,), DN_BETA if i in VALUE_BLOCKS else 1.0, np.float32) for i, w in enumerate(IN_SPLITS)]))
    dt = jnp.exp(jax.random.uniform(ks[8], (DEPTH, 2, GDN_HEADS), f32, math.log(1e-3), math.log(1e-1)))
    return {
        "x": jax.random.normal(ks[0], (BATCH, SEQ, D), f32),
        "meta_tokens": nrm(ks[1], (N_META, D), 1.0),
        "ln0_g": 1.0 + nrm(ks[2], (D,), 0.02),
        "ln0_b": nrm(ks[3], (D,), 0.02),
        "w_in": nrm(ks[4], (DEPTH, D, D_IN), D ** -0.5) * col_scale,
        "na_rpb": nrm(ks[5], (DEPTH, NA_HEADS, 2 * NA_WIN_ROWS - 1, 2 * NA_WIN_COLS - 1), 0.1),
        "gdn_conv_w": nrm(ks[6], (DEPTH, GDN_CONV, 3 * GDN_W), GDN_CONV ** -0.5),
        "gdn_a_log": jnp.log(jax.random.uniform(ks[7], (DEPTH, 2, GDN_HEADS), f32, 1.0, 16.0)),
        "gdn_dt_bias": dt + jnp.log(-jnp.expm1(-dt)),
        "gdn_norm_w": 1.0 + nrm(ks[9], (DEPTH, GDN_HEAD_DIM), 0.02),
        "w_branch_na": nrm(ks[10], (DEPTH, NA_W, D), NA_W ** -0.5 * DN_BETA),
        "w_branch_gdn": nrm(ks[11], (DEPTH, GDN_W, D), GDN_W ** -0.5 * DN_BETA),
        "w_out": nrm(ks[12], (DEPTH, D, D), D ** -0.5 * DN_BETA),
        "ln1_g": 1.0 + nrm(ks[13], (DEPTH, D), 0.02),
        "ln1_b": nrm(ks[14], (DEPTH, D), 0.02),
        "router_group_w": nrm(ks[15], (DEPTH, D, N_GROUPS), D ** -0.5),
        "router_group_b": nrm(ks[16], (DEPTH, N_GROUPS), 0.01),
        "router_expert_w": nrm(ks[17], (DEPTH, D, N_EXPERTS), D ** -0.5),
        "router_expert_b": nrm(ks[18], (DEPTH, N_EXPERTS), 0.01),
        "expert_w_gate": nrm(ks[19], (DEPTH, N_EXPERTS, D, D_EXPERT), D ** -0.5),
        "expert_w_up": nrm(ks[20], (DEPTH, N_EXPERTS, D, D_EXPERT), D ** -0.5 * DN_BETA),
        "expert_w_down": nrm(ks[21], (DEPTH, N_EXPERTS, D_EXPERT, D), D_EXPERT ** -0.5 * DN_BETA),
        "ln2_g": 1.0 + nrm(ks[22], (DEPTH, D), 0.02),
        "ln2_b": nrm(ks[23], (DEPTH, D), 0.02),
    }

def reference(x, meta_tokens, ln0_g, ln0_b, w_in, na_rpb, gdn_conv_w, gdn_a_log, gdn_dt_bias,
              gdn_norm_w, w_branch_na, w_branch_gdn, w_out, ln1_g, ln1_b, router_group_w,
              router_group_b, router_expert_w, router_expert_b, expert_w_gate, expert_w_up,
              expert_w_down, ln2_g, ln2_b):
    B = x.shape[0]
    meta = jnp.broadcast_to(meta_tokens.astype(x.dtype)[None], (B, N_META, D_MODEL))
    h = layer_norm(jnp.concatenate([meta, x], axis=1), ln0_g, ln0_b)
    for l in range(DEPTH):
        keep_meta = l < DEPTH - 1
        mix = token_mixer(h, w_in[l], na_rpb[l], gdn_conv_w[l], gdn_a_log[l], gdn_dt_bias[l],
                          gdn_norm_w[l], w_branch_na[l], w_branch_gdn[l], w_out[l], keep_meta)
        if not keep_meta:
            h = h[:, N_META:]
        h = layer_norm(DN_ALPHA * h + mix, ln1_g[l], ln1_b[l])
        ffn = hierarchical_moe(h, router_group_w[l], router_group_b[l], router_expert_w[l],
                               router_expert_b[l], expert_w_gate[l], expert_w_up[l], expert_w_down[l])
        h = layer_norm(DN_ALPHA * h + ffn, ln2_g[l], ln2_b[l])
    return h


_drawn_inputs = setup_inputs


def setup_inputs(seed=0):
    import zlib

    import numpy as np

    out = dict(_drawn_inputs(seed))
    spreads = {}
    factors = {'meta_tokens': 5.826,
     'na_rpb': 27.735,
     'gdn_a_log': 2.794,
     'gdn_norm_w': 29.836,
     'w_branch_na': 3.705,
     'ln1_b': 2.739,
     'router_group_b': 47.617,
     'router_expert_b': 28.031,
     'ln2_g': 22.318,
     'ln2_b': 23.094}
    for name, (base, spread) in spreads.items():
        noise = np.random.default_rng([zlib.crc32(name.encode()), seed]).standard_normal(out[name].shape)
        drawn = base * np.exp(spread * noise) if base else spread * noise
        out[name] = jnp.asarray(drawn.astype(out[name].dtype))
    for name, factor in factors.items():
        out[name] = (out[name] * factor).astype(out[name].dtype)
    return out
```

```python
from contextlib import ExitStack

import numpy as np
import concourse.bass as bass
from concourse import mybir

F32 = mybir.dt.float32
I32 = mybir.dt.int32
U32 = mybir.dt.uint32
ALU = mybir.AluOpType
ACT = mybir.ActivationFunctionType
AX = mybir.AxisListType

P = 128
D = 1024
DC = D // P
META = 16
SEQ = 1024
L = META + SEQ
TT = SEQ // P
GRID_W = 64
ROWS = SEQ // GRID_W
KR = 8
KC = 16
NH = 8
NDH = 64
NA_W = NH * NDH
NPAIR = NH // 2
DRS = 15
GH = 8
GD = 128
HALF = 512
WT = 10
WIDE = WT * P
W_META = P - META
STEPS = TT + 1
LEVELS = 7
NG = 4
EPG = 8
NE = NG * EPG
FE = 256
TB = 16 + NE - 1
NBLK = 48
SLOTS = NBLK * P
LN_EPS = 1e-5
NORM_EPS = 1e-6
ALPHA = 2 ** 0.25
BIG = 1e30

_CONST = [("ident", P), ("ones", P), ("incl", 2 * P), ("level", LEVELS * 2 * P), ("last", P),
          ("first", P), ("before", P), ("colmask", GRID_W),
          ("eps", 8), ("blk", NBLK), ("eidx", NE), ("gidx", NG), ("tok", TT)]
C_AT = {}
_n = 0
for _name, _w in _CONST:
    C_AT[_name] = (_n, _n + _w)
    _n += _w
C_W = _n

_COLS = [("ln0_g", DC), ("ln0_b", DC), ("dt", 1), ("alog", 1), ("conv", GH * 15), ("norm_w", 1)]
V_AT = {}
_n = 0
for _name, _w in _COLS:
    V_AT[_name] = (_n, _n + _w)
    _n += _w
V_W = _n


def constants():
    c = np.zeros((P, C_W), np.float32)

    def put(name, a):
        a0, a1 = C_AT[name]
        c[:, a0:a1] = np.asarray(a, np.float32).reshape(P, a1 - a0)

    i = np.arange(P)
    part, free = i[:, None], i[None, :]
    put("ident", np.eye(P))
    put("ones", np.ones((P, P)))
    put("incl", np.stack([free >= part, free <= part], 1))
    lev = []
    for s in range(LEVELS):
        same = (part >> (s + 1)) == (free >> (s + 1))
        hi, lo = (i >> s) & 1 == 1, (i >> s) & 1 == 0
        lev += [same & lo[:, None] & hi[None, :], same & hi[:, None] & lo[None, :]]
    put("level", np.stack(lev, 1))
    put("last", np.repeat(part == P - 1, P, 1))
    put("first", np.repeat(part == 0, P, 1))
    put("before", part < free)
    col = np.arange(GRID_W)
    start = np.clip(col - KC // 2, 0, GRID_W - KC)
    inside = (col[None, :] >= start[:, None]) & (col[None, :] < start[:, None] + KC)
    put("colmask", np.tile(np.where(inside, 0.0, -BIG), (2, 1)))
    put("eps", np.tile([LN_EPS, 4 * NORM_EPS, NORM_EPS, -0.5 * np.log(GD), 0, 0, 0, 0], (P, 1)))
    put("blk", np.tile(np.arange(NBLK), (P, 1)))
    put("eidx", np.tile(np.arange(NE), (P, 1)))
    put("gidx", np.tile(np.arange(NG), (P, 1)))
    put("tok", part + P * np.arange(TT)[None, :])
    return c


def scan_masks():
    w = np.arange(WIDE)
    return np.tile(np.stack([w % P != 0, w % P != P - 1]).astype(np.float32), (P, 1, 1))


def meet(eng, on, value, mark):
    eng.wait_ge(on, value)
    eng.sem_inc(mark, 1)


def makers(nc, ctx, prefix):
    taken = []

    def sem(n):
        taken.append(nc.alloc_semaphore(f"{prefix}_{n}"))
        return taken[-1]

    def clear():
        nc.clear_and_free_semaphores(taken)
        nc.all_engine_barrier()

    ctx.callback(clear)
    sb = lambda n, s, dt=F32: ctx.enter_context(nc.sbuf_tensor(f"{prefix}_{n}", s, dt))
    ps = lambda n, s: ctx.enter_context(nc.psum_tensor(f"{prefix}_{n}", s, F32))
    return sb, ps, sem


def input_norm(nc, io, keep):
    hT, con, colv, tab = keep["hT"], keep["con"], keep["colv"], keep["tab"]
    with ExitStack() as ctx:
        sb, ps, sem = makers(nc, ctx, "norm0")
        C = lambda n, *s: con[:, C_AT[n][0]:C_AT[n][1]]
        V = lambda n: colv[:, V_AT[n][0]:V_AT[n][1]]
        x = sb("x_rows", [P, 2, D])
        stats = sb("stats", [P, 2, 12])
        mv = sb("mean_var", [P, 2, 4])
        wg = sb("w_gates", [P, DC, P])
        arg = sb("gate_arg", [P, L])
        mag = sb("gate_mag", [P, L])
        soft = sb("gate_soft", [P, L])
        nega = sb("neg_decay", [P, 1])
        g = sb("log_decay", [P, WIDE])
        rows = sb("gate_rows", [P, WIDE])
        scan = sb("scan_masks", [P, 2, WIDE])
        colr = sb("gate_cols", [P, WT, P])
        ends = sb("gate_ends", [P, 2, WT, GH])
        xp = [ps(f"xT{k}", [P, 4, P]) for k in range(2)]
        gp = [ps(f"gates{k}", [P, HALF]) for k in range(2)]
        gm = ps("gates_meta", [P, HALF])
        tp = ps("rows_T", [P, 4, P])
        lp = ps("ends_all", [P, 2, WT, GH])

        const_in, xn_out = sem("const_in"), [sem(f"xn_out{k}") for k in range(2)]
        x_in = [sem(f"x_in{k}") for k in range(2)]
        stat, rstd, normed = sem("stat"), sem("rstd"), sem("normed")
        turned, h_dve, h_act = sem("turned"), sem("h_dve"), sem("h_act")
        gated, g_dve, g_act = sem("gated"), sem("g_dve"), sem("g_act")
        rows_T, rows_copied, rows_out = sem("rows_T_done"), sem("rows_copied"), sem("rows_out")
        zeroed = sem("zeroed")
        held, met = sem("held"), sem("met")
        block = ctx.enter_context(nc.Block())

        @block.sync
        def _(sp):
            sp.dma_start(con[:, :], io["const"]).then_inc(const_in, 16)
            sp.dma_start(colv[:, :], io["cols"]).then_inc(const_in, 16)
            sp.dma_start(wg[:, :, :], io["w_gates"]).then_inc(const_in, 16)
            sp.dma_start(scan[:, :, :], io["scan"]).then_inc(const_in, 16)
            sp.dma_start(x[0:META, 0, :], io["meta"]).then_inc(x_in[0], 16)

            with sp.Fori(0, TT // 2) as i:
                row = [sp.snap((2 * i + k) * P) for k in range(2)]
                for k in range(2):
                    meet(sp, xn_out[1 - k], 16 * i, met)
                    sp.wait_ge(turned, 4 * i + 2 * k)
                    sp.dma_start(x[:, 1 - k, :], io["x"][bass.ds(row[k], P), :]).then_inc(x_in[1 - k], 16)
                for k in range(2):
                    sp.wait_ge(normed, 2 * i + 2 + k)
                    sp.dma_start(io["xn"][bass.ds(row[k], P), :], x[:, 1 - k, :]).then_inc(xn_out[1 - k], 16)
            for k, (name, lo) in enumerate((("f", 0), ("b", 32))):
                for kind, at in ((0, lo), (1, 64 + lo)):
                    for hp in range(GH // 2):
                        for hh in range(2):
                            p = at + 2 * hp + hh
                            src = rows[p:p + 1, :].rearrange("a (t c) -> a t c", c=P)
                            src = src[:, 0:STEPS, :] if k == 0 else src[:, WT - 1:0:-1, :]
                            if hp == 0 and hh == 0 and kind == 0 and k == 0:
                                sp.wait_ge(g_dve, 13)
                            sp.dma_start(io["rows"][hp:hp + 1, :, hh, k, kind, :], src).then_inc(rows_out, 16)
            sp.wait_ge(rows_out, 16 * 32)
            for k in range(2):
                sp.wait_ge(xn_out[k], 16 * (TT // 2))

        @block.vector
        def _(v):
            def unit(u, slot, n, loads):
                v.wait_ge(x_in[slot], 16 * loads)
                for k in range(2):
                    v.bn_stats(stats[0:n, slot, 6 * k:6 * k + 6], x[0:n, slot, HALF * k:HALF * k + HALF]).then_inc(stat, 1)
                meet(v, stat, 3 * u + 2, held)
                v.bn_aggr(mv[0:n, slot, 0:2], stats[0:n, slot, :]).then_inc(stat, 1)
                v.wait_ge(rstd, 2 * u + 2)
                v.tensor_scalar(x[0:n, slot, :], x[0:n, slot, :], mv[0:n, slot, 0:1], mv[0:n, slot, 3:4],
                                ALU.subtract, ALU.mult).then_inc(normed, 1)

            def spread(u, n):
                v.wait_ge(turned, 2 * u + 1)
                for c in range(4):
                    at = (u - 1) * P + META if n == P else 0
                    v.tensor_scalar(hT[:, c, bass.ds(at, n)], xp[0][:, c, 0:n], V("ln0_g")[:, c:c + 1],
                                    V("ln0_b")[:, c:c + 1], ALU.mult, ALU.add).then_inc(h_dve, 1)

            v.memset(rows[:, :], 0.0).then_inc(zeroed, 1)
            v.memset(g[:, :], 0.0).then_inc(zeroed, 1)
            v.wait_ge(const_in, 64)
            unit(0, 0, META, 1)
            spread(0, META)
            with v.Fori(0, TT // 2) as i:
                for k in range(2):
                    unit(2 * i + 1 + k, 1 - k, P, i + 1 + k)
                    spread(2 * i + 1 + k, P)
            v.wait_ge(gated, 1)
            for k, (bank, a, b) in enumerate(((gm[:, 0:META], 0, META), (gp[0][:, :], META, META + HALF),
                                              (gp[1][:, :], META + HALF, L))):
                v.tensor_scalar(arg[:, a:b], bank, V("dt"), None, ALU.add).then_inc(g_dve, 1)
            v.wait_ge(g_dve, 3)
            v.scalar_tensor_tensor(mag[:, :], arg[:, :], -1.0, arg[:, :], ALU.mult, ALU.max).then_inc(g_dve, 1)
            v.wait_ge(g_act, 3)
            v.scalar_tensor_tensor(soft[0:64, :], arg[0:64, :], 0.0, mag[0:64, :], ALU.max, ALU.add).then_inc(g_dve, 1)
            v.tensor_scalar(nega[:, :], nega[:, :], -1.0, None, ALU.mult).then_inc(g_dve, 1)
            v.scalar_tensor_tensor(soft[64:P, :], arg[64:P, :], 0.0, mag[64:P, :], ALU.min, ALU.subtract).then_inc(g_dve, 1)
            v.wait_ge(g_dve, 7)
            v.wait_ge(zeroed, 2)
            v.tensor_scalar(g[0:64, W_META:W_META + L], soft[0:64, :], nega[0:64, :], None, ALU.mult).then_inc(g_dve, 1)
            v.tensor_scalar(g[0:64, (WT - 1) * P:(WT - 1) * P + META], soft[0:64, 0:META][:, ::-1],
                            nega[0:64, :], None, ALU.mult).then_inc(g_dve, 1)
            v.wait_ge(g_act, 5)
            v.tensor_copy(rows[96:P, (WT - 1) * P:(WT - 1) * P + META], rows[96:P, W_META:P][:, ::-1]).then_inc(g_dve, 1)
            v.wait_ge(g_dve, 9)
            v.tensor_tensor_scan(rows[0:32, 0:(WT - 1) * P], scan[0:32, 0, 0:(WT - 1) * P], g[0:32, 0:(WT - 1) * P],
                                 0.0, ALU.mult, ALU.add).then_inc(g_dve, 1)
            v.tensor_tensor_scan(rows[32:64, P:WIDE][:, ::-1], scan[32:64, 1, P:WIDE][:, ::-1],
                                 g[32:64, P:WIDE][:, ::-1], 0.0, ALU.mult, ALU.add).then_inc(g_dve, 1)
            v.wait_ge(g_dve, 12)
            v.wait_ge(g_act, 5)
            v.memset(ends[:, :, :, :], 0.0).then_inc(g_dve, 1)
            for b, t0, n in ((0, 0, 4), (1, 4, 4), (2, 8, 2)):
                v.wait_ge(rows_T, b + 1)
                v.tensor_copy(colr[:, t0:t0 + n, :], tp[:, 0:n, :]).then_inc(rows_copied, 1)
            v.wait_ge(rows_T, 4)
            v.wait_ge(g_dve, 13)
            v.tensor_copy(ends[:, :, :, :], lp[:, :, :, :]).then_inc(g_dve, 1)
            v.wait_ge(g_dve, 14)
            last = 14
            for d, tiles in ((0, slice(0, STEPS)), (1, slice(WT - 1, 0, -1))):
                e = ends[:, d, tiles, :]
                col = colr[:, tiles, 32 * d:32 * d + GH]
                bet = colr[:, tiles, 64 + 32 * d:64 + 32 * d + GH]
                split = lambda a: a.rearrange("p s (q h) -> p q s h", h=2)
                for q in range(GH // 2):
                    t = lambda kind: tab[:, q, :, :, d, kind]
                    s = slice(2 * q, 2 * q + 2)
                    v.tensor_copy(t(0), col[:, :, s]).then_inc(g_dve, 1)
                    v.tensor_scalar(t(1), bet[:, :, s], 0.5, None, ALU.mult).then_inc(g_dve, 1)
                    v.tensor_copy(t(2), col[:, :, s]).then_inc(g_dve, 1)
                    v.tensor_tensor(t(3), e[:, :, s], col[:, :, s], ALU.subtract).then_inc(g_dve, 1)
                    v.tensor_copy(t(4), e[:, :, s]).then_inc(g_dve, 1)
            v.wait_ge(g_act, 6)
            for d, tiles in ((0, slice(0, STEPS)), (1, slice(WT - 1, 0, -1))):
                bet = colr[:, tiles, 64 + 32 * d:64 + 32 * d + GH]
                for q in range(GH // 2):
                    t = tab[:, q, :, :, d, 2]
                    v.tensor_tensor(t, t, bet[:, :, 2 * q:2 * q + 2], ALU.mult).then_inc(g_dve, 1)

        @block.scalar
        def _(act):
            def unit(u, slot, n):
                act.wait_ge(stat, 3 * u + 3)
                act.activation(mv[0:n, slot, 2:3], mv[0:n, slot, 1:2], ACT.Ln, bias=C("eps")[0:n, 0:1]).then_inc(rstd, 1)
                act.wait_ge(rstd, 2 * u + 1)
                act.activation(mv[0:n, slot, 3:4], mv[0:n, slot, 2:3], ACT.Exp, scale=-0.5).then_inc(rstd, 1)

            def spread(u, n):
                act.wait_ge(turned, 2 * u + 2)
                for c in range(4):
                    at = (u - 1) * P + META if n == P else 0
                    act.activation(hT[:, 4 + c, bass.ds(at, n)], xp[1][:, c, 0:n], ACT.Identity,
                                   bias=V("ln0_b")[:, 4 + c:5 + c], scale=V("ln0_g")[:, 4 + c:5 + c]).then_inc(h_act, 1)

            act.wait_ge(const_in, 64)
            unit(0, 0, META)
            spread(0, META)
            with act.Fori(0, TT // 2) as i:
                for k in range(2):
                    unit(2 * i + 1 + k, 1 - k, P)
                    spread(2 * i + 1 + k, P)
            act.activation(nega[:, :], V("alog"), ACT.Exp).then_inc(g_act, 1)
            act.wait_ge(g_dve, 4)
            act.activation(mag[:, :], mag[:, :], ACT.Exp, scale=-1.0).then_inc(g_act, 1)
            act.wait_ge(g_act, 2)
            act.activation(mag[:, :], mag[:, :], ACT.Ln, bias=1.0).then_inc(g_act, 1)
            act.wait_ge(g_dve, 7)
            act.wait_ge(zeroed, 2)
            for p in (64, 96):
                act.activation(rows[p:p + 32, W_META:W_META + L], soft[p:p + 32, :], ACT.Exp).then_inc(g_act, 1)
            act.wait_ge(g_dve, 14 + 10 * (GH // 2))
            act.activation(tab[:, :, :, :, :, 2:5].rearrange("p q s h d k -> p (q s h d) k"),
                           tab[:, :, :, :, :, 2:5].rearrange("p q s h d k -> p (q s h d) k"), ACT.Exp).then_inc(g_act, 1)

        @block.tensor
        def _(pe):
            ident = C("ident")

            def unit(u, slot, n):
                pe.wait_ge(normed, u + 1)
                for k, read in ((0, h_dve), (1, h_act)):
                    pe.wait_ge(read, 4 * u)
                    for c in range(4):
                        cc = 4 * k + c
                        ins = pe.transpose(xp[k][:, c, 0:n], x[0:n, slot, cc * P:cc * P + P], ident[0:n, 0:n])
                    ins.then_inc(turned, 1)

            pe.wait_ge(const_in, 64)
            unit(0, 0, META)
            with pe.Fori(0, TT // 2) as i:
                for k in range(2):
                    unit(2 * i + 1 + k, 1 - k, P)
            pe.wait_ge(h_dve, 4 * STEPS)
            pe.wait_ge(h_act, 4 * STEPS)
            for bank, a, n in ((gm, 0, META), (gp[0], META, HALF), (gp[1], META + HALF, HALF)):
                for c in range(DC):
                    ins = pe.matmul(bank[:, 0:n], wg[:, c, :], hT[:, c, a:a + n], start=(c == 0), stop=(c == DC - 1))
            ins.then_inc(gated, 1)
            pe.wait_ge(g_dve, 12)
            pe.wait_ge(g_act, 5)
            for b, t0, n in ((0, 0, 4), (1, 4, 4), (2, 8, 2)):
                pe.wait_ge(rows_copied, b)
                for t in range(n):
                    ins = pe.transpose(tp[:, t, :], rows[:, (t0 + t) * P:(t0 + t + 1) * P], ident)
                ins.then_inc(rows_T, 1)
            pe.wait_ge(rows_copied, 3)
            pe.matmul(lp[:, 0, :, :], C("last"), colr[:, :, 0:GH], start=True, stop=True, skip_group_check=True)
            pe.matmul(lp[:, 1, :, :], C("first"), colr[:, :, 32:32 + GH], start=True, stop=True,
                      skip_group_check=True).then_inc(rows_T, 1)


def neighbourhood(nc, io, keep):
    hT, con = keep["hT"], keep["con"]
    with ExitStack() as ctx:
        sb, ps, sem = makers(nc, ctx, "na")
        ident = con[:, C_AT["ident"][0]:C_AT["ident"][1]]
        colmask = con[:, C_AT["colmask"][0]:C_AT["colmask"][1]]
        WIN = KR * GRID_W
        SCALE = NDH ** -0.5
        first_row = [min(max(r - KR // 2, 0), ROWS - KR) for r in range(ROWS)]
        first_bias = [first_row[r] - r + KR - 1 for r in range(ROWS)]
        v_from = [0] + [META + P * m for m in range(TT)] + [META + GRID_W + P * m for m in range(TT - 1)]
        v_tile = lambda row, j: 1 + row // 2 + j if row % 2 == 0 else 1 + TT + row // 2 + j

        w = sb("w_qkv", [P, DC, 3, P])
        bias = sb("bias", [P, DRS, GRID_W])
        qb = sb("q_blocks", [P, ROWS, P])
        kT = sb("kT", [P, L])
        vT = sb("vT", [P, L])
        vt = sb("v_tiles", [P, 2 * TT, P])
        s_ = sb("scores", [P, 2, META + WIN])
        nm = sb("minus_max", [P, 2])
        sm = sb("exp_sum", [P, 2])
        rs = sb("one_over_sum", [P, 2])
        pt = sb("probs_T", [P, 2, WIN])
        ptm = sb("probs_meta_T", [META, 2, P])
        on = sb("o_heads", [P, SEQ])
        bank = [ps(f"bank{k}", [P, HALF]) for k in range(8)]

        w_in, bias_in, bias_ok, q_zero = sem("w_qkv_in"), sem("bias_in"), sem("bias_masked"), sem("q_blocks_zero")
        proj, qkv_in, v_turned, vt_in = sem("projected"), sem("qkv_in"), sem("v_turned"), sem("v_tiles_in")
        scored, biased, maxed, exped = sem("scored"), sem("biased"), sem("maxed"), sem("exp_done")
        inv, normed, p_turned, pt_in = sem("one_over_sum_made"), sem("probs_normed"), sem("probs_turned"), sem("probs_T_in")
        pv, o_in, ona_out = sem("values_weighted"), sem("o_in"), sem("ona_out")
        block = ctx.enter_context(nc.Block())

        @block.sync
        def _(sp):
            with sp.Fori(0, NPAIR) as p:
                sp.wait_ge(proj, p * 3)
                sp.dma_start(w[:, :, :, :], io["w_na3"][bass.ds(p, 1), :, :, :, :]
                             .rearrange("a p c m n -> p (a c) m n")).then_inc(w_in, 16)
                sp.wait_ge(biased, p * ROWS)
                sp.dma_start(bias[:, :, :], io["bias"][bass.ds(p, 1), :, :, :]
                             .rearrange("a p r c -> p (a r) c")).then_inc(bias_in, 16)
                sp.wait_ge(o_in, p * ROWS + ROWS)
                sp.dma_start(io["ona"][bass.ds(p, 1), :, :].rearrange("a p t -> (a p) t"), on[:, :]).then_inc(ona_out, 16)
            sp.wait_ge(ona_out, 16 * NPAIR)

        @block.tensor
        def _(pe):
            with pe.Fori(0, NPAIR) as p:
                at = lambda r: p * ROWS + r
                pe.wait_ge(w_in, p * 16 + 16)
                pe.wait_ge(o_in, p * ROWS)
                for m in range(3):
                    for c in range(DC):
                        first, final = c == 0, c == DC - 1
                        if m:
                            pe.matmul(bank[5 + m][:, 0:META], w[:, c, m, :], hT[:, c, 0:META], start=first, stop=final)
                        for k in range(2):
                            ins = pe.matmul(bank[2 * m + k][:, :], w[:, c, m, :],
                                            hT[:, c, META + HALF * k:META + HALF * (k + 1)], start=first, stop=final)
                    ins.then_inc(proj, 1)
                pe.wait_ge(qkv_in, p * 3 + 3)
                for b in range(4):
                    pe.wait_ge(vt_in, p * 4 + max(b - 1, 0))
                    for j in range(4):
                        i = 4 * b + j
                        n = P if i else META
                        ins = pe.transpose(bank[6 + b % 2][0:n, P * j:P * j + P], vT[:, v_from[i]:v_from[i] + n], ident)
                    ins.then_inc(v_turned, 1)
                for r in range(ROWS + 2):
                    if r < ROWS:
                        pe.wait_ge(biased, at(max(r - 1, 0)))
                        k0 = META + GRID_W * first_row[r]
                        pe.matmul(bank[r % 2][:, :], qb[:, r, :], kT[:, k0:k0 + WIN], start=True, stop=True)
                        pe.matmul(bank[2 + r % 2][:, 0:META], qb[:, r, :], kT[:, 0:META], start=True,
                                  stop=True).then_inc(scored, 1)
                    if 1 <= r <= ROWS:
                        q = r - 1
                        pe.wait_ge(normed, at(q) + 1)
                        pe.wait_ge(pt_in, at(q))
                        if q == 0:
                            pe.wait_ge(vt_in, p * 4 + 4)
                        for j in range(4):
                            pe.transpose(bank[4 + q % 2][:, P * j:P * j + P], s_[:, q % 2, META + P * j:META + P * j + P], ident)
                        pe.transpose(bank[6][0:META, 0:P], s_[:, q % 2, 0:META], ident).then_inc(p_turned, 1)
                    if r >= 2:
                        q = r - 2
                        pe.wait_ge(pt_in, at(q) + 1)
                        pe.wait_ge(o_in, at(q))
                        pe.matmul(bank[7][:, 0:P], vt[0:META, 0, :], ptm[:, q % 2, :], start=True, stop=False)
                        for j in range(4):
                            ins = pe.matmul(bank[7][:, 0:P], vt[:, v_tile(first_row[q], j), :],
                                            pt[:, q % 2, P * j:P * j + P], start=False, stop=(j == 3))
                        ins.then_inc(pv, 1)

        @block.scalar
        def _(act):
            with act.Fori(0, NPAIR) as p:
                at = lambda r: p * ROWS + r
                act.wait_ge(proj, p * 3 + 1)
                act.wait_ge(q_zero, 1)
                for k in range(2):
                    rows = slice(ROWS // 2 * k, ROWS // 2 * (k + 1))
                    src = bank[k][:, :].rearrange("p (r c) -> p r c", c=GRID_W)
                    act.activation(qb[0:NDH, rows, 0:GRID_W], src[0:NDH, :, :], ACT.Copy)
                    ins = act.activation(qb[NDH:P, rows, GRID_W:P], src[NDH:P, :, :], ACT.Copy)
                ins.then_inc(qkv_in, 1)
                for m, dst in ((1, kT), (2, vT)):
                    act.wait_ge(proj, p * 3 + m + 1)
                    act.activation(dst[:, 0:META], bank[5 + m][:, 0:META], ACT.Copy)
                    for k in range(2):
                        ins = act.activation(dst[:, META + HALF * k:META + HALF * (k + 1)], bank[2 * m + k][:, :], ACT.Copy)
                    ins.then_inc(qkv_in, 1)
                for b in range(4):
                    act.wait_ge(v_turned, p * 4 + b + 1)
                    if b == 0:
                        act.activation(vt[0:META, 0, :], bank[6][0:META, 0:P], ACT.Copy)
                    lo = 1 if b == 0 else 0
                    act.activation(vt[:, 4 * b + lo:4 * b + 4, :], bank[6 + b % 2][:, P * lo:4 * P]
                                   .rearrange("p (j c) -> p j c", c=P), ACT.Copy).then_inc(vt_in, 1)
                for r in range(ROWS + 1):
                    if r < ROWS:
                        act.wait_ge(maxed, at(r) + 1)
                        act.wait_ge(inv, at(max(r - 1, 0)))
                        act.activation(s_[:, r % 2, :], s_[:, r % 2, :], ACT.Exp, bias=nm[:, r % 2:r % 2 + 1],
                                       accum_out=sm[:, r % 2:r % 2 + 1]).then_inc(exped, 1)
                    if r >= 1:
                        q = r - 1
                        act.wait_ge(p_turned, at(q) + 1)
                        act.wait_ge(pv, at(max(q - 1, 0)))
                        act.activation(pt[:, q % 2, :], bank[4 + q % 2][:, :], ACT.Copy)
                        act.activation(ptm[:, q % 2, :], bank[6][0:META, 0:P], ACT.Copy).then_inc(pt_in, 1)

        @block.vector
        def _(v):
            v.memset(qb[:, :, :], 0.0).then_inc(q_zero, 1)
            with v.Fori(0, NPAIR) as p:
                at = lambda r: p * ROWS + r
                v.wait_ge(bias_in, p * 16 + 16)
                v.tensor_tensor(bias[:, :, :], bias[:, :, :], colmask.unsqueeze(1).to_broadcast([P, DRS, GRID_W]),
                                ALU.add).then_inc(bias_ok, 1)
                v.wait_ge(bias_ok, p + 1)
                for r in range(ROWS + 3):
                    if r < ROWS:
                        v.wait_ge(scored, at(r) + 1)
                        v.wait_ge(p_turned, at(max(r - 1, 0)))
                        v.scalar_tensor_tensor(s_[:, r % 2, META:META + WIN], bank[r % 2][:, :], SCALE,
                                               bias[:, first_bias[r]:first_bias[r] + KR, :].rearrange("p r c -> p (r c)"),
                                               ALU.mult, ALU.add)
                        v.tensor_scalar(s_[:, r % 2, 0:META], bank[2 + r % 2][:, 0:META], SCALE, None, ALU.mult).then_inc(biased, 1)
                        v.wait_ge(biased, at(r) + 1)
                        v.wait_ge(exped, at(max(r - 1, 0)))
                        v.tensor_reduce(nm[:, r % 2:r % 2 + 1], s_[:, r % 2, :], AX.X, ALU.max, negate=True).then_inc(maxed, 1)
                    if 1 <= r <= ROWS:
                        q = r - 1
                        v.wait_ge(exped, at(q) + 1)
                        v.wait_ge(normed, at(max(q - 1, 0)))
                        v.reciprocal(rs[:, q % 2:q % 2 + 1], sm[:, q % 2:q % 2 + 1]).then_inc(inv, 1)
                        v.wait_ge(inv, at(q) + 1)
                        v.tensor_scalar(s_[:, q % 2, :], s_[:, q % 2, :], rs[:, q % 2:q % 2 + 1], None, ALU.mult).then_inc(normed, 1)
                    if r >= 3:
                        q = r - 3
                        v.wait_ge(pv, at(q) + 1)
                        if q == 0:
                            v.wait_ge(ona_out, p * 16)
                        for h in range(2):
                            a = NDH * h
                            ins = v.tensor_copy(on[a:a + NDH, GRID_W * q:GRID_W * (q + 1)], bank[7][a:a + NDH, a:a + NDH])
                        ins.then_inc(o_in, 1)


def deltanet(nc, io, keep):
    hT, con, colv, tab = keep["hT"], keep["con"], keep["colv"], keep["tab"]
    NI = 4
    with ExitStack() as ctx:
        sb, ps, sem = makers(nc, ctx, "gdn")
        C = lambda n: con[:, C_AT[n][0]:C_AT[n][1]]
        V = lambda n: colv[:, V_AT[n][0]:V_AT[n][1]]
        ident = C("ident")
        ident4 = ident.unsqueeze(1).to_broadcast([P, NI, P])
        incl = C("incl").rearrange("p (d t) -> p d t", d=2).unsqueeze(1).to_broadcast([P, 2, 2, P])
        level = lambda k: C("level").rearrange("p (l d t) -> p l d t", l=LEVELS, d=2)[:, k, :, :]\
            .unsqueeze(1).to_broadcast([P, 2, 2, P])
        by_dir = lambda a: a.rearrange("p (h d) t -> p h d t", d=2)

        w = sb("w_head", [P, DC, 4, P])
        raw = sb("raw", [P, 3, L + 4])
        acc = sb("conv_sum", [P, 3, L])
        th = sb("tanh", [P, 2, L])
        wide = sb("wide", [P, 2, 3, WIDE])
        zb = sb("z_gate", [P, 2, SEQ])
        ot = sb("o_scan", [P, 2, 2, STEPS * P])
        rows = sb("decay_beta_rows", [P, NI, 2, P])
        kqv = sb("kqv", [P, NI, 3, P])
        tc = sb("tile_cols", [P, NI, 5])
        dd = sb("decays", [P, NI, P])
        mt = sb("M_T", [P, NI, P])
        at = sb("A_T", [P, NI, P])
        ml = sb("M_level_T", [P, 4, NI, P])
        t_ = sb("T", [P, NI, P])
        tt = sb("T_T", [P, NI, P])
        x_ = sb("M_T_product", [P, NI, P])
        kbe = sb("k_beta_decay", [P, NI, P])
        kde = sb("k_to_end", [P, NI, P])
        vb = sb("v_beta", [P, NI, P])
        eq = sb("q_decay", [P, NI, P])
        qd = sb("q_decayed", [P, NI, P])
        wtn = sb("minus_W_T", [P, NI, P])
        vn = sb("v_new", [P, NI, P])
        st = sb("state", [P, NI, P])
        bank = [ps(f"bank{k}", [P, NI, P]) for k in range(8)]
        flat = lambda b: bank[b][:, :, :].rearrange("p a b -> p (a b)")
        G0, G1, KB, VB, XB, P1B, P2B, RB = range(8)

        pads = sem("pads_zero")
        w_in, proj, raw_in, conv = sem("w_head_in"), sem("projected"), sem("raw_in"), sem("conv_step")
        tanhd, silu, squared, ssq = sem("tanh_done"), sem("silu_done"), sem("squared"), sem("square_sums")
        rn, wide_in, back_in = sem("reciprocal_norms"), sem("wide_in"), sem("meta_reversed")
        rows_in, kqv_in, tc_in = sem("rows_in"), sem("kqv_in"), sem("tile_cols_in")
        gram, turned = sem("gram"), sem("k_v_turned")
        dd_d, dd_e, dd_m = sem("decay_differences"), sem("decays_done"), sem("decays_masked")
        mt_d, at_d, mt_b, ml_d = sem("M_T_made"), sem("A_T_made"), sem("M_T_beta"), sem("M_level_made")
        xs, p1s, p2s = sem("MT_product"), sem("T_MT_product"), sem("transposed_product")
        tt0, t_up, tt_up, x_cp = sem("T_T_started"), sem("T_updated"), sem("T_T_updated"), sem("product_copied")
        kbe_d, kde_d, vb_d = sem("k_beta_decay_made"), sem("k_to_end_made"), sem("v_beta_made")
        eq_d, qd_d, pw, wtn_d = sem("q_decay_made"), sem("q_decayed_made"), sem("W_T"), sem("minus_W_T_made")
        vnp, vn_d, op, o_cp = sem("v_new_sum"), sem("v_new_made"), sem("o_sum"), sem("o_copied")
        sps, s_up, s_zero = sem("state_sum"), sem("state_updated"), sem("state_zero")
        o_add, o_sq, o_ssq, o_rn = sem("o_added"), sem("o_squared"), sem("o_square_sums"), sem("o_rms")
        o_gated, og_out, met, held = sem("o_gated"), sem("og_out"), sem("met"), sem("held")
        block = ctx.enter_context(nc.Block())

        @block.sync
        def _(sp):
            with sp.Fori(0, NPAIR) as p:
                with sp.Fori(0, 2) as hh:
                    hd = p * 2 + hh
                    sp.wait_ge(proj, hd * 4)
                    sp.dma_start(w[:, :, :, :], io["w_gdn"][bass.ds(hd, 1), :, :, :, :]
                                 .rearrange("a p c m n -> p (a c) m n")).then_inc(w_in, 16)
                with sp.Fori(0, STEPS) as s:
                    u = p * STEPS + s
                    for used in (dd_d, eq_d):
                        meet(sp, used, u, met)
                    sp.wait_ge(mt_b, u)
                    src = io["rows"].rearrange("q s h d k t -> (q s) (h d k t)")[bass.ds(u, 1), :]
                    sp.dma_start(rows[:, :, :, :].rearrange("p i k t -> p (i k t)"),
                                 src.to_broadcast([P, NI * 2 * P])).then_inc(rows_in, 16)
                with sp.Fori(0, 2) as hh:
                    hd = p * 2 + hh
                    sp.wait_ge(o_gated, hd * 2 + 2)
                    sp.dma_start(io["og"][bass.ds(hd, 1), :, :].rearrange("a p t -> (a p) t"),
                                 acc[:, 0, 0:SEQ]).then_inc(og_out, 16)
            sp.wait_ge(og_out, 16 * GH)

        @block.tensor
        def _(pe):
            ones = C("ones")

            def head(p, hd):
                pe.wait_ge(w_in, hd * 16 + 16)
                pe.wait_ge(s_up, p * STEPS)
                pe.wait_ge(o_rn, p * 4)
                pe.wait_ge(rn, hd * 4)
                for m in range(4):
                    b = 2 * (m % 2)
                    pe.wait_ge(raw_in, hd * 4 + max(m - 1, 0))
                    for c in range(DC):
                        first, final = c == 0, c == DC - 1
                        if m < 3:
                            pe.matmul(flat(XB + m % 2)[:, 0:META], w[:, c, m, :], hT[:, c, 0:META], start=first, stop=final)
                        for k in range(2):
                            ins = pe.matmul(flat(b + k), w[:, c, m, :], hT[:, c, META + HALF * k:META + HALF * (k + 1)],
                                            start=first, stop=final)
                    ins.then_inc(proj, 1)
                for m in range(2):
                    pe.wait_ge(squared, hd * 2 + m + 1)
                    pe.wait_ge(rn, hd * 4 + m)
                    pe.wait_ge(raw_in, hd * 4 + 4)
                    pe.matmul(flat(XB + m)[:, 0:META], ones, raw[:, m, 0:META], start=True, stop=True)
                    for k in range(2):
                        ins = pe.matmul(flat(P2B + k), ones, raw[:, m, META + HALF * k:META + HALF * (k + 1)],
                                        start=True, stop=True)
                    ins.then_inc(ssq, 1)

            def step(u):
                each = range(NI)
                pe.wait_ge(kqv_in, u + 1)
                pe.wait_ge(at_d, u)
                for j in each:
                    ins = pe.matmul(bank[G0 + j // 2][:, 2 * (j % 2):2 * (j % 2) + 2, :], kqv[:, j, 0, :],
                                    kqv[:, j, 0:2, :], start=True, stop=True, skip_group_check=True)
                ins.then_inc(gram, 1)
                for m, b, read in ((0, KB, kde_d), (2, VB, vb_d)):
                    pe.wait_ge(read, u)
                    for j in each:
                        ins = pe.transpose(bank[b][:, j, :], kqv[:, j, m, :], ident)
                    ins.then_inc(turned, 1)
                pe.wait_ge(vn_d, u)
                for k in range(LEVELS):
                    pe.wait_ge(ml_d, u * LEVELS + k + 1)
                    if k:
                        pe.wait_ge(t_up, u * (LEVELS - 1) + k)
                    for j in each:
                        ins = pe.matmul(bank[XB][:, j, :], ml[:, k % 4, j, :], t_[:, j, :] if k else ident,
                                        start=True, stop=True, skip_group_check=True)
                    ins.then_inc(xs, 1)
                    if k == 0:
                        continue
                    pe.wait_ge(x_cp, u * (LEVELS - 1) + k)
                    if k == 1:
                        pe.wait_ge(tt0, u + 1)
                        pe.wait_ge(s_up, u)
                        pe.wait_ge(o_cp, u)
                    else:
                        pe.wait_ge(tt_up, u * (LEVELS - 1) + k - 1)
                    if k < LEVELS - 1:
                        for j in each:
                            ins = pe.matmul(bank[P1B][:, j, :], tt[:, j, :], x_[:, j, :], start=True, stop=True,
                                            skip_group_check=True)
                        ins.then_inc(p1s, 1)
                    for j in each:
                        ins = pe.matmul(bank[P2B][:, j, :], x_[:, j, :], tt[:, j, :], start=True, stop=True,
                                        skip_group_check=True)
                    ins.then_inc(p2s, 1)
                pe.wait_ge(kbe_d, u + 1)
                pe.wait_ge(tt_up, (u + 1) * (LEVELS - 1))
                for j in each:
                    ins = pe.matmul(bank[P1B][:, j, :], kbe[:, j, :], tt[:, j, :], start=True, stop=True,
                                    skip_group_check=True)
                ins.then_inc(pw, 1)
                pe.wait_ge(vb_d, u + 1)
                pe.wait_ge(wtn_d, u + 1)
                pe.wait_ge(s_up, u)
                for j in each:
                    pe.matmul(bank[XB][:, j, :], tt[:, j, :], vb[:, j, :], start=True, stop=False, skip_group_check=True)
                    ins = pe.matmul(bank[XB][:, j, :], wtn[:, j, :], st[:, j, :], start=False, stop=True,
                                    skip_group_check=True)
                ins.then_inc(vnp, 1)
                pe.wait_ge(vn_d, u + 1)
                pe.wait_ge(kde_d, u + 1)
                for j in each:
                    ins = pe.matmul(bank[P1B][:, j, :], kde[:, j, :], vn[:, j, :], start=True, stop=True,
                                    skip_group_check=True)
                ins.then_inc(sps, 1)
                pe.wait_ge(qd_d, u + 1)
                pe.wait_ge(at_d, u + 1)
                for j in each:
                    pe.matmul(bank[P2B][:, j, :], st[:, j, :], qd[:, j, :], start=True, stop=False, skip_group_check=True)
                    ins = pe.matmul(bank[P2B][:, j, :], vn[:, j, :], at[:, j, :], start=False, stop=True,
                                    skip_group_check=True)
                ins.then_inc(op, 1)

            with pe.Fori(0, NPAIR) as p:
                with pe.Fori(0, 2) as hh:
                    head(p, p * 2 + hh)
                with pe.Fori(0, STEPS) as s:
                    pe.wait_ge(s_zero, p + 1)
                    step(p * STEPS + s)
                with pe.Fori(0, 2) as hh:
                    hd = p * 2 + hh
                    pe.wait_ge(o_sq, hd + 1)
                    pe.wait_ge(o_rn, hd * 2)
                    pe.wait_ge(o_cp, (p + 1) * STEPS)
                    for k in range(2):
                        ins = pe.matmul(flat(P2B + k), ones, th[:, 0, HALF * k:HALF * (k + 1)], start=True, stop=True)
                    ins.then_inc(o_ssq, 1)

        @block.scalar
        def _(act):
            eps = C("eps")

            def head(p, hd, hh):
                def fetch(m):
                    act.wait_ge(proj, hd * 4 + m + 1)
                    for k, (a, n) in enumerate(((0, META), (META, HALF), (META + HALF, HALF))):
                        src = (flat(XB + m % 2)[:, 0:META], flat(2 * (m % 2)), flat(2 * (m % 2) + 1))[k]
                        if m == 3:
                            if k:
                                ins = act.activation(zb[:, bass.ds(hh, 1), HALF * (k - 1):HALF * k], src.unsqueeze(1), ACT.Copy)
                        else:
                            ins = act.activation(raw[:, m, 2 + a:2 + a + n], src, ACT.Copy)
                    ins.then_inc(raw_in, 1)

                def tanh(m):
                    if m < 3:
                        act.wait_ge(conv, hd * 15 + 5 * m + 5)
                    meet(act, silu, hd * 4 + max(m - 1, 0), held)
                    src = acc[:, m, :] if m < 3 else zb[:, bass.ds(hh, 1), :].rearrange("p a t -> p (a t)")
                    if m == 3:
                        meet(act, raw_in, hd * 4 + 4, held)
                    act.activation(th[:, m % 2, 0:src.shape[1]], src, ACT.Tanh, scale=0.5).then_inc(tanhd, 1)

                act.wait_ge(wide_in, hd * 2)
                act.wait_ge(o_gated, p * 4)
                act.wait_ge(pads, 2)
                fetch(0)
                fetch(1)
                tanh(0)
                fetch(2)
                tanh(1)
                fetch(3)
                tanh(2)
                tanh(3)
                for m in range(2):
                    act.wait_ge(silu, hd * 4 + m + 1)
                    act.wait_ge(conv, hd * 15 + 15)
                    act.activation(raw[:, m, 0:L], acc[:, m, :], ACT.Square).then_inc(squared, 1)
                for m in range(2):
                    act.wait_ge(ssq, hd * 2 + m + 1)
                    for src, a, n in ((flat(XB + m)[:, 0:META], 0, META), (flat(P2B), META, HALF), (flat(RB), META + HALF, HALF)):
                        ins = act.activation(raw[:, m, a:a + n], src, ACT.Ln, bias=eps[:, 1:2])
                    ins.then_inc(rn, 1)
                for m in range(2):
                    act.wait_ge(rn, hd * 4 + m + 1)
                    if m == 0:
                        act.activation(raw[:, m, 0:L], raw[:, m, 0:L], ACT.Exp, scale=-0.5).then_inc(rn, 1)
                    else:
                        act.activation(raw[:, m, 0:L], raw[:, m, 0:L], ACT.Exp, scale=-0.5, bias=eps[:, 3:4]).then_inc(rn, 1)

            def step(u, s):
                act.wait_ge(dd_d, u + 1)
                act.activation(dd[:, :, :], dd[:, :, :], ACT.Exp).then_inc(dd_e, 1)
                act.wait_ge(rows_in, u * 16 + 16)
                act.wait_ge(qd_d, u)
                act.activation(eq[:, :, :], rows[:, :, 0, :], ACT.Exp).then_inc(eq_d, 1)
                act.wait_ge(tc_in, u + 1)
                for k in range(1, LEVELS):
                    act.wait_ge(xs, u * LEVELS + k + 1)
                    act.wait_ge(p2s, u * (LEVELS - 1) + k - 1)
                    act.activation(x_[:, :, :], bank[XB][:, :, :], ACT.Copy).then_inc(x_cp, 1)
                    if k < 3:
                        dst, kind, done = ((kbe, 2, kbe_d), (kde, 3, kde_d))[k - 1]
                        if k == 1:
                            act.wait_ge(turned, u * 2 + 1)
                            act.wait_ge(sps, u)
                        for j in range(NI):
                            ins = act.activation(dst[:, j, :], bank[KB][:, j, :], ACT.Copy, scale=tc[:, j, kind:kind + 1])
                        ins.then_inc(done, 1)
                act.wait_ge(pw, u + 1)
                act.wait_ge(vnp, u)
                act.activation(wtn[:, :, :], bank[P1B][:, :, :], ACT.Copy, scale=-1.0).then_inc(wtn_d, 1)
                meet(act, op, u + 1, held)
                act.activation(ot[:, :, 0, bass.ds(s * P, P)], by_dir(bank[P2B][:, :, :])[:, :, 0, :], ACT.Copy)
                act.activation(ot[:, :, 1, bass.ds((STEPS - 1) * P - s * P, P)], by_dir(bank[P2B][:, :, :])[:, :, 1, :],
                               ACT.Copy).then_inc(o_cp, 1)

            with act.Fori(0, NPAIR) as p:
                with act.Fori(0, 2) as hh:
                    head(p, p * 2 + hh, hh)
                with act.Fori(0, STEPS) as s:
                    step(p * STEPS + s, s)
                with act.Fori(0, 2) as hh:
                    hd = p * 2 + hh
                    act.wait_ge(o_add, hd + 1)
                    act.activation(th[:, 0, 0:SEQ], acc[:, 0, 0:SEQ], ACT.Square).then_inc(o_sq, 1)
                    act.wait_ge(o_ssq, hd + 1)
                    act.wait_ge(o_gated, hd * 2)
                    for k in range(2):
                        ins = act.activation(th[:, 1, HALF * k:HALF * (k + 1)], flat(P2B + k), ACT.Ln, scale=1.0 / GD,
                                             bias=eps[:, 2:3])
                    ins.then_inc(o_rn, 1)
                    act.wait_ge(o_rn, hd * 2 + 1)
                    act.activation(th[:, 1, 0:SEQ], th[:, 1, 0:SEQ], ACT.Exp, scale=-0.5).then_inc(o_rn, 1)

        @block.vector
        def _(v):
            def head(p, hd, hh):
                for m in range(3):
                    taps = V("conv")[:, bass.ds(hd * 15 + 5 * m, 5)]
                    v.wait_ge(raw_in, hd * 4 + m + 1)
                    if m == 0:
                        v.wait_ge(og_out, p * 32)
                        v.wait_ge(wide_in, hd * 2)
                        v.wait_ge(rn, hd * 4)
                    v.tensor_scalar(acc[:, m, :], raw[:, m, 0:L], taps[:, 0:1], None, ALU.mult).then_inc(conv, 1)
                    for j in range(1, 5):
                        v.wait_ge(conv, hd * 15 + 5 * m + j)
                        v.scalar_tensor_tensor(acc[:, m, :], raw[:, m, j:j + L], taps[:, j:j + 1], acc[:, m, :],
                                               ALU.mult, ALU.add).then_inc(conv, 1)
                    v.wait_ge(tanhd, hd * 4 + m + 1)
                    if m == 2:
                        v.wait_ge(kqv_in, p * STEPS)
                        v.wait_ge(pads, 3)
                    dst = acc[:, m, :] if m < 2 else wide[:, bass.ds(hh, 1), 2, W_META:W_META + L].rearrange("p a t -> p (a t)")
                    v.scalar_tensor_tensor(dst, th[:, m % 2, :], 1.0, acc[:, m, :], ALU.add, ALU.mult).then_inc(silu, 1)
                v.wait_ge(tanhd, hd * 4 + 4)
                zz = zb[:, bass.ds(hh, 1), :].rearrange("p a t -> p (a t)")
                v.scalar_tensor_tensor(zz, th[:, 1, 0:SEQ], 1.0, zz, ALU.add, ALU.mult).then_inc(silu, 1)
                for m in range(2):
                    v.wait_ge(rn, hd * 4 + 3 + m)
                    v.tensor_tensor(wide[:, bass.ds(hh, 1), m, W_META:W_META + L].rearrange("p a t -> p (a t)"), acc[:, m, :],
                                    raw[:, m, 0:L], ALU.mult).then_inc(wide_in, 1)

            def step(u):
                v.wait_ge(kde_d, u)
                v.wait_ge(s_up, u)
                v.tensor_copy(tc[:, :, :], tab[:, :, :, :, :, :].rearrange("p q s h d k -> p (q s) (h d) k")[:, bass.ds(u, 1), :, :]
                              .rearrange("p a i k -> p (a i) k")).then_inc(tc_in, 1)
                v.wait_ge(rows_in, u * 16 + 16)
                v.wait_ge(tc_in, u + 1)
                for j in range(NI):
                    ins = v.tensor_scalar(dd[:, j, :], rows[:, j, 0, :], tc[:, j, 0:1], 0.0, ALU.subtract, ALU.min)
                ins.then_inc(dd_d, 1)
                v.wait_ge(gram, u + 1)
                v.wait_ge(dd_m, u + 1)
                for dst, half, done in ((mt, 0, mt_d), (at, 1, at_d)):
                    for b in range(2):
                        ins = v.tensor_tensor(dst[:, 2 * b:2 * b + 2, :],
                                              bank[G0 + b][:, :, :].rearrange("p (i k) t -> p i k t", k=2)[:, :, half, :],
                                              dd[:, 2 * b:2 * b + 2, :], ALU.mult)
                    ins.then_inc(done, 1)
                v.wait_ge(xs, u * LEVELS + 1)
                v.tensor_tensor(t_[:, :, :], ident4, bank[XB][:, :, :], ALU.subtract).then_inc(t_up, 1)
                v.wait_ge(turned, u * 2 + 2)
                for j in range(NI):
                    ins = v.tensor_scalar(vb[:, j, :], bank[VB][:, j, :], tc[:, j, 1:2], None, ALU.mult)
                ins.then_inc(vb_d, 1)
                for k in range(1, LEVELS):
                    if k < LEVELS - 1:
                        v.wait_ge(p1s, u * (LEVELS - 2) + k)
                        v.wait_ge(t_up, u * (LEVELS - 1) + k)
                        v.tensor_tensor(t_[:, :, :], t_[:, :, :], bank[P1B][:, :, :], ALU.subtract).then_inc(t_up, 1)
                    v.wait_ge(p2s, u * (LEVELS - 1) + k)
                    if k == 1:
                        v.wait_ge(tt0, u + 1)
                    else:
                        v.wait_ge(tt_up, u * (LEVELS - 1) + k - 1)
                    v.tensor_tensor(tt[:, :, :], tt[:, :, :], bank[P2B][:, :, :], ALU.subtract).then_inc(tt_up, 1)
                v.wait_ge(vnp, u + 1)
                v.tensor_copy(vn[:, :, :], bank[XB][:, :, :]).then_inc(vn_d, 1)
                v.wait_ge(sps, u + 1)
                v.wait_ge(op, u + 1)
                for j in range(NI):
                    ins = v.scalar_tensor_tensor(st[:, j, :], st[:, j, :], tc[:, j, 4:5], bank[P1B][:, j, :],
                                                 ALU.mult, ALU.add)
                ins.then_inc(s_up, 1)

            for k in range(3):
                v.memset(raw[:, k, 0:2], 0.0)
            v.memset(raw[:, :, L + 2:L + 4], 0.0).then_inc(pads, 1)
            v.memset(wide[:, :, :, 0:W_META], 0.0).then_inc(pads, 1)
            v.memset(wide[:, :, :, (WT - 1) * P:WIDE], 0.0).then_inc(pads, 1)
            with v.Fori(0, NPAIR) as p:
                with v.Fori(0, 2) as hh:
                    head(p, p * 2 + hh, hh)
                v.wait_ge(wide_in, p * 4 + 4)
                v.wait_ge(silu, p * 8 + 8)
                both = wide[:, :, :, :].rearrange("p h m t -> p (h m) t")
                v.tensor_copy(both[:, :, (WT - 1) * P:(WT - 1) * P + META], both[:, :, W_META:P][:, :, ::-1]).then_inc(back_in, 1)
                v.wait_ge(s_up, p * STEPS)
                v.memset(st[:, :, :], 0.0).then_inc(s_zero, 1)
                with v.Fori(0, STEPS) as s:
                    v.wait_ge(s_zero, p + 1)
                    step(p * STEPS + s)
                with v.Fori(0, 2) as hh:
                    hd = p * 2 + hh
                    v.wait_ge(o_cp, (p + 1) * STEPS)
                    v.wait_ge(og_out, hd * 16)
                    of = ot[:, bass.ds(hh, 1), 0, P:].rearrange("p a t -> p (a t)")
                    ob = ot[:, bass.ds(hh, 1), 1, 0:SEQ].rearrange("p a t -> p (a t)")
                    v.tensor_tensor(acc[:, 0, 0:SEQ], of, ob, ALU.add).then_inc(o_add, 1)
                    v.wait_ge(o_rn, hd * 2 + 2)
                    v.scalar_tensor_tensor(acc[:, 0, 0:SEQ], acc[:, 0, 0:SEQ], V("norm_w"), th[:, 1, 0:SEQ],
                                           ALU.mult, ALU.mult).then_inc(o_gated, 1)
                    v.wait_ge(o_gated, hd * 2 + 1)
                    v.scalar_tensor_tensor(acc[:, 0, 0:SEQ], acc[:, 0, 0:SEQ], 0.5,
                                           zb[:, bass.ds(hh, 1), :].rearrange("p a t -> p (a t)"),
                                           ALU.mult, ALU.mult).then_inc(o_gated, 1)

        @block.gpsimd
        def _(g):
            with g.Fori(0, NPAIR) as p:
                with g.Fori(0, STEPS) as s:
                    u = p * STEPS + s
                    g.wait_ge(back_in, p + 1)
                    g.wait_ge(turned, u * 2)
                    g.wait_ge(qd_d, u)
                    for j in range(NI):
                        off = s * P if j % 2 == 0 else (WT - 1) * P - s * P
                        ins = g.tensor_copy(kqv[:, j, :, :], wide[:, j // 2, :, bass.ds(off, P)])
                    ins.then_inc(kqv_in, 1)
                    g.wait_ge(dd_e, u + 1)
                    g.tensor_tensor(by_dir(dd[:, :, :]), by_dir(dd[:, :, :]), incl, ALU.mult).then_inc(dd_m, 1)
                    g.wait_ge(mt_d, u + 1)
                    g.wait_ge(rows_in, u * 16 + 16)
                    g.tensor_tensor(mt[:, :, :], mt[:, :, :], rows[:, :, 1, :], ALU.mult).then_inc(mt_b, 1)
                    g.wait_ge(mt_b, u + 1)
                    for k in range(LEVELS):
                        g.wait_ge(xs, u * LEVELS + max(k - 3, 0))
                        if k == 4:
                            g.wait_ge(tt0, u + 1)
                        g.tensor_tensor(by_dir(ml[:, k % 4, :, :]), by_dir(mt[:, :, :]), level(k), ALU.mult).then_inc(ml_d, 1)
                        if k == 0:
                            g.wait_ge(ml_d, u * LEVELS + 1)
                            g.wait_ge(vnp, u)
                            g.tensor_tensor(tt[:, :, :], ident4, ml[:, 0, :, :], ALU.subtract).then_inc(tt0, 1)
                        if k == 3:
                            g.wait_ge(eq_d, u + 1)
                            g.wait_ge(kqv_in, u + 1)
                            g.wait_ge(op, u)
                            g.tensor_tensor(qd[:, :, :], kqv[:, :, 1, :], eq[:, :, :], ALU.mult).then_inc(qd_d, 1)


def merge(nc, io, keep):
    hT = keep["hT"]
    KN, KG = NA_W // P, GH
    PARTS = (("gate_na", 0, DC), ("gate_gdn", DC, DC), ("y_na", 2 * DC, KN), ("y_gdn", 2 * DC + KN, KG))
    NW = 2 * DC + KN + KG
    with ExitStack() as ctx:
        sb, ps, sem = makers(nc, ctx, "merge")
        og = sb("o_gdn", [P, GH, SEQ])
        ona = sb("o_na", [P, KN, SEQ])
        w = sb("w_merge", [P, 2, NW, P])
        th = sb("gate_tanh", [P, 2, 2, HALF])
        y = sb("gated_y", [P, 2, 2, HALF])
        mg = sb("merged", [P, 2, HALF])
        bank = [ps(f"bank{k}", [P, HALF]) for k in range(8)]
        o_in, w_in = sem("o_in"), [sem(f"w_merge_in{k}") for k in range(2)]
        prod, th_d, y_d, mg_d = sem("product"), sem("tanh_done"), sem("gated"), sem("merged_done")
        out, met = [sem(f"merged_out{k}") for k in range(2)], sem("met")
        block = ctx.enter_context(nc.Block())

        @block.sync
        def _(sp):
            sp.dma_start(ona[:, :, :], io["ona"].rearrange("q p t -> p q t")).then_inc(o_in, 16)
            sp.dma_start(og[:, :, :], io["og"].rearrange("h p t -> p h t")).then_inc(o_in, 16)
            with sp.Fori(0, DC // 2) as i:
                for b in range(2):
                    sp.wait_ge(prod, i * 16)
                    sp.dma_start(w[:, b, :, :], io["w_merge"][bass.ds(2 * i + b, 1), :, :, :]
                                 .rearrange("a p j n -> p (a j) n")).then_inc(w_in[b], 16)

        @block.tensor
        def _(pe):
            pe.wait_ge(o_in, 32)
            with pe.Fori(0, DC // 2) as i:
                for b in range(2):
                    pe.wait_ge(w_in[b], i * 16 + 16)
                    for k in range(2):
                        n = i * 4 + 2 * b + k
                        for q, (name, lo, num) in enumerate(PARTS):
                            if q == 0:
                                pe.wait_ge(th_d, i * 8 + max(2 * b + k - 1, 0) * 2)
                            if q == 2:
                                pe.wait_ge(y_d, i * 8 + max(2 * b + k - 1, 0) * 2)
                            tok = slice(HALF * k, HALF * (k + 1))
                            for c in range(num):
                                rhs = (hT[:, c, META + HALF * k:META + HALF * (k + 1)] if q < 2
                                       else ona[:, c, tok] if q == 2 else og[:, c, tok])
                                ins = pe.matmul(bank[4 * k + q][:, :], w[:, b, lo + c, :], rhs,
                                                start=(c == 0), stop=(c == num - 1))
                            ins.then_inc(prod, 1)

        @block.scalar
        def _(act):
            with act.Fori(0, DC // 2) as i:
                for b in range(2):
                    for k in range(2):
                        j = 2 * b + k
                        for q in range(2):
                            act.wait_ge(prod, i * 16 + 4 * j + q + 1)
                            act.wait_ge(y_d, i * 8 + max(j - 1, 0) * 2)
                            act.activation(th[:, k, q, :], bank[4 * k + q][:, :], ACT.Tanh, scale=0.5).then_inc(th_d, 1)

        @block.vector
        def _(v):
            with v.Fori(0, DC // 2) as i:
                for b in range(2):
                    for k in range(2):
                        j = 2 * b + k
                        for q in range(2):
                            v.wait_ge(prod, i * 16 + 4 * j + q + 3)
                            v.wait_ge(th_d, i * 8 + 2 * j + q + 1)
                            v.wait_ge(mg_d, i * 4 + max(j - 1, 0))
                            v.scalar_tensor_tensor(y[:, k, q, :], th[:, k, q, :], 1.0, bank[4 * k + 2 + q][:, :],
                                                   ALU.add, ALU.mult).then_inc(y_d, 1)

        @block.gpsimd
        def _(g):
            with g.Fori(0, DC // 2) as i:
                for b in range(2):
                    for k in range(2):
                        j = 2 * b + k
                        g.wait_ge(y_d, i * 8 + 2 * j + 2)
                        g.wait_ge(out[k], i * 32 + 16 * b)
                        g.tensor_tensor(mg[:, k, :], y[:, k, 0, :], y[:, k, 1, :], ALU.add).then_inc(mg_d, 1)
                        meet(g, mg_d, i * 4 + j + 1, met)
                        dst = io["merged"].rearrange("t p c n -> p t (c n)")[:, (TT // 2) * k:(TT // 2) * (k + 1),
                                                                             bass.ds((2 * i + b) * P, P)]
                        g.dma_start(dst, mg[:, k, :].rearrange("p (t n) -> p t n", n=P)).then_inc(out[k], 16)
            for k in range(2):
                g.wait_ge(out[k], 16 * DC)


def first_norm(nc, io, keep):
    con, lg = keep["con"], keep["logits"]
    ident = con[:, C_AT["ident"][0]:C_AT["ident"][1]]
    eps = con[:, C_AT["eps"][0]:C_AT["eps"][1]]
    NL = NG + NE
    with ExitStack() as ctx:
        sb, ps, sem = makers(nc, ctx, "norm1")
        wo = sb("w_out", [P, DC, D])
        vec = sb("norm_rows", [P, 4, D])
        wr = sb("w_router", [P, DC, NL])
        br = sb("b_router", [P, NL])
        mg = sb("merged", [P, 2, DC, P])
        h = sb("h_rows", [P, 2, D])
        hT1 = sb("h1_T", [P, 2, DC, P])
        stats = sb("stats", [P, 2, 12])
        mv = sb("mean_var", [P, 2, 4])
        bank = [ps(f"bank{k}", [P, HALF]) for k in range(8)]
        con_in, scaled = sem("constants_in"), sem("rows_scaled")
        mg_in, xn_in = [sem(f"merged_in{k}") for k in range(2)], [sem(f"xn_in{k}") for k in range(2)]
        mixed, skip, added, stat, rstd = sem("mixed"), sem("skip_made"), sem("added"), sem("stat"), sem("rstd")
        normed, h1_d, turned, hT_in = sem("normed"), sem("h1_made"), sem("h1_turned"), sem("h1_T_in")
        routed, lg_d = sem("logits_done"), sem("logits_in")
        h1_out, held, met = [sem(f"h1_out{k}") for k in range(2)], sem("held"), sem("met")
        block = ctx.enter_context(nc.Block())

        @block.sync
        def _(sp):
            sp.dma_start(wo[:, :, :], io["w_out"]).then_inc(con_in, 16)
            for k, name in enumerate(("ln0_g", "ln0_b", "ln1_g", "ln1_b")):
                sp.dma_start(vec[:, k, :], io[name].to_broadcast([P, D])).then_inc(con_in, 16)
            sp.dma_start(wr[:, :, :], io["w_router"]).then_inc(con_in, 16)
            sp.dma_start(br[:, :], io["b_router"].to_broadcast([P, NL])).then_inc(con_in, 16)
            with sp.Fori(0, TT // 2) as i:
                for k in range(2):
                    t = 2 * i + k
                    meet(sp, mixed, i * 2, met)
                    sp.dma_start(mg[:, k, :, :], io["merged"][bass.ds(t, 1), :, :, :]
                                 .rearrange("a p c n -> p (a c) n")).then_inc(mg_in[k], 16)
                    meet(sp, h1_out[k], i * 16, met)
                    sp.wait_ge(turned, i * 2)
                    sp.dma_start(h[:, k, :], io["xn"][bass.ds(t * P, P), :]).then_inc(xn_in[k], 16)
                for k in range(2):
                    sp.wait_ge(h1_d, i * 4 + 2 * k + 2)
                    sp.dma_start(io["h1"][bass.ds((2 * i + k) * P, P), :], h[:, k, :]).then_inc(h1_out[k], 16)
            for k in range(2):
                sp.wait_ge(h1_out[k], 16 * (TT // 2))

        @block.tensor
        def _(pe):
            pe.wait_ge(con_in, 16 * 7)

            def mix(i, k):
                pe.wait_ge(mg_in[k], i * 16 + 16)
                pe.wait_ge(added, i * 2)
                for f in range(2):
                    for c in range(DC):
                        ins = pe.matmul(bank[2 * k + f][:, :], mg[:, k, c, :], wo[:, c, HALF * f:HALF * (f + 1)],
                                        start=(c == 0), stop=(c == DC - 1))
                ins.then_inc(mixed, 1)

            with pe.Fori(0, TT // 2) as i:
                mix(i, 0)
                mix(i, 1)
                for k in range(2):
                    pe.wait_ge(h1_d, i * 4 + 2 * k + 2)
                    pe.wait_ge(hT_in, i * 2 + k)
                    for c in range(DC):
                        ins = pe.transpose(bank[4 + c // 4][:, P * (c % 4):P * (c % 4) + P], h[:, k, P * c:P * c + P], ident)
                    ins.then_inc(turned, 1)
                for k in range(2):
                    pe.wait_ge(hT_in, i * 2 + k + 1)
                    pe.wait_ge(lg_d, i * 2 + k)
                    for c in range(DC):
                        ins = pe.matmul(bank[6][:, 0:NL], hT1[:, k, c, :], wr[:, c, :], start=(c == 0), stop=(c == DC - 1))
                    ins.then_inc(routed, 1)

        @block.gpsimd
        def _(g):
            g.wait_ge(con_in, 16 * 7)
            for k in range(2):
                g.tensor_scalar(vec[:, k, :], vec[:, k, :], ALPHA, None, ALU.mult).then_inc(scaled, 1)
            g.wait_ge(scaled, 2)
            with g.Fori(0, TT // 2) as i:
                for k in range(2):
                    g.wait_ge(xn_in[k], i * 16 + 16)
                    g.tensor_tensor(h[:, k, :], h[:, k, :], vec[:, 0, :], ALU.mult).then_inc(skip, 1)
                    g.wait_ge(skip, i * 4 + 2 * k + 1)
                    g.tensor_tensor(h[:, k, :], h[:, k, :], vec[:, 1, :], ALU.add).then_inc(skip, 1)
                for k in range(2):
                    g.wait_ge(normed, i * 2 + k + 1)
                    g.tensor_tensor(h[:, k, :], h[:, k, :], vec[:, 2, :], ALU.mult).then_inc(h1_d, 1)
                    g.wait_ge(h1_d, i * 4 + 2 * k + 1)
                    g.tensor_tensor(h[:, k, :], h[:, k, :], vec[:, 3, :], ALU.add).then_inc(h1_d, 1)

        @block.vector
        def _(v):
            v.wait_ge(con_in, 16 * 7)
            with v.Fori(0, TT // 2) as i:
                for k in range(2):
                    t = i * 2 + k
                    v.wait_ge(mixed, t + 1)
                    v.wait_ge(skip, i * 4 + 2 * k + 2)
                    for f in range(2):
                        part = h[:, k, HALF * f:HALF * (f + 1)]
                        ins = v.scalar_tensor_tensor(part, bank[2 * k + f][:, :], 0.5, part, ALU.mult, ALU.add)
                    ins.then_inc(added, 1)
                    v.wait_ge(added, t + 1)
                    for f in range(2):
                        ins = v.bn_stats(stats[:, k, 6 * f:6 * f + 6], h[:, k, HALF * f:HALF * (f + 1)])
                    ins.then_inc(stat, 1)
                    meet(v, stat, t * 2 + 1, held)
                    v.bn_aggr(mv[:, k, 0:2], stats[:, k, :]).then_inc(stat, 1)
                    v.wait_ge(rstd, t * 2 + 2)
                    v.tensor_scalar(h[:, k, :], h[:, k, :], mv[:, k, 0:1], mv[:, k, 3:4], ALU.subtract, ALU.mult).then_inc(normed, 1)
                for k in range(2):
                    t = i * 2 + k
                    v.wait_ge(routed, t + 1)
                    v.tensor_tensor(lg[:, bass.ds(t, 1), :].rearrange("p a n -> p (a n)"), bank[6][:, 0:NL], br[:, :],
                                    ALU.add).then_inc(lg_d, 1)

        @block.scalar
        def _(act):
            with act.Fori(0, TT // 2) as i:
                for k in range(2):
                    t = i * 2 + k
                    act.wait_ge(stat, t * 2 + 2)
                    act.activation(mv[:, k, 2:3], mv[:, k, 1:2], ACT.Ln, bias=eps[:, 0:1]).then_inc(rstd, 1)
                    act.wait_ge(rstd, t * 2 + 1)
                    act.activation(mv[:, k, 3:4], mv[:, k, 2:3], ACT.Exp, scale=-0.5).then_inc(rstd, 1)
                for k in range(2):
                    t = i * 2 + k
                    act.wait_ge(turned, t + 1)
                    act.wait_ge(routed, i * 2)
                    for f in range(2):
                        ins = act.activation(hT1[:, k, 4 * f:4 * f + 4, :].rearrange("p c n -> p (c n)"), bank[4 + f][:, :], ACT.Copy)
                    ins.then_inc(hT_in, 1)


def route(nc, io, keep):
    con, lg, slot, wt, owner = keep["con"], keep["logits"], keep["slot"], keep["weight"], keep["owner"]
    C = lambda n: con[:, C_AT[n][0]:C_AT[n][1]]
    with ExitStack() as ctx:
        sb, ps, sem = makers(nc, ctx, "route")
        top = sb("top", [P, 4, TT])
        eq = sb("group_rank", [P, TT, NG])
        goh = sb("group_onehot", [P, TT, NG])
        gex = sb("group_exp", [P, TT, NG])
        gw = sb("group_weight", [P, TT])
        tmp = sb("picked", [P, TT, NG, EPG])
        sel = sb("expert_logits", [P, TT, EPG])
        rank = sb("expert_rank", [P, TT, EPG])
        oh = sb("expert_onehot", [P, 2, TT, EPG])
        hot = sb("onehot", [P, 3, TT, NE])
        dif = sb("logit_difference", [P, 2, TT])
        base = sb("tile_base", [P, TT + 1, NE])
        k128 = sb("block_edges", [P, TT])
        over = sb("over_edge", [P, NE, TT])
        nb = sb("expert_blocks", [P, NE])
        bend = sb("block_end", [P, NE])
        one = sb("one", [P, NE])
        dest = sb("dest", [P, TT, NE])
        own = sb("own", [1, NBLK, NE])
        ownf = sb("own_sum", [1, NBLK])
        sl = sb("slot_f", [P, 2, TT])
        ids = sb("token_ids", [P, TT], U32)
        zero = sb("zero", [P, NBLK], U32)
        pre = ps("prefix", [P, TT, NE])
        tot = ps("totals", [P, TT, NE])
        step, ex, pfx = sem("route_step"), sem("exp_done"), sem("prefix_done")
        cleared, table = sem("table_cleared"), sem("table_out")
        block = ctx.enter_context(nc.Block())
        MARK = 99.0
        count = {}

        @block.vector
        def _(v):
            n = [0]

            def link(ins, name=None):
                n[0] += 1
                ins.then_inc(step, 1)
                v.wait_ge(step, n[0])
                if name:
                    count[name] = n[0]

            last = lambda a, k: a.unsqueeze(a.ndim).to_broadcast(list(a.shape) + [k])
            G = lg[:, :, 0:NG]
            E = lg[:, :, NG:NG + NE].rearrange("p t (g e) -> p t g e", e=EPG)
            gidx = C("gidx").unsqueeze(1).to_broadcast([P, TT, NG])
            eidx = C("eidx")[:, 0:EPG].unsqueeze(1).to_broadcast([P, TT, EPG])
            link(v.memset(zero[:, :], 0))
            link(v.tensor_copy(ids[:, :], C("tok")), "ids")
            link(v.memset(one[:, :], 1.0))
            link(v.memset(base[:, 0, :], 0.0))
            link(v.tensor_reduce(top[:, 0, :], G, AX.X, ALU.max))
            link(v.tensor_tensor(eq[:, :, :], G, last(top[:, 0, :], NG), ALU.is_equal))
            link(v.scalar_tensor_tensor(eq[:, :, :], eq[:, :, :], -MARK, gidx, ALU.mult, ALU.add))
            link(v.tensor_reduce(top[:, 1, :], eq[:, :, :], AX.X, ALU.min))
            link(v.tensor_tensor(goh[:, :, :], eq[:, :, :], last(top[:, 1, :], NG), ALU.is_equal))
            link(v.tensor_tensor(gex[:, :, :], G, last(top[:, 0, :], NG), ALU.subtract), "group_shifted")
            link(v.tensor_tensor(tmp[:, :, :, :], E, last(goh[:, :, :], EPG), ALU.mult))
            link(v.tensor_reduce(sel[:, :, :], tmp[:, :, :, :].rearrange("p t g e -> p t e g"), AX.X, ALU.add))
            for k in range(2):
                link(v.tensor_reduce(top[:, 2 + k, :], sel[:, :, :], AX.X, ALU.max))
                link(v.tensor_tensor(rank[:, :, :], sel[:, :, :], last(top[:, 2 + k, :], EPG), ALU.is_equal))
                link(v.scalar_tensor_tensor(rank[:, :, :], rank[:, :, :], -MARK, eidx, ALU.mult, ALU.add))
                link(v.tensor_reduce(dif[:, 0, :], rank[:, :, :], AX.X, ALU.min))
                link(v.tensor_tensor(oh[:, k, :, :], rank[:, :, :], last(dif[:, 0, :], EPG), ALU.is_equal))
                if k == 0:
                    link(v.scalar_tensor_tensor(sel[:, :, :], oh[:, 0, :, :], -BIG, sel[:, :, :], ALU.mult, ALU.add))
            link(v.tensor_tensor(dif[:, 1, :], top[:, 3, :], top[:, 2, :], ALU.subtract), "pair_shifted")
            for k in range(2):
                link(v.tensor_tensor(hot[:, k, :, :].rearrange("p t (g e) -> p t g e", e=EPG), last(goh[:, :, :], EPG),
                                     oh[:, k, :, :].unsqueeze(2).to_broadcast([P, TT, NG, EPG]), ALU.mult))
            link(v.tensor_tensor(hot[:, 2, :, :], hot[:, 0, :, :], hot[:, 1, :, :], ALU.add), "hot")
            v.wait_ge(ex, 2)
            link(v.tensor_reduce(gw[:, :], gex[:, :, :], AX.X, ALU.add))
            link(v.tensor_scalar(top[:, 0, :], dif[:, 1, :], 1.0, None, ALU.add))
            link(v.tensor_tensor(gw[:, :], gw[:, :], top[:, 0, :], ALU.mult))
            link(v.reciprocal(wt[:, 0, :], gw[:, :]))
            link(v.tensor_tensor(wt[:, 1, :], wt[:, 0, :], dif[:, 1, :], ALU.mult))
            v.wait_ge(pfx, 2)
            for t in range(TT):
                link(v.tensor_tensor(base[:, t + 1, :], base[:, t, :], tot[:, t, :], ALU.add))
            link(v.tensor_scalar(k128[:, :], C("blk")[:, 0:TT], float(P), None, ALU.mult))
            link(v.tensor_tensor(over[:, :, :], last(base[:, TT, :], TT), k128[:, :].unsqueeze(1).to_broadcast([P, NE, TT]),
                                 ALU.is_gt))
            link(v.tensor_reduce(nb[:, :], over[:, :, :], AX.X, ALU.add))
            link(v.tensor_tensor_scan(bend[:, :], one[:, :], nb[:, :], 0.0, ALU.mult, ALU.add))
            link(v.tensor_tensor(nb[:, :], bend[:, :], nb[:, :], ALU.subtract))
            link(v.tensor_tensor(dest[:, :, :], pre[:, :, :], base[:, 0:TT, :], ALU.add))
            link(v.scalar_tensor_tensor(dest[:, :, :], nb[:, :].unsqueeze(1).to_broadcast([P, TT, NE]), float(P), dest[:, :, :],
                                        ALU.mult, ALU.add))
            for k in range(2):
                link(v.tensor_tensor(hot[:, k, :, :], hot[:, k, :, :], dest[:, :, :], ALU.mult))
                link(v.tensor_reduce(sl[:, k, :], hot[:, k, :, :], AX.X, ALU.add))
            link(v.tensor_copy(slot[:, :, :], sl[:, :, :]), "slot")
            link(v.tensor_tensor(own[:, :, :], bend[0:1, :].unsqueeze(1).to_broadcast([1, NBLK, NE]),
                                 last(C("blk")[0:1, :], NE), ALU.is_le))
            link(v.tensor_reduce(ownf[:, :], own[:, :, :], AX.X, ALU.add))
            link(v.tensor_scalar(owner[:, 0:NBLK], ownf[:, :], float(NE - 1), None, ALU.min))
            link(v.tensor_copy(owner[:, NBLK:NBLK + 1], bend[0:1, NE - 1:NE]))

        @block.scalar
        def _(act):
            act.wait_ge(step, count["group_shifted"])
            act.activation(gex[:, :, :], gex[:, :, :], ACT.Exp).then_inc(ex, 1)
            act.wait_ge(step, count["pair_shifted"])
            act.activation(dif[:, 1, :], dif[:, 1, :], ACT.Exp).then_inc(ex, 1)

        @block.tensor
        def _(pe):
            pe.wait_ge(step, count["hot"])
            for dst, tri in ((pre, "before"), (tot, "ones")):
                pe.matmul(dst[:, :, :], C(tri), hot[:, 2, :, :], start=True, stop=True).then_inc(pfx, 1)

        @block.gpsimd
        def _(g):
            g.wait_ge(step, count["ids"])
            g.dma_start(io["token_of"].rearrange("(p b) a -> p (b a)", p=P), zero[:, :]).then_inc(cleared, 16)
            g.wait_ge(cleared, 16)
            g.wait_ge(step, count["slot"])
            for k in range(2):
                for t in range(TT):
                    g.indirect_dma_start(out=io["token_of"], out_offset=bass.IndirectOffsetOnAxis(ap=slot[:, k, t:t + 1], axis=0),
                                         in_=ids[:, t:t + 1], in_offset=None).then_inc(table, 16)
            g.wait_ge(table, 16 * 2 * TT)


def experts(nc, io, keep):
    con, owner = keep["con"], keep["owner"]
    ident = con[:, C_AT["ident"][0]:C_AT["ident"][1]]
    FC = FE // P
    with ExitStack() as ctx:
        sb, ps, sem = makers(nc, ctx, "moe")
        wgu = sb("w_gate_up", [P, 2, DC, 2 * FE])
        wdn = sb("w_down", [P, 2, FC, D])
        idx = sb("token_index", [P, 2], U32)
        x = sb("x_rows", [P, 2, D])
        xT = sb("x_T", [P, 2, DC, P])
        th = sb("gate_tanh", [P, 2, FE])
        hid = sb("hidden", [P, 2, FE])
        hidT = sb("hidden_T", [P, 2, FC, P])
        y = sb("y_rows", [P, 2, D])
        bank = [ps(f"bank{k}", [P, HALF]) for k in range(8)]
        two = lambda n: [sem(f"{n}{k}") for k in range(2)]
        gu_in, dn_in, idx_in, x_in, y_out = two("gate_up_in"), two("down_in"), two("index_in"), two("x_in"), two("y_out")
        turned, xT_a, xT_v, gu, th_d = sem("x_turned"), sem("x_T_low"), sem("x_T_high"), sem("gate_up"), sem("tanh_done")
        hid_d, hid_t, hidT_in, down = sem("hidden_step"), sem("hidden_turned"), sem("hidden_T_in"), sem("down_done")
        y_a, y_v, met, met_g = sem("y_low"), sem("y_high"), sem("met"), sem("met_g")
        block = ctx.enter_context(nc.Block())

        @block.sync
        def _(sp):
            with sp.Fori(0, NBLK // 2) as i:
                for k in range(2):
                    e = sp.value_load(owner[0:1, bass.ds(2 * i + k, 1)], min_val=0, max_val=NE - 1)
                    meet(sp, x_in[k], i * 16, met)
                    sp.dma_start(idx[:, k:k + 1], io["token_of"][bass.ds((2 * i + k) * P, P), :]).then_inc(idx_in[k], 16)
                    meet(sp, gu, i * 2, met)
                    sp.dma_start(wgu[:, k, :, :], io["w_gate_up"][bass.ds(e, 1), :, :, :]
                                 .rearrange("a p c n -> p (a c) n")).then_inc(gu_in[k], 16)
                    meet(sp, down, i * 2, met)
                    sp.dma_start(wdn[:, k, :, :], io["w_down"][bass.ds(e, 1), :, :, :]
                                 .rearrange("a p c n -> p (a c) n")).then_inc(dn_in[k], 16)

        @block.gpsimd
        def _(g):
            with g.Fori(0, NBLK // 2) as i:
                for k in range(2):
                    meet(g, idx_in[k], i * 16 + 16, met_g)
                    meet(g, turned, i * 2, met_g)
                    g.indirect_dma_start(out=x[:, k, :], out_offset=None, in_=io["h1"],
                                         in_offset=bass.IndirectOffsetOnAxis(ap=idx[:, k:k + 1], axis=0)).then_inc(x_in[k], 16)

        @block.tensor
        def _(pe):
            with pe.Fori(0, NBLK // 2) as i:
                for k in range(2):
                    b = i * 2 + k
                    pe.wait_ge(x_in[k], i * 16 + 16)
                    pe.wait_ge(xT_a, b)
                    pe.wait_ge(xT_v, b)
                    for c in range(DC):
                        ins = pe.transpose(bank[c // 4][:, P * (c % 4):P * (c % 4) + P], x[:, k, P * c:P * c + P], ident)
                    ins.then_inc(turned, 1)
                    pe.wait_ge(gu_in[k], i * 16 + 16)
                    pe.wait_ge(hid_d, i * 4)
                    for c in range(DC):
                        if c == 0:
                            pe.wait_ge(xT_a, b + 1)
                        if c == 4:
                            pe.wait_ge(xT_v, b + 1)
                        ins = pe.matmul(bank[2 + k][:, :], xT[:, k, c, :], wgu[:, k, c, :], start=(c == 0), stop=(c == DC - 1))
                    ins.then_inc(gu, 1)
                for k in range(2):
                    b = i * 2 + k
                    pe.wait_ge(hid_d, i * 4 + 2 * k + 2)
                    pe.wait_ge(hidT_in, b)
                    for f in range(FC):
                        ins = pe.transpose(bank[4][:, P * f:P * f + P], hid[:, k, P * f:P * f + P], ident)
                    ins.then_inc(hid_t, 1)
                    pe.wait_ge(dn_in[k], i * 16 + 16)
                    pe.wait_ge(hidT_in, b + 1)
                    pe.wait_ge(y_a, b)
                    pe.wait_ge(y_v, b)
                    for half in range(2):
                        for f in range(FC):
                            ins = pe.matmul(bank[5 + half][:, :], hidT[:, k, f, :], wdn[:, k, f, HALF * half:HALF * (half + 1)],
                                            start=(f == 0), stop=(f == FC - 1))
                    ins.then_inc(down, 1)

        @block.scalar
        def _(act):
            with act.Fori(0, NBLK // 2) as i:
                for k in range(2):
                    b = i * 2 + k
                    act.wait_ge(turned, b + 1)
                    act.wait_ge(gu, i * 2)
                    act.activation(xT[:, k, 0:4, :].rearrange("p c n -> p (c n)"), bank[0][:, :], ACT.Copy).then_inc(xT_a, 1)
                    act.wait_ge(gu, b + 1)
                    act.wait_ge(hid_d, i * 4)
                    act.activation(th[:, k, :], bank[2 + k][:, 0:FE], ACT.Tanh, scale=0.5).then_inc(th_d, 1)
                for k in range(2):
                    b = i * 2 + k
                    act.wait_ge(hid_t, b + 1)
                    act.wait_ge(down, i * 2)
                    act.activation(hidT[:, k, :, :].rearrange("p f n -> p (f n)"), bank[4][:, 0:FE], ACT.Copy).then_inc(hidT_in, 1)
                    act.wait_ge(down, b + 1)
                    act.wait_ge(y_out[k], i * 16)
                    act.activation(y[:, k, 0:HALF], bank[5][:, :], ACT.Copy).then_inc(y_a, 1)
                    act.wait_ge(y_a, b + 1)
                    act.wait_ge(y_v, b + 1)
                    act.dma_start(io["y"][bass.ds(b * P, P), :], y[:, k, :]).then_inc(y_out[k], 16)
            for k in range(2):
                act.wait_ge(y_out[k], 16 * (NBLK // 2))

        @block.vector
        def _(v):
            with v.Fori(0, NBLK // 2) as i:
                for k in range(2):
                    b = i * 2 + k
                    v.wait_ge(turned, b + 1)
                    v.wait_ge(gu, i * 2)
                    v.tensor_copy(xT[:, k, 4:8, :].rearrange("p c n -> p (c n)"), bank[1][:, :]).then_inc(xT_v, 1)
                    v.wait_ge(th_d, b + 1)
                    v.wait_ge(hid_t, i * 2)
                    v.scalar_tensor_tensor(hid[:, k, :], th[:, k, :], 1.0, bank[2 + k][:, 0:FE], ALU.add, ALU.mult).then_inc(hid_d, 1)
                    v.wait_ge(hid_d, i * 4 + 2 * k + 1)
                    v.scalar_tensor_tensor(hid[:, k, :], hid[:, k, :], 0.5, bank[2 + k][:, FE:2 * FE], ALU.mult, ALU.mult).then_inc(hid_d, 1)
                for k in range(2):
                    b = i * 2 + k
                    v.wait_ge(down, b + 1)
                    v.wait_ge(y_out[k], i * 16)
                    v.tensor_copy(y[:, k, HALF:D], bank[6][:, :]).then_inc(y_v, 1)


def last_norm(nc, io, keep):
    con, slot, wt = keep["con"], keep["slot"], keep["weight"]
    eps = con[:, C_AT["eps"][0]:C_AT["eps"][1]]
    with ExitStack() as ctx:
        sb, ps, sem = makers(nc, ctx, "norm2")
        vec = sb("norm_rows", [P, 2, D])
        pick = sb("slot_index", [P, 2, 2], U32)
        pw = sb("slot_weight", [P, 2, 2])
        y = sb("y_rows", [P, 2, 2, D])
        h = sb("h_rows", [P, 2, D])
        stats = sb("stats", [P, 2, 12])
        mv = sb("mean_var", [P, 2, 4])
        two = lambda n: [sem(f"{n}{k}") for k in range(2)]
        vec_in, h_in, y_in, out = sem("rows_in"), two("h_in"), two("y_in"), two("out_stored")
        picked, summed, stat, rstd, normed, fin = sem("picked"), sem("summed"), sem("stat"), sem("rstd"), sem("normed"), sem("final")
        held, met, met_g = sem("held"), sem("met"), sem("met_g")
        block = ctx.enter_context(nc.Block())

        @block.sync
        def _(sp):
            for k, name in enumerate(("ln2_g", "ln2_b")):
                sp.dma_start(vec[:, k, :], io[name].to_broadcast([P, D])).then_inc(vec_in, 16)
            with sp.Fori(0, TT // 2) as i:
                for k in range(2):
                    sp.wait_ge(out[k], i * 16)
                    sp.dma_start(h[:, k, :], io["h1"][bass.ds((2 * i + k) * P, P), :]).then_inc(h_in[k], 16)
                for k in range(2):
                    sp.wait_ge(fin, i * 4 + 2 * k + 2)
                    sp.dma_start(io["out"][bass.ds((2 * i + k) * P, P), :], h[:, k, :]).then_inc(out[k], 16)
            for k in range(2):
                sp.wait_ge(out[k], 16 * (TT // 2))

        @block.gpsimd
        def _(g):
            def gather(i, k):
                meet(g, picked, i * 4 + 2 * k + 2, met_g)
                for e in range(2):
                    g.indirect_dma_start(out=y[:, k, e, :], out_offset=None, in_=io["y"],
                                         in_offset=bass.IndirectOffsetOnAxis(ap=pick[:, k, e:e + 1], axis=0)).then_inc(y_in[k], 16)

            with g.Fori(0, TT // 2) as i:
                gather(i, 0)
                gather(i, 1)
                for k in range(2):
                    g.wait_ge(normed, i * 2 + k + 1)
                    g.wait_ge(vec_in, 32)
                    g.tensor_tensor(h[:, k, :], h[:, k, :], vec[:, 0, :], ALU.mult).then_inc(fin, 1)
                    g.wait_ge(fin, i * 4 + 2 * k + 1)
                    g.tensor_tensor(h[:, k, :], h[:, k, :], vec[:, 1, :], ALU.add).then_inc(fin, 1)

        @block.vector
        def _(v):
            with v.Fori(0, TT // 2) as i:
                for k in range(2):
                    t = i * 2 + k
                    v.wait_ge(y_in[k], i * 32)
                    v.wait_ge(summed, i * 6)
                    v.tensor_copy(pick[:, k, :], slot[:, :, bass.ds(t, 1)].rearrange("p e a -> p (e a)")).then_inc(picked, 1)
                    v.tensor_copy(pw[:, k, :], wt[:, :, bass.ds(t, 1)].rearrange("p e a -> p (e a)")).then_inc(picked, 1)
                for k in range(2):
                    t = i * 2 + k
                    v.wait_ge(y_in[k], i * 32 + 32)
                    v.wait_ge(picked, i * 4 + 2 * k + 2)
                    v.tensor_scalar(y[:, k, 0, :], y[:, k, 0, :], pw[:, k, 0:1], None, ALU.mult).then_inc(summed, 1)
                    v.wait_ge(summed, i * 6 + 3 * k + 1)
                    v.scalar_tensor_tensor(y[:, k, 0, :], y[:, k, 1, :], pw[:, k, 1:2], y[:, k, 0, :], ALU.mult, ALU.add).then_inc(summed, 1)
                    v.wait_ge(summed, i * 6 + 3 * k + 2)
                    v.wait_ge(h_in[k], i * 16 + 16)
                    v.scalar_tensor_tensor(h[:, k, :], h[:, k, :], ALPHA, y[:, k, 0, :], ALU.mult, ALU.add).then_inc(summed, 1)
                    v.wait_ge(summed, i * 6 + 3 * k + 3)
                    for f in range(2):
                        ins = v.bn_stats(stats[:, k, 6 * f:6 * f + 6], h[:, k, HALF * f:HALF * (f + 1)])
                    ins.then_inc(stat, 1)
                    meet(v, stat, t * 2 + 1, held)
                    v.bn_aggr(mv[:, k, 0:2], stats[:, k, :]).then_inc(stat, 1)
                    v.wait_ge(rstd, t * 2 + 2)
                    v.tensor_scalar(h[:, k, :], h[:, k, :], mv[:, k, 0:1], mv[:, k, 3:4], ALU.subtract, ALU.mult).then_inc(normed, 1)

        @block.scalar
        def _(act):
            with act.Fori(0, TT // 2) as i:
                for k in range(2):
                    t = i * 2 + k
                    act.wait_ge(stat, t * 2 + 2)
                    act.activation(mv[:, k, 2:3], mv[:, k, 1:2], ACT.Ln, bias=eps[:, 0:1]).then_inc(rstd, 1)
                    act.wait_ge(rstd, t * 2 + 1)
                    act.activation(mv[:, k, 3:4], mv[:, k, 2:3], ACT.Exp, scale=-0.5).then_inc(rstd, 1)


def kernel(**inputs):
    from concourse import bacc
    from concourse.bass_utils import run_bass_kernel_spmd

    f = {k: np.asarray(v) for k, v in inputs.items()}
    for name in f:
        if f[name].shape[0] == 1 and name not in ("x", "meta_tokens"):
            f[name] = f[name][0]
    w = f["w_in"]
    rowsof = lambda a: a.reshape(-1, P, a.shape[-1]).transpose(1, 0, 2)
    at = 3 * NA_W + 4 * D
    wg = np.zeros((P, DC, P), w.dtype)
    for k in range(4):
        wg[:, :, 32 * k:32 * k + GH] = rowsof(w[:, at + GH * k:at + GH * k + GH])
    cols = np.zeros((P, V_W), w.dtype)

    def put(name, a, lo=0):
        cols[lo:lo + a.shape[0], V_AT[name][0]:V_AT[name][1]] = a

    put("ln0_g", f["ln0_g"].reshape(DC, P).T)
    put("ln0_b", f["ln0_b"].reshape(DC, P).T)
    for d in range(2):
        put("dt", f["gdn_dt_bias"][d][:, None], 32 * d)
        put("alog", f["gdn_a_log"][d][:, None], 32 * d)
    put("conv", f["gdn_conv_w"].reshape(5, 3, GH, P)[:, [1, 0, 2]].transpose(3, 2, 1, 0).reshape(P, -1))
    put("norm_w", f["gdn_norm_w"][:, None])
    at = 3 * NA_W
    w_gdn = np.stack([w[:, at + D * m:at + D * m + D].reshape(DC, P, GH, P) for m in (1, 0, 2, 3)], 3)
    w_gdn = w_gdn.transpose(2, 1, 0, 3, 4)
    w_na3 = np.stack([w[:, NA_W * m:NA_W * (m + 1)].reshape(DC, P, NPAIR, P) for m in range(3)], 3).transpose(2, 1, 0, 3, 4)
    col = np.arange(GRID_W)
    distance = np.clip(col[None, :] - col[:, None] + KC - 1, 0, 2 * KC - 2)
    bias = f["na_rpb"][:, :, distance].transpose(0, 2, 1, 3).reshape(NPAIR, P, DRS, GRID_W)
    at = 3 * NA_W + 4 * D + 4 * GH
    by_out = lambda a: a.reshape(a.shape[0] // P, P, DC, P).transpose(2, 1, 0, 3)
    w_merge = np.concatenate([by_out(w[:, at:at + D]), by_out(w[:, at + D:at + 2 * D]), by_out(f["w_branch_na"]),
                              by_out(f["w_branch_gdn"])], 2)
    w_router = np.concatenate([f["router_group_w"], f["router_expert_w"]], 1)
    b_router = np.concatenate([f["router_group_b"], f["router_expert_b"]])[None, :]
    w_gate_up = np.concatenate([f["expert_w_gate"], f["expert_w_up"]], 2).reshape(NE, DC, P, 2 * FE).transpose(0, 2, 1, 3)
    arrays = {
        "const": constants(), "scan": scan_masks(), "cols": cols, "w_gates": wg,
        "x": f["x"][0], "meta": f["meta_tokens"], "w_gdn": w_gdn, "w_na3": w_na3, "bias": bias,
        "w_merge": w_merge, "w_out": rowsof(f["w_out"]), "w_router": rowsof(w_router), "b_router": b_router,
        "w_gate_up": w_gate_up, "w_down": f["expert_w_down"].reshape(NE, FE // P, P, D).transpose(0, 2, 1, 3),
        **{n: f[n].reshape(1, D) for n in ("ln0_g", "ln0_b", "ln1_g", "ln1_b", "ln2_g", "ln2_b")},
    }
    nc = bacc.Bacc("TRN2", target_bir_lowering=False, num_devices=1)
    io = {}
    for name, a in arrays.items():
        arrays[name] = a = np.ascontiguousarray(a)
        io[name] = nc.dram_tensor(f"in_{name}", a.shape, mybir.dt.from_np(a.dtype), kind="ExternalInput").ap()
    for name, shape, dt in SCRATCH:
        io[name] = nc.dram_tensor(f"s_{name}", shape, dt, kind="Internal").ap()
    io["out"] = nc.dram_tensor("out", (SEQ, D), F32, kind="ExternalOutput").ap()
    program(nc, io)
    r = run_bass_kernel_spmd(nc, [{f"in_{n}": a for n, a in arrays.items()}], core_ids=[0])
    return r.results[0]["out"].reshape(1, SEQ, D)


SCRATCH = [
    ("xn", (SEQ, D), F32),
    ("rows", (GH // 2, STEPS, 2, 2, 2, P), F32),
    ("og", (GH, P, SEQ), F32),
    ("ona", (NPAIR, P, SEQ), F32),
    ("merged", (TT, P, DC, P), F32),
    ("h1", (SEQ, D), F32),
    ("token_of", (SLOTS, 1), U32),
    ("y", (SLOTS, D), F32),
]


def program(nc, io):
    with ExitStack() as ctx:
        keep = {
            "con": ctx.enter_context(nc.sbuf_tensor("con", [P, C_W], F32)),
            "colv": ctx.enter_context(nc.sbuf_tensor("colv", [P, V_W], F32)),
        }
        with nc.sbuf_tensor("hT", [P, DC, L], F32) as hT, \
                nc.sbuf_tensor("tab", [P, GH // 2, STEPS, 2, 2, 5], F32) as tab:
            keep["hT"], keep["tab"] = hT, tab
            input_norm(nc, io, keep)
            neighbourhood(nc, io, keep)
            deltanet(nc, io, keep)
            merge(nc, io, keep)
        with nc.sbuf_tensor("logits", [P, TT, NG + NE], F32) as logits, \
                nc.sbuf_tensor("slot", [P, 2, TT], U32) as slot, \
                nc.sbuf_tensor("weight", [P, 2, TT], F32) as weight, \
                nc.sbuf_tensor("owner", [1, NBLK + 1], I32) as owner:
            keep.update(logits=logits, slot=slot, weight=weight, owner=owner)
            first_norm(nc, io, keep)
            route(nc, io, keep)
            experts(nc, io, keep)
            last_norm(nc, io, keep)
```

```python
from contextlib import ExitStack

import numpy as np
import concourse.bass as bass
from concourse import mybir

F32 = mybir.dt.float32
I32 = mybir.dt.int32
U32 = mybir.dt.uint32
ALU = mybir.AluOpType
ACT = mybir.ActivationFunctionType
AX = mybir.AxisListType

P = 128
D = 1024
DC = D // P
META = 16
SEQ = 1024
L = META + SEQ
TT = SEQ // P
GRID_W = 64
ROWS = SEQ // GRID_W
KR = 8
KC = 16
NH = 8
NDH = 64
NA_W = NH * NDH
NPAIR = NH // 2
DRS = 15
GH = 8
GD = 128
HALF = 512
WT = 10
WIDE = WT * P
W_META = P - META
STEPS = TT + 1
LEVELS = 7
NG = 4
EPG = 8
NE = NG * EPG
FE = 256
TB = 16 + NE - 1
NBLK = 48
FULL = 2 * SEQ // P
SLOTS = NBLK * P
LN_EPS = 1e-5
NORM_EPS = 1e-6
ALPHA = 2 ** 0.25
BIG = 1e30

_CONST = [("ident", P), ("ones", P), ("incl", 2 * P), ("level", LEVELS * 2 * P), ("last", P),
          ("first", P), ("before", P), ("colmask", GRID_W),
          ("eps", 8), ("blk", NBLK), ("eidx", NE), ("gidx", NG), ("tok", TT)]
C_AT = {}
_n = 0
for _name, _w in _CONST:
    C_AT[_name] = (_n, _n + _w)
    _n += _w
C_W = _n

_COLS = [("ln0_g", DC), ("ln0_b", DC), ("dt", 1), ("alog", 1), ("conv", GH * 15), ("norm_w", 1)]
V_AT = {}
_n = 0
for _name, _w in _COLS:
    V_AT[_name] = (_n, _n + _w)
    _n += _w
V_W = _n


def constants():
    c = np.zeros((P, C_W), np.float32)

    def put(name, a):
        a0, a1 = C_AT[name]
        c[:, a0:a1] = np.asarray(a, np.float32).reshape(P, a1 - a0)

    i = np.arange(P)
    part, free = i[:, None], i[None, :]
    put("ident", np.eye(P))
    put("ones", np.ones((P, P)))
    put("incl", np.stack([free >= part, free <= part], 1))
    lev = []
    for s in range(LEVELS):
        same = (part >> (s + 1)) == (free >> (s + 1))
        hi, lo = (i >> s) & 1 == 1, (i >> s) & 1 == 0
        lev += [same & lo[:, None] & hi[None, :], same & hi[:, None] & lo[None, :]]
    put("level", np.stack(lev, 1))
    put("last", np.repeat(part == P - 1, P, 1))
    put("first", np.repeat(part == 0, P, 1))
    put("before", part < free)
    col = np.arange(GRID_W)
    start = np.clip(col - KC // 2, 0, GRID_W - KC)
    inside = (col[None, :] >= start[:, None]) & (col[None, :] < start[:, None] + KC)
    put("colmask", np.tile(np.where(inside, 0.0, -BIG), (2, 1)))
    put("eps", np.tile([LN_EPS, 4 * NORM_EPS, NORM_EPS, -0.5 * np.log(GD), 0, 0, 0, 0], (P, 1)))
    put("blk", np.tile(np.arange(NBLK), (P, 1)))
    put("eidx", np.tile(np.arange(NE), (P, 1)))
    put("gidx", np.tile(np.arange(NG), (P, 1)))
    put("tok", part + P * np.arange(TT)[None, :])
    return c


def scan_masks():
    w = np.arange(WIDE)
    return np.tile(np.stack([w % P != 0, w % P != P - 1]).astype(np.float32), (P, 1, 1))


def meet(eng, on, value, mark):
    eng.wait_ge(on, value)
    eng.sem_inc(mark, 1)


def makers(nc, ctx, prefix):
    taken = []

    def sem(n):
        taken.append(nc.alloc_semaphore(f"{prefix}_{n}"))
        return taken[-1]

    def clear():
        nc.clear_and_free_semaphores(taken)
        nc.all_engine_barrier()

    ctx.callback(clear)
    sb = lambda n, s, dt=F32: ctx.enter_context(nc.sbuf_tensor(f"{prefix}_{n}", s, dt))
    ps = lambda n, s: ctx.enter_context(nc.psum_tensor(f"{prefix}_{n}", s, F32))
    return sb, ps, sem


def input_norm(nc, io, keep):
    hT, con, colv, tab = keep["hT"], keep["con"], keep["colv"], keep["tab"]
    with ExitStack() as ctx:
        sb, ps, sem = makers(nc, ctx, "norm0")
        C = lambda n, *s: con[:, C_AT[n][0]:C_AT[n][1]]
        V = lambda n: colv[:, V_AT[n][0]:V_AT[n][1]]
        B = 4
        x = sb("x_rows", [P, B + 1, D])
        stats = sb("stats", [P, B + 1, 12])
        mv = sb("mean_var", [P, B + 1, 4])
        wg = sb("w_gates", [P, DC, P])
        arg = sb("gate_arg", [P, L])
        mag = sb("gate_mag", [P, L])
        soft = sb("gate_soft", [P, L])
        nega = sb("neg_decay", [P, 1])
        g = sb("log_decay", [P, WIDE])
        rows = sb("gate_rows", [P, WIDE])
        scan = sb("scan_masks", [P, 2, WIDE])
        colr = sb("gate_cols", [P, WT, P])
        ends = sb("gate_ends", [P, 2, WT, GH])
        xp = [ps(f"xT{k}", [P, 4, P]) for k in range(2)]
        gp = [ps(f"gates{k}", [P, HALF]) for k in range(2)]
        gm = ps("gates_meta", [P, HALF])
        tp = ps("rows_T", [P, 4, P])
        lp = ps("ends_all", [P, 2, WT, GH])

        const_in, gate_in, xn_out = sem("const_in"), sem("gate_weights_in"), [sem(f"xn_out{k}") for k in range(B)]
        x_in = [sem(f"x_in{k}") for k in range(B + 1)]
        stat, rstd, normed = sem("stat"), sem("rstd"), sem("normed")
        turned, h_dve, h_act = sem("turned"), sem("h_dve"), sem("h_act")
        gated, g_dve, g_act = sem("gated"), sem("g_dve"), sem("g_act")
        rows_T, rows_copied, rows_out = sem("rows_T_done"), sem("rows_copied"), sem("rows_out")
        zeroed = sem("zeroed")
        held, met = sem("held"), sem("met")
        block = ctx.enter_context(nc.Block())

        @block.sync
        def _(sp):
            def load(i, k):
                sp.dma_start(x[:, k, :], io["x"][bass.ds((B * i + k) * P, P), :]).then_inc(x_in[k], 16)

            def store(i, k):
                meet(sp, normed, B * i + k + 2, met)
                sp.dma_start(io["xn"][bass.ds((B * i + k) * P, P), :], x[:, k, :]).then_inc(xn_out[k], 16)

            sp.dma_start(x[0:META, B, :], io["meta"]).then_inc(x_in[B], 16)
            load(0, 0)
            load(0, 1)
            sp.dma_start(con[:, :], io["const"]).then_inc(const_in, 16)
            sp.dma_start(colv[:, :], io["cols"]).then_inc(const_in, 16)
            load(0, 2)
            load(0, 3)
            sp.dma_start(wg[:, :, :], io["w_gates"]).then_inc(gate_in, 16)
            sp.dma_start(scan[:, :, :], io["scan"]).then_inc(gate_in, 16)
            with sp.Fori(0, TT // B - 1) as i:
                for k in range(0, B, 2):
                    store(i, k)
                    store(i, k + 1)
                    for n in (k, k + 1):
                        meet(sp, xn_out[n], 16 * i + 16, met)
                        meet(sp, turned, 2 * (B * i + n) + 4, met)
                        load(i + 1, n)
            for k in range(B):
                store(TT // B - 1, k)
            for k, (name, lo) in enumerate((("f", 0), ("b", 32))):
                for kind, at in ((0, lo), (1, 64 + lo)):
                    for hh in range(2):
                        src = rows[at + hh:at + GH:2, :].rearrange("a (t c) -> a t c", c=P)
                        src = src[:, 0:STEPS, :] if k == 0 else src[:, WT - 1:0:-1, :]
                        if hh == 0 and kind == 0 and k == 0:
                            sp.wait_ge(g_dve, 13)
                        sp.dma_start(io["rows"][:, :, hh, k, kind, :], src).then_inc(rows_out, 16)
            sp.wait_ge(rows_out, 16 * 8)
            for k in range(B):
                sp.wait_ge(xn_out[k], 16 * (TT // B))

        @block.vector
        def _(v):
            def stats_of(u, slot, n, loads):
                v.wait_ge(x_in[slot], 16 * loads)
                for k in range(2):
                    v.bn_stats(stats[0:n, slot, 6 * k:6 * k + 6], x[0:n, slot, HALF * k:HALF * k + HALF]).then_inc(stat, 1)
                meet(v, stat, 3 * u + 2, held)
                v.bn_aggr(mv[0:n, slot, 0:2], stats[0:n, slot, :]).then_inc(stat, 1)

            def norm(u, slot, n, scaled):
                v.wait_ge(rstd, scaled)
                v.tensor_scalar(x[0:n, slot, :], x[0:n, slot, :], mv[0:n, slot, 0:1], mv[0:n, slot, 3:4],
                                ALU.subtract, ALU.mult).then_inc(normed, 1)

            def spread(u, n):
                v.wait_ge(turned, 2 * u + 1)
                for c in range(4):
                    at = (u - 1) * P + META if n == P else 0
                    v.tensor_scalar(hT[:, c, bass.ds(at, n)], xp[0][:, c, 0:n], V("ln0_g")[:, c:c + 1],
                                    V("ln0_b")[:, c:c + 1], ALU.mult, ALU.add).then_inc(h_dve, 1)

            v.memset(rows[:, :], 0.0).then_inc(zeroed, 1)
            v.memset(g[:, :], 0.0).then_inc(zeroed, 1)
            def pairs(i, more):
                for k in range(0, B, 2):
                    if k + 2 < B or more:
                        for n in (k + 2, k + 3):
                            stats_of(B * i + n + 1, n % B, P, i + 1 + n // B)
                    for n in (k, k + 1):
                        norm(B * i + n + 1, n, P, 2 * (B * i + k) + 6)
                    for n in (k, k + 1):
                        spread(B * i + n + 1, P)

            stats_of(0, B, META, 1)
            stats_of(1, 0, P, 1)
            stats_of(2, 1, P, 1)
            norm(0, B, META, 2)
            v.wait_ge(const_in, 32)
            spread(0, META)
            with v.Fori(0, TT // B - 1) as i:
                pairs(i, True)
            pairs(TT // B - 1, False)
            v.wait_ge(gated, 1)
            for k, (bank, a, b) in enumerate(((gm[:, 0:META], 0, META), (gp[0][:, :], META, META + HALF),
                                              (gp[1][:, :], META + HALF, L))):
                v.tensor_scalar(arg[:, a:b], bank, V("dt"), None, ALU.add).then_inc(g_dve, 1)
            v.wait_ge(g_dve, 3)
            v.scalar_tensor_tensor(mag[:, :], arg[:, :], -1.0, arg[:, :], ALU.mult, ALU.max).then_inc(g_dve, 1)
            v.wait_ge(g_act, 3)
            v.scalar_tensor_tensor(soft[0:64, :], arg[0:64, :], 0.0, mag[0:64, :], ALU.max, ALU.add).then_inc(g_dve, 1)
            v.tensor_scalar(nega[:, :], nega[:, :], -1.0, None, ALU.mult).then_inc(g_dve, 1)
            v.scalar_tensor_tensor(soft[64:P, :], arg[64:P, :], 0.0, mag[64:P, :], ALU.min, ALU.subtract).then_inc(g_dve, 1)
            v.wait_ge(g_dve, 7)
            v.wait_ge(zeroed, 2)
            v.tensor_scalar(g[0:64, W_META:W_META + L], soft[0:64, :], nega[0:64, :], None, ALU.mult).then_inc(g_dve, 1)
            v.tensor_scalar(g[0:64, (WT - 1) * P:(WT - 1) * P + META], soft[0:64, 0:META][:, ::-1],
                            nega[0:64, :], None, ALU.mult).then_inc(g_dve, 1)
            v.wait_ge(g_act, 5)
            v.tensor_copy(rows[96:P, (WT - 1) * P:(WT - 1) * P + META], rows[96:P, W_META:P][:, ::-1]).then_inc(g_dve, 1)
            v.wait_ge(g_dve, 9)
            v.wait_ge(gate_in, 32)
            v.tensor_tensor_scan(rows[0:32, 0:(WT - 1) * P], scan[0:32, 0, 0:(WT - 1) * P], g[0:32, 0:(WT - 1) * P],
                                 0.0, ALU.mult, ALU.add).then_inc(g_dve, 1)
            v.tensor_tensor_scan(rows[32:64, P:WIDE][:, ::-1], scan[32:64, 1, P:WIDE][:, ::-1],
                                 g[32:64, P:WIDE][:, ::-1], 0.0, ALU.mult, ALU.add).then_inc(g_dve, 1)
            v.wait_ge(g_dve, 12)
            v.wait_ge(g_act, 5)
            v.memset(ends[:, :, :, :], 0.0).then_inc(g_dve, 1)
            for b, t0, n in ((0, 0, 4), (1, 4, 4), (2, 8, 2)):
                v.wait_ge(rows_T, b + 1)
                v.tensor_copy(colr[:, t0:t0 + n, :], tp[:, 0:n, :]).then_inc(rows_copied, 1)
            v.wait_ge(rows_T, 4)
            v.wait_ge(g_dve, 13)
            v.tensor_copy(ends[:, :, :, :], lp[:, :, :, :]).then_inc(g_dve, 1)
            v.wait_ge(g_dve, 14)
            last = 14
            for d, tiles in ((0, slice(0, STEPS)), (1, slice(WT - 1, 0, -1))):
                e = ends[:, d, tiles, :]
                col = colr[:, tiles, 32 * d:32 * d + GH]
                bet = colr[:, tiles, 64 + 32 * d:64 + 32 * d + GH]
                split = lambda a: a.rearrange("p s (q h) -> p q s h", h=2)
                for q in range(GH // 2):
                    t = lambda kind: tab[:, q, :, :, d, kind]
                    s = slice(2 * q, 2 * q + 2)
                    v.tensor_copy(t(0), col[:, :, s]).then_inc(g_dve, 1)
                    v.tensor_scalar(t(1), bet[:, :, s], 0.5, None, ALU.mult).then_inc(g_dve, 1)
                    v.tensor_copy(t(2), col[:, :, s]).then_inc(g_dve, 1)
                    v.tensor_tensor(t(3), e[:, :, s], col[:, :, s], ALU.subtract).then_inc(g_dve, 1)
                    v.tensor_copy(t(4), e[:, :, s]).then_inc(g_dve, 1)
            v.wait_ge(g_act, 6)
            for d, tiles in ((0, slice(0, STEPS)), (1, slice(WT - 1, 0, -1))):
                bet = colr[:, tiles, 64 + 32 * d:64 + 32 * d + GH]
                for q in range(GH // 2):
                    t = tab[:, q, :, :, d, 2]
                    v.tensor_tensor(t, t, bet[:, :, 2 * q:2 * q + 2], ALU.mult).then_inc(g_dve, 1)

        @block.scalar
        def _(act):
            def scale_of(u, num, slot, n):
                act.wait_ge(stat, 3 * (u + num))
                act.activation(mv[0:n, slot:slot + num, 2:3], mv[0:n, slot:slot + num, 1:2], ACT.Ln,
                               bias=C("eps")[0:n, 0:1]).then_inc(rstd, num)
                act.wait_ge(rstd, 2 * u + num)
                act.activation(mv[0:n, slot:slot + num, 3:4], mv[0:n, slot:slot + num, 2:3], ACT.Exp, scale=-0.5).then_inc(rstd, num)

            def spread(u, n):
                act.wait_ge(turned, 2 * u + 2)
                for c in range(4):
                    at = (u - 1) * P + META if n == P else 0
                    act.activation(hT[:, 4 + c, bass.ds(at, n)], xp[1][:, c, 0:n], ACT.Identity,
                                   bias=V("ln0_b")[:, 4 + c:5 + c], scale=V("ln0_g")[:, 4 + c:5 + c]).then_inc(h_act, 1)

            def pairs(i, more):
                for k in range(0, B, 2):
                    if k + 2 < B or more:
                        scale_of(B * i + k + 3, 2, (k + 2) % B, P)
                    for n in (k, k + 1):
                        spread(B * i + n + 1, P)

            act.wait_ge(const_in, 32)
            scale_of(0, 1, B, META)
            scale_of(1, 2, 0, P)
            spread(0, META)
            with act.Fori(0, TT // B - 1) as i:
                pairs(i, True)
            pairs(TT // B - 1, False)
            act.activation(nega[:, :], V("alog"), ACT.Exp).then_inc(g_act, 1)
            act.wait_ge(g_dve, 4)
            act.activation(mag[:, :], mag[:, :], ACT.Exp, scale=-1.0).then_inc(g_act, 1)
            act.wait_ge(g_act, 2)
            act.activation(mag[:, :], mag[:, :], ACT.Ln, bias=1.0).then_inc(g_act, 1)
            act.wait_ge(g_dve, 7)
            act.wait_ge(zeroed, 2)
            for p in (64, 96):
                act.activation(rows[p:p + 32, W_META:W_META + L], soft[p:p + 32, :], ACT.Exp).then_inc(g_act, 1)
            act.wait_ge(g_dve, 14 + 10 * (GH // 2))
            act.activation(tab[:, :, :, :, :, 2:5].rearrange("p q s h d k -> p (q s h d) k"),
                           tab[:, :, :, :, :, 2:5].rearrange("p q s h d k -> p (q s h d) k"), ACT.Exp).then_inc(g_act, 1)

        @block.tensor
        def _(pe):
            ident = C("ident")

            def unit(u, slot, n):
                pe.wait_ge(normed, u + 1)
                for k, read in ((0, h_dve), (1, h_act)):
                    pe.wait_ge(read, 4 * u)
                    for c in range(4):
                        cc = 4 * k + c
                        ins = pe.transpose(xp[k][:, c, 0:n], x[0:n, slot, cc * P:cc * P + P], ident[0:n, 0:n])
                    ins.then_inc(turned, 1)

            pe.wait_ge(const_in, 32)
            unit(0, B, META)
            with pe.Fori(0, TT // B) as i:
                for k in range(B):
                    unit(B * i + k + 1, k, P)
            pe.wait_ge(gate_in, 32)
            pe.wait_ge(h_dve, 4 * STEPS)
            pe.wait_ge(h_act, 4 * STEPS)
            for bank, a, n in ((gm, 0, META), (gp[0], META, HALF), (gp[1], META + HALF, HALF)):
                for c in range(DC):
                    ins = pe.matmul(bank[:, 0:n], wg[:, c, :], hT[:, c, a:a + n], start=(c == 0), stop=(c == DC - 1))
            ins.then_inc(gated, 1)
            pe.wait_ge(g_dve, 12)
            pe.wait_ge(g_act, 5)
            for b, t0, n in ((0, 0, 4), (1, 4, 4), (2, 8, 2)):
                pe.wait_ge(rows_copied, b)
                for t in range(n):
                    ins = pe.transpose(tp[:, t, :], rows[:, (t0 + t) * P:(t0 + t + 1) * P], ident)
                ins.then_inc(rows_T, 1)
            pe.wait_ge(rows_copied, 3)
            pe.matmul(lp[:, 0, :, :], C("last"), colr[:, :, 0:GH], start=True, stop=True, skip_group_check=True)
            pe.matmul(lp[:, 1, :, :], C("first"), colr[:, :, 32:32 + GH], start=True, stop=True,
                      skip_group_check=True).then_inc(rows_T, 1)


def neighbourhood(nc, io, keep):
    hT, con = keep["hT"], keep["con"]
    with ExitStack() as ctx:
        sb, ps, sem = makers(nc, ctx, "na")
        ident = con[:, C_AT["ident"][0]:C_AT["ident"][1]]
        colmask = con[:, C_AT["colmask"][0]:C_AT["colmask"][1]]
        WIN = KR * GRID_W
        SCALE = NDH ** -0.5
        first_row = [min(max(r - KR // 2, 0), ROWS - KR) for r in range(ROWS)]
        first_bias = [first_row[r] - r + KR - 1 for r in range(ROWS)]
        v_from = [0] + [META + P * m for m in range(TT)] + [META + GRID_W + P * m for m in range(TT - 1)]
        v_tile = lambda row, j: 1 + row // 2 + j if row % 2 == 0 else 1 + TT + row // 2 + j

        w = sb("w_qkv", [P, DC, 3, P])
        bias = sb("bias", [P, DRS, GRID_W])
        qb = sb("q_blocks", [P, ROWS, P])
        kT = sb("kT", [P, L])
        vT = sb("vT", [P, L])
        vt = sb("v_tiles", [P, 2 * TT, P])
        s_ = sb("scores", [P, 3, META + WIN])
        nm = sb("minus_max", [P, 3])
        sm = sb("exp_sum", [P, 3])
        rs = sb("one_over_sum", [P, 3])
        pt = sb("probs_T", [P, 2, WIN])
        ptm = sb("probs_meta_T", [META, 2, P])
        on = sb("o_heads", [P, SEQ])
        bank = [ps(f"bank{k}", [P, HALF]) for k in range(8)]

        w_in, bias_in, bias_ok, q_zero = sem("w_qkv_in"), sem("bias_in"), sem("bias_masked"), sem("q_blocks_zero")
        proj, qkv_in, v_turned, vt_in = sem("projected"), sem("qkv_in"), sem("v_turned"), sem("v_tiles_in")
        scored, biased, maxed, exped = sem("scored"), sem("biased"), sem("maxed"), sem("exp_done")
        inv, normed, p_turned, pt_in = sem("one_over_sum_made"), sem("probs_normed"), sem("probs_turned"), sem("probs_T_in")
        pv, o_in, ona_out, met = sem("values_weighted"), sem("o_in"), sem("ona_out"), sem("met")
        block = ctx.enter_context(nc.Block())

        @block.sync
        def _(sp):
            def weights(p):
                sp.dma_start(w[:, :, :, :], io["w_na3"][bass.ds(p, 1), :, :, :, :]
                             .rearrange("a p c m n -> p (a c) m n")).then_inc(w_in, 16)

            def pair(p, more):
                meet(sp, biased, p * ROWS, met)
                sp.dma_start(bias[:, :, :], io["bias"][bass.ds(p, 1), :, :, :]
                             .rearrange("a p r c -> p (a r) c")).then_inc(bias_in, 16)
                if more:
                    meet(sp, proj, p * 3 + 3, met)
                    weights(p + 1)
                meet(sp, o_in, p * ROWS + ROWS, met)
                sp.dma_start(io["ona"][bass.ds(p, 1), :, :].rearrange("a p t -> (a p) t"), on[:, :]).then_inc(ona_out, 16)

            weights(0)
            with sp.Fori(0, NPAIR - 1) as p:
                pair(p, True)
            pair(NPAIR - 1, False)
            sp.wait_ge(ona_out, 16 * NPAIR)

        @block.tensor
        def _(pe):
            with pe.Fori(0, NPAIR) as p:
                at = lambda r: p * ROWS + r
                pe.wait_ge(w_in, p * 16 + 16)
                pe.wait_ge(o_in, p * ROWS)
                for m in range(3):
                    for c in range(DC):
                        first, final = c == 0, c == DC - 1
                        if m:
                            pe.matmul(bank[5 + m][:, 0:META], w[:, c, m, :], hT[:, c, 0:META], start=first, stop=final)
                        for k in range(2):
                            ins = pe.matmul(bank[2 * m + k][:, :], w[:, c, m, :],
                                            hT[:, c, META + HALF * k:META + HALF * (k + 1)], start=first, stop=final)
                    ins.then_inc(proj, 1)
                pe.wait_ge(qkv_in, p * 3 + 3)
                for b in range(4):
                    pe.wait_ge(vt_in, p * 4 + max(b - 1, 0))
                    for j in range(4):
                        i = 4 * b + j
                        n = P if i else META
                        ins = pe.transpose(bank[6 + b % 2][0:n, P * j:P * j + P], vT[:, v_from[i]:v_from[i] + n], ident)
                    ins.then_inc(v_turned, 1)
                for r in range(ROWS + 3):
                    if r < ROWS:
                        pe.wait_ge(biased, at(max(r - 1, 0)))
                        k0 = META + GRID_W * first_row[r]
                        pe.matmul(bank[r % 2][:, :], qb[:, r, :], kT[:, k0:k0 + WIN], start=True, stop=True)
                        pe.matmul(bank[2 + r % 2][:, 0:META], qb[:, r, :], kT[:, 0:META], start=True,
                                  stop=True).then_inc(scored, 1)
                    if 2 <= r < ROWS + 2:
                        q = r - 2
                        pe.wait_ge(normed, at(q) + 1)
                        pe.wait_ge(pt_in, at(q))
                        if q == 0:
                            pe.wait_ge(vt_in, p * 4 + 4)
                        for j in range(4):
                            pe.transpose(bank[4 + q % 2][:, P * j:P * j + P], s_[:, q % 3, META + P * j:META + P * j + P], ident)
                        pe.transpose(bank[6][0:META, 0:P], s_[:, q % 3, 0:META], ident).then_inc(p_turned, 1)
                    if r >= 3:
                        q = r - 3
                        pe.wait_ge(pt_in, at(q) + 1)
                        pe.wait_ge(o_in, at(q))
                        pe.matmul(bank[7][:, 0:P], vt[0:META, 0, :], ptm[:, q % 2, :], start=True, stop=False)
                        for j in range(4):
                            ins = pe.matmul(bank[7][:, 0:P], vt[:, v_tile(first_row[q], j), :],
                                            pt[:, q % 2, P * j:P * j + P], start=False, stop=(j == 3))
                        ins.then_inc(pv, 1)

        @block.scalar
        def _(act):
            with act.Fori(0, NPAIR) as p:
                at = lambda r: p * ROWS + r
                act.wait_ge(proj, p * 3 + 1)
                act.wait_ge(q_zero, 1)
                for k in range(2):
                    rows = slice(ROWS // 2 * k, ROWS // 2 * (k + 1))
                    src = bank[k][:, :].rearrange("p (r c) -> p r c", c=GRID_W)
                    act.activation(qb[0:NDH, rows, 0:GRID_W], src[0:NDH, :, :], ACT.Copy)
                    ins = act.activation(qb[NDH:P, rows, GRID_W:P], src[NDH:P, :, :], ACT.Copy)
                ins.then_inc(qkv_in, 1)
                for m, dst in ((1, kT), (2, vT)):
                    act.wait_ge(proj, p * 3 + m + 1)
                    act.activation(dst[:, 0:META], bank[5 + m][:, 0:META], ACT.Copy)
                    for k in range(2):
                        ins = act.activation(dst[:, META + HALF * k:META + HALF * (k + 1)], bank[2 * m + k][:, :], ACT.Copy)
                    ins.then_inc(qkv_in, 1)
                for b in range(4):
                    act.wait_ge(v_turned, p * 4 + b + 1)
                    if b == 0:
                        act.activation(vt[0:META, 0, :], bank[6][0:META, 0:P], ACT.Copy)
                    lo = 1 if b == 0 else 0
                    act.activation(vt[:, 4 * b + lo:4 * b + 4, :], bank[6 + b % 2][:, P * lo:4 * P]
                                   .rearrange("p (j c) -> p j c", c=P), ACT.Copy).then_inc(vt_in, 1)
                for r in range(ROWS + 2):
                    if r < ROWS:
                        act.wait_ge(maxed, at(r) + 1)
                        act.wait_ge(inv, at(max(r - 2, 0)))
                        act.activation(s_[:, r % 3, :], s_[:, r % 3, :], ACT.Exp, bias=nm[:, r % 3:r % 3 + 1],
                                       accum_out=sm[:, r % 3:r % 3 + 1]).then_inc(exped, 1)
                    if r >= 2:
                        q = r - 2
                        act.wait_ge(p_turned, at(q) + 1)
                        act.wait_ge(pv, at(max(q - 1, 0)))
                        act.activation(pt[:, q % 2, :], bank[4 + q % 2][:, :], ACT.Copy)
                        act.activation(ptm[:, q % 2, :], bank[6][0:META, 0:P], ACT.Copy).then_inc(pt_in, 1)

        @block.vector
        def _(v):
            v.memset(qb[:, :, :], 0.0).then_inc(q_zero, 1)
            with v.Fori(0, NPAIR) as p:
                at = lambda r: p * ROWS + r
                v.wait_ge(bias_in, p * 16 + 16)
                v.tensor_tensor(bias[:, :, :], bias[:, :, :], colmask.unsqueeze(1).to_broadcast([P, DRS, GRID_W]),
                                ALU.add).then_inc(bias_ok, 1)
                v.wait_ge(bias_ok, p + 1)
                for r in range(ROWS + 4):
                    if r >= 4:
                        q = r - 4
                        v.wait_ge(pv, at(q) + 1)
                        if q == 0:
                            v.wait_ge(ona_out, p * 16)
                        for h in range(2):
                            a = NDH * h
                            ins = v.tensor_copy(on[a:a + NDH, GRID_W * q:GRID_W * (q + 1)], bank[7][a:a + NDH, a:a + NDH])
                        ins.then_inc(o_in, 1)
                    if r < ROWS:
                        v.wait_ge(scored, at(r) + 1)
                        v.wait_ge(p_turned, at(max(r - 2, 0)))
                        v.scalar_tensor_tensor(s_[:, r % 3, META:META + WIN], bank[r % 2][:, :], SCALE,
                                               bias[:, first_bias[r]:first_bias[r] + KR, :].rearrange("p r c -> p (r c)"),
                                               ALU.mult, ALU.add)
                        v.tensor_scalar(s_[:, r % 3, 0:META], bank[2 + r % 2][:, 0:META], SCALE, None, ALU.mult).then_inc(biased, 1)
                        v.wait_ge(biased, at(r) + 1)
                        v.wait_ge(exped, at(max(r - 2, 0)))
                        v.tensor_reduce(nm[:, r % 3:r % 3 + 1], s_[:, r % 3, :], AX.X, ALU.max, negate=True).then_inc(maxed, 1)
                    if 1 <= r <= ROWS:
                        q = r - 1
                        v.wait_ge(exped, at(q) + 1)
                        v.wait_ge(normed, at(max(q - 2, 0)))
                        v.reciprocal(rs[:, q % 3:q % 3 + 1], sm[:, q % 3:q % 3 + 1]).then_inc(inv, 1)
                        v.wait_ge(inv, at(q) + 1)
                        v.tensor_scalar(s_[:, q % 3, :], s_[:, q % 3, :], rs[:, q % 3:q % 3 + 1], None, ALU.mult).then_inc(normed, 1)


def deltanet(nc, io, keep):
    hT, con, colv, tab = keep["hT"], keep["con"], keep["colv"], keep["tab"]
    NI = 4
    with ExitStack() as ctx:
        sb, ps, sem = makers(nc, ctx, "gdn")
        C = lambda n: con[:, C_AT[n][0]:C_AT[n][1]]
        V = lambda n: colv[:, V_AT[n][0]:V_AT[n][1]]
        ident = C("ident")
        ident4 = ident.unsqueeze(1).to_broadcast([P, NI, P])
        incl = C("incl").rearrange("p (d t) -> p d t", d=2).unsqueeze(1).to_broadcast([P, 2, 2, P])
        level = lambda k: C("level").rearrange("p (l d t) -> p l d t", l=LEVELS, d=2)[:, k, :, :]\
            .unsqueeze(1).to_broadcast([P, 2, 2, P])
        by_dir = lambda a: a.rearrange("p (h d) t -> p h d t", d=2)

        w = sb("w_head", [P, 4, DC, P])
        raw = sb("raw", [P, 3, L + 4])
        acc = sb("conv_sum", [P, 3, L])
        th = sb("tanh", [P, 2, L])
        wide = sb("wide", [P, 2, 3, WIDE])
        zb = sb("z_gate", [P, 2, SEQ])
        ot = sb("o_scan", [P, 2, 2, STEPS * P])
        rows = sb("decay_beta_rows", [P, NI, 2, P])
        kqv = sb("kqv", [P, NI, 3, P])
        tc = sb("tile_cols", [P, 2, NI, 4])
        te = sb("end_decay", [P, NI, 1])
        dd = sb("decays", [P, NI, P])
        mt = sb("M_T", [P, NI, P])
        at = sb("A_T", [P, 2, NI, P])
        ml = sb("M_level_T", [P, LEVELS, NI, P])
        vb = sb("v_beta", [P, 2, NI, P])
        eq = sb("q_decay", [P, NI, P])
        qd = sb("q_decayed", [P, 2, NI, P])
        vn = sb("v_new", [P, NI, P])
        st = sb("state", [P, NI, P])
        zeros = sb("zeros", [P, P])
        part = lambda b, a, n: b[:, :, :].rearrange("p a t -> p (a t)")[:, a * P:(a + n) * P].rearrange("p (j t) -> p j t", t=P)
        ttt = part(acc, 0, 16).rearrange("p (r h a d) t -> p r h a d t", r=2, h=2, a=2)
        x_ = part(acc, 16, NI)
        wtn = part(acc, 16 + NI, NI)
        kbe = part(th, 0, 2 * NI).rearrange("p (r i) t -> p r i t", r=2)
        kde = part(th, 2 * NI, 2 * NI).rearrange("p (r i) t -> p r i t", r=2)
        bank = [ps(f"bank{k}", [P, NI, P]) for k in range(8)]
        flat = lambda b: bank[b][:, :, :].rearrange("p a b -> p (a b)")
        G0, G1, KB, VB, XB, _, PB, _ = range(8)
        nth = lambda u, k, h: u * (2 * (LEVELS - 1)) + (2 * (k - 1) + h)
        PER = 2 * (LEVELS - 1)

        pads = sem("pads_zero")
        w_in = [sem(f"w_head_in{m}") for m in range(4)]
        proj, raw_in, conv = sem("projected"), sem("raw_in"), sem("conv_step")
        tanhd, silu, squared, ssq = sem("tanh_done"), sem("silu_done"), sem("squared"), sem("square_sums")
        rn, wide_in, back_in = sem("reciprocal_norms"), sem("wide_in"), sem("meta_reversed")
        rows_in, kqv_in, tc_in = sem("rows_in"), sem("kqv_in"), sem("tile_cols_in")
        gram, turned = sem("gram"), sem("k_v_turned")
        dd_d, dd_e, dd_m = sem("decay_differences"), sem("decays_done"), sem("decays_masked")
        mt_d, at_d, mt_b, ml_d = sem("M_T_made"), sem("A_T_made"), sem("M_T_beta"), sem("M_level_made")
        x0, xs, pr = sem("first_level_turned"), sem("M_T_product"), sem("T_M_T_product")
        t0, tt0, t_up, x_cp, te_in = sem("T_started"), sem("T_T_started"), sem("T_updated"), sem("product_copied"), sem("end_decay_in")
        kbe_d, kde_d, vb_d = sem("k_beta_decay_made"), sem("k_to_end_made"), sem("v_beta_made")
        eq_d, qd_d, pw, wtn_d = sem("q_decay_made"), sem("q_decayed_made"), sem("W_T"), sem("minus_W_T_made")
        vnp, vn_d, op, o_cp = sem("v_new_sum"), sem("v_new_made"), sem("o_sum"), sem("o_copied")
        sps, s_up, s_zero = sem("state_sum"), sem("state_updated"), sem("state_zero")
        o_add, o_sq, o_ssq, o_rn = sem("o_added"), sem("o_squared"), sem("o_square_sums"), sem("o_rms")
        o_gated, og_out, met, held = sem("o_gated"), sem("og_out"), sem("met"), sem("held")
        y_zero = sem("y_rows_zero")
        block = ctx.enter_context(nc.Block())

        @block.sync
        def _(sp):
            def weights(hd, m):
                sp.dma_start(w[:, m, :, :], io["w_gdn"][bass.ds(hd, 1), :, m, :, :]
                             .rearrange("a p c n -> p (a c) n")).then_inc(w_in[m], 16)

            def next_weights(hd):
                for m in range(4):
                    meet(sp, proj, hd * 4 + m + 1, met)
                    weights(hd + 1, m)

            for m in range(4):
                weights(0, m)
            def pair(p, more):
                next_weights(2 * p)
                if more:
                    next_weights(2 * p + 1)
                with sp.Fori(0, STEPS) as s:
                    u = p * STEPS + s
                    for used in (dd_d, eq_d):
                        meet(sp, used, u, met)
                    meet(sp, mt_b, u, met)
                    src = io["rows"].rearrange("q s h d k t -> (q s) (h d k t)")[bass.ds(u, 1), :]
                    sp.dma_start(rows[:, :, :, :].rearrange("p i k t -> p (i k t)"),
                                 src.to_broadcast([P, NI * 2 * P])).then_inc(rows_in, 16)
                meet(sp, o_gated, p * 2 + 2, met)
                sp.dma_start(io["og"][bass.ds(2 * p, 2), :, :].rearrange("h p t -> p h t"), ot[:, :, 0, P:]).then_inc(og_out, 16)

            with sp.Fori(0, NPAIR - 1) as p:
                pair(p, True)
            pair(NPAIR - 1, False)
            sp.wait_ge(og_out, 16 * NPAIR)
            sp.wait_ge(y_zero, 16)

        @block.tensor
        def _(pe):
            ones = C("ones")

            def project(hd, m, copied, read=None):
                pe.wait_ge(w_in[m], hd * 16 + 16)
                if copied is not None:
                    pe.wait_ge(raw_in, copied)
                if read is not None:
                    pe.wait_ge(rn, read)
                b = 2 * (m % 2)
                for c in range(DC):
                    first, final = c == 0, c == DC - 1
                    if m < 3:
                        pe.matmul(flat(XB + m % 2)[:, 0:META], w[:, m, c, :], hT[:, c, 0:META], start=first, stop=final,
                                  skip_group_check=True)
                    for k in range(2):
                        ins = pe.matmul(flat(b + k), w[:, m, c, :], hT[:, c, META + HALF * k:META + HALF * (k + 1)],
                                        start=first, stop=final)
                ins.then_inc(proj, 1)

            def square_sum(hd, m):
                pe.wait_ge(squared, hd * 2 + m + 1)
                pe.wait_ge(rn, hd * 4 + m)
                pe.wait_ge(raw_in, hd * 4 + 2)
                pe.matmul(flat(XB + 1)[:, META:2 * META], ones, raw[:, m, 0:META], start=True, stop=True, skip_group_check=True)
                for k in range(2):
                    ins = pe.matmul(flat(PB + k), ones, raw[:, m, META + HALF * k:META + HALF * (k + 1)], start=True, stop=True)
                ins.then_inc(ssq, 1)

            def rest_of_head(hd):
                square_sum(hd, 0)
                project(hd, 2, hd * 4 + 1)
                square_sum(hd, 1)
                project(hd, 3, hd * 4 + 2)

            each = range(NI)

            def gram_w(w, tails):
                pe.wait_ge(kqv_in, w + 1)
                pe.wait_ge(o_cp, tails)
                pe.wait_ge(wtn_d, tails)
                for j in each:
                    ins = pe.matmul(bank[G0 + j // 2][:, 2 * (j % 2):2 * (j % 2) + 2, :], kqv[:, j, 0, :],
                                    kqv[:, j, 0:2, :], start=True, stop=True, skip_group_check=True)
                ins.then_inc(gram, 1)

            def turn_w(w, tails):
                for m, b, read in ((0, KB, vn_d), (2, VB, s_up)):
                    pe.wait_ge(read, tails)
                    for j in each:
                        ins = pe.transpose(bank[b][:, j, :], kqv[:, j, m, :], ident)
                    ins.then_inc(turned, 1)

            def first_level(w):
                pe.wait_ge(ml_d, w * LEVELS + 1)
                pe.wait_ge(at_d, w + 1)
                for j in each:
                    ins = pe.transpose(bank[G0][:, j, :], ml[:, 0, j, :], ident)
                ins.then_inc(x0, 1)

            def tail_w(v, prepared, r):
                pe.wait_ge(kbe_d, v + 1)
                pe.wait_ge(t_up, (v + 1) * PER)
                pe.wait_ge(at_d, prepared)
                for j in each:
                    ins = pe.matmul(bank[G1][:, j, :], kbe[:, r, j, :], ttt[:, r, j // 2, 1, j % 2, :], start=True, stop=True,
                                    skip_group_check=True)
                ins.then_inc(pw, 1)

            def tail_v(v, prepared, r):
                pe.wait_ge(vb_d, v + 1)
                pe.wait_ge(wtn_d, v + 1)
                pe.wait_ge(s_up, v)
                pe.wait_ge(kde_d, prepared)
                for j in each:
                    pe.matmul(bank[KB][:, j, :], ttt[:, r, j // 2, 1, j % 2, :], vb[:, r, j, :], start=True, stop=False,
                              skip_group_check=True)
                    ins = pe.matmul(bank[KB][:, j, :], wtn[:, j, :], st[:, j, :], start=False, stop=True,
                                    skip_group_check=True)
                ins.then_inc(vnp, 1)

            def tail_o(v, prepared, r):
                pe.wait_ge(vn_d, v + 1)
                pe.wait_ge(vb_d, prepared)
                for j in each:
                    ins = pe.matmul(bank[VB][:, j, :], kde[:, r, j, :], vn[:, j, :], start=True, stop=True,
                                    skip_group_check=True)
                ins.then_inc(sps, 1)
                pe.wait_ge(qd_d, v + 1)
                pe.wait_ge(t0, prepared)
                for j in each:
                    pe.matmul(bank[G0][:, j, :], st[:, j, :], qd[:, r, j, :], start=True, stop=False, skip_group_check=True)
                    ins = pe.matmul(bank[G0][:, j, :], vn[:, j, :], at[:, r, j, :], start=False, stop=True,
                                    skip_group_check=True)
                ins.then_inc(op, 1)

            def step(u, r, tail, prepare):
                def product(k, h):
                    pe.wait_ge(ml_d, u * LEVELS + k + 1)
                    if k == 1:
                        pe.wait_ge(t0, u + 1)
                    else:
                        pe.wait_ge(t_up, nth(u, k - 1, h) + 1)
                    for j in range(2):
                        ins = pe.matmul(bank[XB + h][:, j, :], ml[:, k, 2 * h + j, :], ttt[:, r, h, 0, j, :],
                                        start=True, stop=True, skip_group_check=True)
                    ins.then_inc(xs, 1)

                for k in range(1, LEVELS):
                    product(k, 0)
                    if k == 1:
                        product(k, 1)
                    if tail and k <= 3:
                        (tail_w, tail_v, tail_o)[k - 1](u - 1, u + 1, 1 - r)
                    if prepare:
                        if k == 4:
                            gram_w(u + 1, u)
                        if k == 5:
                            turn_w(u + 1, u)
                        if k == 6:
                            first_level(u + 1)
                    if k > 1:
                        product(k, 1)
                    for h in range(2):
                        pe.wait_ge(x_cp, nth(u, k, h) + 1)
                        if k == 1:
                            pe.wait_ge(tt0, u + 1)
                            pe.wait_ge(t_up, u * PER)
                        for j in range(2):
                            if k < LEVELS - 1:
                                pe.matmul(bank[PB + h][:, j, :], ttt[:, r, h, 1, j, :], x_[:, 2 * h + j, :], start=True,
                                          stop=True, skip_group_check=True)
                            ins = pe.matmul(bank[PB + h][:, 2 + j, :], x_[:, 2 * h + j, :], ttt[:, r, h, 1, j, :],
                                            start=True, stop=True, skip_group_check=True)
                        ins.then_inc(pr, 1)

            for m in range(2):
                project(0, m, None)
            with pe.Fori(0, NPAIR) as p:
                h0, h1 = 2 * p, 2 * p + 1
                rest_of_head(h0)
                project(h1, 0, h1 * 4 - 1)
                project(h1, 1, h1 * 4, h1 * 4 - 2)
                rest_of_head(h1)
                pe.wait_ge(rn, h1 * 4 + 4)
                pe.wait_ge(raw_in, h1 * 4 + 3)
                u0 = p * STEPS
                pe.wait_ge(s_zero, p + 1)
                gram_w(u0, u0)
                pe.wait_ge(raw_in, h1 * 4 + 4)
                turn_w(u0, u0)
                first_level(u0)
                step(u0, 0, False, True)
                with pe.Fori(0, (STEPS - 3) // 2) as i:
                    step(u0 + 2 * i + 1, 1, True, True)
                    step(u0 + 2 * i + 2, 0, True, True)
                step(u0 + STEPS - 2, 1, True, True)
                step(u0 + STEPS - 1, 0, True, False)
                for part in (tail_w, tail_v, tail_o):
                    part(u0 + STEPS - 1, u0 + STEPS, 0)
                pe.wait_ge(o_sq, p + 1)
                pe.wait_ge(vn_d, (p + 1) * STEPS)
                pe.wait_ge(s_up, (p + 1) * STEPS)
                pe.wait_ge(o_cp, (p + 1) * STEPS)
                for h in range(2):
                    for k in range(2):
                        ins = pe.matmul(flat((PB, KB)[h] + k), ones, th[:, h, HALF * k:HALF * (k + 1)], start=True, stop=True)
                ins.then_inc(o_ssq, 1)
                with pe.If(p < NPAIR - 1):
                    project(h0 + 2, 0, h0 * 4 + 8)
                    pe.wait_ge(o_rn, p * 2 + 1)
                    project(h0 + 2, 1, h0 * 4 + 8, h0 * 4 + 8)

        @block.scalar
        def _(act):
            eps = C("eps")
            act.wait_ge(pads, 4)
            act.wait_ge(w_in[1], 16)
            act.dma_start(io["y"][FULL * P:SLOTS, :].rearrange("(p n) (a b) -> p (n a) b", p=P, b=P),
                          zeros[:, :].unsqueeze(1).to_broadcast([P, (NBLK - FULL) * DC, P])).then_inc(y_zero, 16)
            each = range(NI)

            def head(p, hd, hh):
                def fetch(m):
                    act.wait_ge(proj, hd * 4 + m + 1)
                    for k, (a, n) in enumerate(((0, META), (META, HALF), (META + HALF, HALF))):
                        src = (flat(XB + m % 2)[:, 0:META], flat(2 * (m % 2)), flat(2 * (m % 2) + 1))[k]
                        if m == 3:
                            if k:
                                ins = act.activation(zb[:, bass.ds(hh, 1), HALF * (k - 1):HALF * k], src.unsqueeze(1), ACT.Copy)
                        else:
                            ins = act.activation(raw[:, m, 2 + a:2 + a + n], src, ACT.Copy)
                    ins.then_inc(raw_in, 1)

                def tanh(m):
                    if m < 3:
                        act.wait_ge(conv, hd * 15 + 5 * m + 5)
                    meet(act, silu, hd * 4 + max(m - 1, 0), held)
                    src = acc[:, m, :] if m < 3 else zb[:, bass.ds(hh, 1), :].rearrange("p a t -> p (a t)")
                    if m == 3:
                        meet(act, raw_in, hd * 4 + 4, held)
                    act.activation(th[:, m % 2, 0:src.shape[1]], src, ACT.Tanh, scale=0.5).then_inc(tanhd, 1)

                def square(m):
                    act.wait_ge(silu, hd * 4 + m + 1)
                    act.wait_ge(conv, hd * 15 + 5 * m + 5)
                    act.activation(raw[:, m, 0:L], acc[:, m, :], ACT.Square).then_inc(squared, 1)

                def log_of(m):
                    act.wait_ge(ssq, hd * 2 + m + 1)
                    for src, a, n in ((flat(XB + 1)[:, META:2 * META], 0, META), (flat(PB), META, HALF), (flat(PB + 1), META + HALF, HALF)):
                        ins = act.activation(raw[:, m, a:a + n], src, ACT.Ln, bias=eps[:, 1:2])
                    ins.then_inc(rn, 1)

                def gate():
                    fetch(3)
                    tanh(3)

                act.wait_ge(wide_in, hd * 2)
                act.wait_ge(pads, 2)
                fetch(0)
                act.wait_ge(o_gated, p * 2)
                tanh(0)
                square(0)
                fetch(1)
                tanh(1)
                square(1)
                log_of(0)
                act.wait_ge(conv, hd * 15)
                fetch(2)
                tanh(2)
                log_of(1)
                for m in range(2):
                    act.wait_ge(rn, hd * 4 + m + 1)
                    if m == 0:
                        act.activation(raw[:, m, 0:L], raw[:, m, 0:L], ACT.Exp, scale=-0.5).then_inc(rn, 1)
                    else:
                        act.activation(raw[:, m, 0:L], raw[:, m, 0:L], ACT.Exp, scale=-0.5, bias=eps[:, 3:4]).then_inc(rn, 1)
                return gate

            def decay_w(w):
                act.wait_ge(dd_d, w + 1)
                act.activation(dd[:, :, :], dd[:, :, :], ACT.Exp).then_inc(dd_e, 1)

            def tiles_w(w, s):
                meet(act, turned, w * 2, held)
                meet(act, qd_d, w, held)
                for j in each:
                    off = s * P if j % 2 == 0 else (WT - 1) * P - s * P
                    ins = act.activation(kqv[:, j, :, :], wide[:, j // 2, :, bass.ds(off, P)], ACT.Copy)
                ins.then_inc(kqv_in, 1)

            def rows_w(w):
                act.wait_ge(rows_in, w * 16 + 16)
                act.wait_ge(qd_d, w)
                act.activation(eq[:, :, :], rows[:, :, 0, :], ACT.Exp).then_inc(eq_d, 1)

            def scaled_w(w, tails, r, dst, kind, done):
                act.wait_ge(tc_in, w + 1)
                act.wait_ge(turned, w * 2 + 1)
                act.wait_ge(sps, tails)
                for j in each:
                    ins = act.activation(dst[:, r, j, :], bank[KB][:, j, :], ACT.Copy, scale=tc[:, r, j, kind:kind + 1])
                ins.then_inc(done, 1)

            def tail_w(v):
                act.wait_ge(pw, v + 1)
                act.wait_ge(vnp, v)
                act.activation(wtn[:, :, :], bank[G1][:, :, :], ACT.Copy, scale=-1.0).then_inc(wtn_d, 1)

            def tail_o(v, s):
                meet(act, op, v + 1, held)
                act.activation(ot[:, :, 0, bass.ds(s * P, P)], by_dir(bank[G0][:, :, :])[:, :, 0, :], ACT.Copy)
                act.activation(ot[:, :, 1, bass.ds((STEPS - 1) * P - s * P, P)], by_dir(bank[G0][:, :, :])[:, :, 1, :],
                               ACT.Copy).then_inc(o_cp, 1)

            def step(u, s, r, tail, prepare):
                for k in range(1, LEVELS):
                    for h in range(2):
                        act.wait_ge(xs, nth(u, k, h) + 1)
                        act.wait_ge(pr, nth(u, k, h) - 1 if k > 1 else u * PER)
                        act.activation(x_[:, 2 * h:2 * h + 2, :], bank[XB + h][:, 0:2, :], ACT.Copy).then_inc(x_cp, 1)
                    if tail:
                        if k == 1:
                            tail_w(u - 1)
                        if k == 3:
                            tail_o(u - 1, s - 1)
                    if prepare:
                        if k == 1:
                            decay_w(u + 1)
                        if k == 2:
                            tiles_w(u + 1, s + 1)
                        if k == 4:
                            rows_w(u + 1)
                        if k == 5:
                            scaled_w(u + 1, u, 1 - r, kbe, 2, kbe_d)
                        if k == 6:
                            scaled_w(u + 1, u, 1 - r, kde, 3, kde_d)

            with act.Fori(0, NPAIR) as p:
                u0 = p * STEPS
                head(p, p * 2, 0)()
                gate = head(p, p * 2 + 1, 1)
                act.wait_ge(back_in, p + 1)
                act.wait_ge(og_out, p * 16)
                tiles_w(u0, 0)
                decay_w(u0)
                rows_w(u0)
                gate()
                act.wait_ge(silu, p * 8 + 8)
                scaled_w(u0, u0, 0, kbe, 2, kbe_d)
                scaled_w(u0, u0, 0, kde, 3, kde_d)
                step(u0, 0, 0, False, True)
                with act.Fori(0, (STEPS - 3) // 2) as i:
                    step(u0 + 2 * i + 1, 2 * i + 1, 1, True, True)
                    step(u0 + 2 * i + 2, 2 * i + 2, 0, True, True)
                step(u0 + STEPS - 2, STEPS - 2, 1, True, True)
                step(u0 + STEPS - 1, STEPS - 1, 0, True, False)
                tail_w(u0 + STEPS - 1)
                tail_o(u0 + STEPS - 1, STEPS - 1)
                act.wait_ge(o_add, p + 1)
                act.activation(th[:, :, 0:SEQ], ot[:, :, 0, P:], ACT.Square).then_inc(o_sq, 1)
                act.wait_ge(o_ssq, p + 1)
                for h in range(2):
                    for k in range(2):
                        ins = act.activation(th[:, h, HALF * k:HALF * (k + 1)], flat((PB, KB)[h] + k), ACT.Ln, scale=1.0 / GD,
                                             bias=eps[:, 2:3])
                ins.then_inc(o_rn, 1)
                act.wait_ge(o_rn, p * 2 + 1)
                act.activation(th[:, :, 0:SEQ], th[:, :, 0:SEQ], ACT.Exp, scale=-0.5).then_inc(o_rn, 1)

        @block.vector
        def _(v):
            def head(p, hd, hh):
                for m in range(3):
                    taps = V("conv")[:, bass.ds(hd * 15 + 5 * m, 5)]
                    v.wait_ge(raw_in, hd * 4 + m + 1)
                    if m == 0:
                        v.wait_ge(wide_in, hd * 2)
                        v.wait_ge(rn, hd * 4)
                    v.tensor_scalar(acc[:, m, :], raw[:, m, 0:L], taps[:, 0:1], None, ALU.mult).then_inc(conv, 1)
                    for j in range(1, 5):
                        v.wait_ge(conv, hd * 15 + 5 * m + j)
                        v.scalar_tensor_tensor(acc[:, m, :], raw[:, m, j:j + L], taps[:, j:j + 1], acc[:, m, :],
                                               ALU.mult, ALU.add).then_inc(conv, 1)
                    v.wait_ge(tanhd, hd * 4 + m + 1)
                    if m == 2:
                        v.wait_ge(kqv_in, p * STEPS)
                        v.wait_ge(pads, 3)
                    dst = acc[:, m, :] if m < 2 else wide[:, bass.ds(hh, 1), 2, W_META:W_META + L].rearrange("p a t -> p (a t)")
                    v.scalar_tensor_tensor(dst, th[:, m % 2, :], 1.0, acc[:, m, :], ALU.add, ALU.mult).then_inc(silu, 1)
                for m in range(2):
                    v.wait_ge(rn, hd * 4 + 3 + m)
                    v.tensor_tensor(wide[:, bass.ds(hh, 1), m, W_META:W_META + L].rearrange("p a t -> p (a t)"), acc[:, m, :],
                                    raw[:, m, 0:L], ALU.mult).then_inc(wide_in, 1)

            def gate(hd, hh):
                v.wait_ge(tanhd, hd * 4 + 4)
                v.scalar_tensor_tensor(zb[:, hh, :], th[:, 1, 0:SEQ], 1.0, zb[:, hh, :], ALU.add, ALU.mult).then_inc(silu, 1)

            each = range(NI)
            tab_of = lambda u: tab[:, :, :, :, :, :].rearrange("p q s h d k -> p (q s) (h d) k")[:, bass.ds(u, 1), :, :]\
                .rearrange("p a i k -> p (a i) k")

            def decay_w(w, r):
                v.wait_ge(kde_d, w)
                v.wait_ge(vb_d, w)
                v.tensor_copy(tc[:, r, :, :], tab_of(w)[:, :, 0:4]).then_inc(tc_in, 1)
                v.wait_ge(rows_in, w * 16 + 16)
                v.wait_ge(tc_in, w + 1)
                v.wait_ge(at_d, w)
                for j in each:
                    ins = v.tensor_scalar(dd[:, j, :], rows[:, j, 0, :], tc[:, r, j, 0:1], 0.0, ALU.subtract, ALU.min)
                ins.then_inc(dd_d, 1)

            def gram_w(w, tails, r):
                v.wait_ge(gram, w + 1)
                v.wait_ge(dd_m, w + 1)
                v.wait_ge(ml_d, w * LEVELS)
                v.wait_ge(op, tails)
                for dst, half, done in ((mt, 0, mt_d), (at[:, r, :, :], 1, at_d)):
                    for b in range(2):
                        ins = v.tensor_tensor(dst[:, 2 * b:2 * b + 2, :],
                                              bank[G0 + b][:, :, :].rearrange("p (i k) t -> p i k t", k=2)[:, :, half, :],
                                              dd[:, 2 * b:2 * b + 2, :], ALU.mult)
                    ins.then_inc(done, 1)

            def scaled_w(w, tails, r):
                v.wait_ge(turned, w * 2 + 2)
                v.wait_ge(vnp, tails)
                for j in each:
                    ins = v.tensor_scalar(vb[:, r, j, :], bank[VB][:, j, :], tc[:, r, j, 1:2], None, ALU.mult)
                ins.then_inc(vb_d, 1)

            def first_level(w, r):
                v.wait_ge(x0, w + 1)
                v.tensor_tensor(ttt[:, r, :, 0, :, :], ident4.rearrange("p (h d) t -> p h d t", d=2),
                                by_dir(bank[G0][:, :, :]), ALU.subtract).then_inc(t0, 1)

            def tail_v(n):
                v.wait_ge(vnp, n + 1)
                v.wait_ge(op, n)
                v.tensor_copy(vn[:, :, :], bank[KB][:, :, :]).then_inc(vn_d, 1)

            def tail_s(n):
                v.wait_ge(s_up, n)
                v.tensor_copy(te[:, :, :], tab_of(n)[:, :, 4:5]).then_inc(te_in, 1)
                v.wait_ge(sps, n + 1)
                v.wait_ge(op, n + 1)
                v.wait_ge(te_in, n + 1)
                for j in each:
                    ins = v.scalar_tensor_tensor(st[:, j, :], st[:, j, :], te[:, j, :], bank[VB][:, j, :],
                                                 ALU.mult, ALU.add)
                ins.then_inc(s_up, 1)

            def step(u, r, tail, prepare):
                for k in range(1, LEVELS):
                    if tail and k == 2:
                        tail_v(u - 1)
                    if prepare and k == 6:
                        first_level(u + 1, 1 - r)
                    for h in range(2):
                        v.wait_ge(pr, nth(u, k, h) + 1)
                        if k == 1:
                            v.wait_ge(t0, u + 1)
                            v.wait_ge(tt0, u + 1)
                        else:
                            v.wait_ge(t_up, nth(u, k - 1, h) + 1)
                        a = 1 if k == LEVELS - 1 else 0
                        v.tensor_tensor(ttt[:, r, h, a:2, :, :], ttt[:, r, h, a:2, :, :],
                                        bank[PB + h][:, :, :].rearrange("p (a d) t -> p a d t", d=2)[:, a:2, :, :],
                                        ALU.subtract).then_inc(t_up, 1)
                    if tail and k == 3:
                        tail_s(u - 1)
                    if prepare:
                        if k == 1:
                            decay_w(u + 1, 1 - r)
                        if k == 4:
                            gram_w(u + 1, u, 1 - r)
                        if k == 5:
                            scaled_w(u + 1, u, 1 - r)

            for k in range(3):
                v.memset(raw[:, k, 0:2], 0.0)
            v.memset(raw[:, :, L + 2:L + 4], 0.0).then_inc(pads, 1)
            v.memset(wide[:, :, :, 0:W_META], 0.0).then_inc(pads, 1)
            v.memset(wide[:, :, :, (WT - 1) * P:WIDE], 0.0).then_inc(pads, 1)
            v.memset(zeros[:, :], 0.0).then_inc(pads, 1)
            with v.Fori(0, NPAIR) as p:
                head(p, p * 2, 0)
                gate(p * 2, 0)
                head(p, p * 2 + 1, 1)
                v.wait_ge(wide_in, p * 4 + 4)
                v.wait_ge(silu, p * 8 + 7)
                both = wide[:, :, :, :].rearrange("p h m t -> p (h m) t")
                v.tensor_copy(both[:, :, (WT - 1) * P:(WT - 1) * P + META], both[:, :, W_META:P][:, :, ::-1]).then_inc(back_in, 1)
                v.wait_ge(s_up, p * STEPS)
                v.memset(st[:, :, :], 0.0).then_inc(s_zero, 1)
                u0 = p * STEPS
                v.wait_ge(s_zero, p + 1)
                decay_w(u0, 0)
                gate(p * 2 + 1, 1)
                gram_w(u0, u0, 0)
                scaled_w(u0, u0, 0)
                first_level(u0, 0)
                step(u0, 0, False, True)
                with v.Fori(0, (STEPS - 3) // 2) as i:
                    step(u0 + 2 * i + 1, 1, True, True)
                    step(u0 + 2 * i + 2, 0, True, True)
                step(u0 + STEPS - 2, 1, True, True)
                step(u0 + STEPS - 1, 0, True, False)
                tail_v(u0 + STEPS - 1)
                tail_s(u0 + STEPS - 1)
                v.wait_ge(o_cp, (p + 1) * STEPS)
                o = ot[:, :, 0, P:]
                v.tensor_tensor(o, o, ot[:, :, 1, 0:SEQ], ALU.add).then_inc(o_add, 1)
                v.wait_ge(o_rn, p * 2 + 2)
                v.wait_ge(o_add, p + 1)
                v.scalar_tensor_tensor(o, o, V("norm_w"), th[:, :, 0:SEQ], ALU.mult, ALU.mult).then_inc(o_gated, 1)
                v.wait_ge(o_gated, p * 2 + 1)
                v.wait_ge(silu, p * 8 + 8)
                v.scalar_tensor_tensor(o, o, 0.5, zb[:, :, :], ALU.mult, ALU.mult).then_inc(o_gated, 1)

        @block.gpsimd
        def _(g):
            def prepare(w, tails, r, first):
                g.wait_ge(dd_e, w + 1)
                g.tensor_tensor(by_dir(dd[:, :, :]), by_dir(dd[:, :, :]), incl, ALU.mult).then_inc(dd_m, 1)
                g.wait_ge(mt_d, w + 1)
                g.wait_ge(rows_in, w * 16 + 16)
                g.tensor_tensor(mt[:, :, :], mt[:, :, :], rows[:, :, 1, :], ALU.mult).then_inc(mt_b, 1)
                g.wait_ge(mt_b, w + 1)
                for k in range(LEVELS):
                    if k == 0:
                        g.wait_ge(x0, w)
                    else:
                        g.wait_ge(xs, w * PER if first else (w - 1) * PER + 2 * k)
                    g.tensor_tensor(by_dir(ml[:, k, :, :]), by_dir(mt[:, :, :]), level(k), ALU.mult).then_inc(ml_d, 1)
                    if k == 0:
                        g.wait_ge(ml_d, w * LEVELS + 1)
                        g.wait_ge(vnp, tails)
                        g.tensor_tensor(ttt[:, r, :, 1, :, :], ident4.rearrange("p (h d) t -> p h d t", d=2),
                                        by_dir(ml[:, 0, :, :]), ALU.subtract).then_inc(tt0, 1)
                    if k == 2:
                        g.wait_ge(eq_d, w + 1)
                        g.wait_ge(kqv_in, w + 1)
                        g.wait_ge(op, tails)
                        g.tensor_tensor(qd[:, r, :, :], kqv[:, :, 1, :], eq[:, :, :], ALU.mult).then_inc(qd_d, 1)

            with g.Fori(0, NPAIR) as p:
                u0 = p * STEPS
                prepare(u0, u0, 0, True)
                with g.Fori(0, (STEPS - 1) // 2) as i:
                    prepare(u0 + 2 * i + 1, u0 + 2 * i, 1, False)
                    prepare(u0 + 2 * i + 2, u0 + 2 * i + 1, 0, False)


def merge(nc, io, keep):
    hT = keep["hT"]
    KN, KG = NA_W // P, GH
    PARTS = (("gate_na", 0, DC), ("gate_gdn", DC, DC), ("y_na", 2 * DC, KN), ("y_gdn", 2 * DC + KN, KG))
    NW = 2 * DC + KN + KG
    with ExitStack() as ctx:
        sb, ps, sem = makers(nc, ctx, "merge")
        og = sb("o_gdn", [P, GH, SEQ])
        ona = sb("o_na", [P, KN, SEQ])
        w = sb("w_merge", [P, 2, NW, P])
        th = sb("gate_tanh", [P, 2, 2, HALF])
        y = sb("gated_y", [P, 2, 2, HALF])
        mg = sb("merged", [P, 2, HALF])
        bank = [ps(f"bank{k}", [P, HALF]) for k in range(8)]
        ona_in, og_in, w_in = sem("o_na_in"), sem("o_gdn_in"), [sem(f"w_merge_in{k}") for k in range(2)]
        prod, th_d, y_d, mg_d = sem("product"), sem("tanh_done"), sem("gated"), sem("merged_done")
        out, met, met_w = [sem(f"merged_out{k}") for k in range(2)], sem("met"), sem("met_w")
        block = ctx.enter_context(nc.Block())

        @block.sync
        def _(sp):
            def weights(i, b):
                sp.dma_start(w[:, b, :, :], io["w_merge"][bass.ds(2 * i + b, 1), :, :, :]
                             .rearrange("a p j n -> p (a j) n")).then_inc(w_in[b], 16)

            weights(0, 0)
            sp.dma_start(ona[:, :, :], io["ona"].rearrange("q p t -> p q t")).then_inc(ona_in, 16)
            sp.dma_start(og[:, :, :], io["og"].rearrange("h p t -> p h t")).then_inc(og_in, 16)
            weights(0, 1)
            with sp.Fori(1, DC // 2) as i:
                for b in range(2):
                    meet(sp, prod, i * 16 - 8 + 8 * b, met_w)
                    weights(i, b)

        @block.tensor
        def _(pe):
            with pe.Fori(0, DC // 2) as i:
                for b in range(2):
                    pe.wait_ge(w_in[b], i * 16 + 16)
                    for k in range(2):
                        n = i * 4 + 2 * b + k
                        for q, (name, lo, num) in enumerate(PARTS):
                            if q == 0:
                                pe.wait_ge(th_d, i * 8 + max(2 * b + k - 1, 0) * 2)
                            if q == 2:
                                pe.wait_ge(ona_in, 16)
                                pe.wait_ge(y_d, i * 8 + max(2 * b + k - 1, 0) * 2)
                            if q == 3:
                                pe.wait_ge(og_in, 16)
                            tok = slice(HALF * k, HALF * (k + 1))
                            for c in range(num):
                                rhs = (hT[:, c, META + HALF * k:META + HALF * (k + 1)] if q < 2
                                       else ona[:, c, tok] if q == 2 else og[:, c, tok])
                                ins = pe.matmul(bank[4 * k + q][:, :], w[:, b, lo + c, :], rhs,
                                                start=(c == 0), stop=(c == num - 1))
                            ins.then_inc(prod, 1)

        @block.scalar
        def _(act):
            with act.Fori(0, DC // 2) as i:
                for b in range(2):
                    for k in range(2):
                        j = 2 * b + k
                        for q in range(2):
                            act.wait_ge(prod, i * 16 + 4 * j + q + 1)
                            act.wait_ge(y_d, i * 8 + max(j - 1, 0) * 2)
                            act.activation(th[:, k, q, :], bank[4 * k + q][:, :], ACT.Tanh, scale=0.5).then_inc(th_d, 1)

        @block.vector
        def _(v):
            with v.Fori(0, DC // 2) as i:
                for b in range(2):
                    for k in range(2):
                        j = 2 * b + k
                        for q in range(2):
                            v.wait_ge(prod, i * 16 + 4 * j + q + 3)
                            v.wait_ge(th_d, i * 8 + 2 * j + q + 1)
                            v.wait_ge(mg_d, i * 4 + max(j - 1, 0))
                            v.scalar_tensor_tensor(y[:, k, q, :], th[:, k, q, :], 1.0, bank[4 * k + 2 + q][:, :],
                                                   ALU.add, ALU.mult).then_inc(y_d, 1)

        @block.gpsimd
        def _(g):
            with g.Fori(0, DC // 2) as i:
                for b in range(2):
                    for k in range(2):
                        j = 2 * b + k
                        g.wait_ge(y_d, i * 8 + 2 * j + 2)
                        g.wait_ge(out[k], i * 32 + 16 * b)
                        g.tensor_tensor(mg[:, k, :], y[:, k, 0, :], y[:, k, 1, :], ALU.add).then_inc(mg_d, 1)
                        meet(g, mg_d, i * 4 + j + 1, met)
                        dst = io["merged"].rearrange("t p c n -> p t (c n)")[:, (TT // 2) * k:(TT // 2) * (k + 1),
                                                                             bass.ds((2 * i + b) * P, P)]
                        g.dma_start(dst, mg[:, k, :].rearrange("p (t n) -> p t n", n=P)).then_inc(out[k], 16)
            for k in range(2):
                g.wait_ge(out[k], 16 * DC)


def first_norm(nc, io, keep):
    con, lg = keep["con"], keep["logits"]
    ident = con[:, C_AT["ident"][0]:C_AT["ident"][1]]
    eps = con[:, C_AT["eps"][0]:C_AT["eps"][1]]
    NL = NG + NE
    with ExitStack() as ctx:
        sb, ps, sem = makers(nc, ctx, "norm1")
        wo = sb("w_out", [P, DC, D])
        vec = sb("norm_rows", [P, 4, D])
        wr = sb("w_router", [P, DC, NL])
        br = sb("b_router", [P, NL])
        mg = sb("merged", [P, 2, DC, P])
        h = sb("h_rows", [P, 2, D])
        hT1 = sb("h1_T", [P, 2, DC, P])
        stats = sb("stats", [P, 2, 12])
        mv = sb("mean_var", [P, 2, 4])
        bank = [ps(f"bank{k}", [P, HALF]) for k in range(8)]
        con_in, wo_in, scaled = sem("constants_in"), [sem(f"w_out_in{f}") for f in range(2)], sem("rows_scaled")
        mg_in, xn_in = [sem(f"merged_in{k}") for k in range(2)], [sem(f"xn_in{k}") for k in range(2)]
        mixed, skip, added, stat, rstd = sem("mixed"), sem("skip_made"), sem("added"), sem("stat"), sem("rstd")
        normed, h1_d, turned, hT_in = sem("normed"), sem("h1_made"), sem("h1_turned"), sem("h1_T_in")
        routed, lg_d = sem("logits_done"), sem("logits_in")
        h1_out, held, met = [sem(f"h1_out{k}") for k in range(2)], sem("held"), sem("met")
        block = ctx.enter_context(nc.Block())

        @block.sync
        def _(sp):
            def merged(i, k):
                sp.dma_start(mg[:, k, :, :], io["merged"][bass.ds(2 * i + k, 1), :, :, :]
                             .rearrange("a p c n -> p (a c) n")).then_inc(mg_in[k], 16)

            def pair(i, more):
                for k in range(2):
                    meet(sp, h1_out[k], i * 16, met)
                    meet(sp, turned, i * 2, met)
                    sp.dma_start(h[:, k, :], io["xn"][bass.ds((2 * i + k) * P, P), :]).then_inc(xn_in[k], 16)
                if more:
                    for k in range(2):
                        meet(sp, mixed, i * 2 + k + 1, met)
                        merged(i + 1, k)
                for k in range(2):
                    meet(sp, h1_d, i * 4 + 2 * k + 2, met)
                    sp.dma_start(io["h1"][bass.ds((2 * i + k) * P, P), :], h[:, k, :]).then_inc(h1_out[k], 16)

            merged(0, 0)
            for f in range(2):
                half = slice(HALF * f, HALF * (f + 1))
                sp.dma_start(wo[:, :, half], io["w_out"][:, :, half]).then_inc(wo_in[f], 16)
            merged(0, 1)
            for k, name in enumerate(("ln0_g", "ln0_b", "ln1_g", "ln1_b")):
                sp.dma_start(vec[:, k, :], io[name].to_broadcast([P, D])).then_inc(con_in, 16)
            sp.dma_start(wr[:, :, :], io["w_router"]).then_inc(con_in, 16)
            sp.dma_start(br[:, :], io["b_router"].to_broadcast([P, NL])).then_inc(con_in, 16)
            with sp.Fori(0, TT // 2 - 1) as i:
                pair(i, True)
            pair(TT // 2 - 1, False)
            for k in range(2):
                sp.wait_ge(h1_out[k], 16 * (TT // 2))

        @block.tensor
        def _(pe):
            def mix(i, k, read):
                pe.wait_ge(mg_in[k], i * 16 + 16)
                if read is not None:
                    pe.wait_ge(added, read)
                for f in range(2):
                    pe.wait_ge(wo_in[f], 16)
                    for c in range(DC):
                        ins = pe.matmul(bank[2 * k + f][:, :], mg[:, k, c, :], wo[:, c, HALF * f:HALF * (f + 1)],
                                        start=(c == 0), stop=(c == DC - 1))
                ins.then_inc(mixed, 1)

            def pair(i, more):
                for k in range(2):
                    if more:
                        mix(i + 1, k, i * 2 + k + 1)
                    pe.wait_ge(h1_d, i * 4 + 2 * k + 2)
                    pe.wait_ge(hT_in, i * 2 + k)
                    for c in range(DC):
                        ins = pe.transpose(bank[4 + c // 4][:, P * (c % 4):P * (c % 4) + P], h[:, k, P * c:P * c + P], ident)
                    ins.then_inc(turned, 1)
                for k in range(2):
                    pe.wait_ge(hT_in, i * 2 + k + 1)
                    pe.wait_ge(lg_d, i * 2 + k)
                    for c in range(DC):
                        ins = pe.matmul(bank[6][:, 0:NL], hT1[:, k, c, :], wr[:, c, :], start=(c == 0), stop=(c == DC - 1))
                    ins.then_inc(routed, 1)

            mix(0, 0, None)
            mix(0, 1, None)
            pe.wait_ge(con_in, 16 * 6)
            with pe.Fori(0, TT // 2 - 1) as i:
                pair(i, True)
            pair(TT // 2 - 1, False)

        @block.gpsimd
        def _(g):
            g.wait_ge(con_in, 16 * 6)
            for k in range(2):
                g.tensor_scalar(vec[:, k, :], vec[:, k, :], ALPHA, None, ALU.mult).then_inc(scaled, 1)
            g.wait_ge(scaled, 2)
            with g.Fori(0, TT // 2) as i:
                for k in range(2):
                    g.wait_ge(xn_in[k], i * 16 + 16)
                    g.tensor_tensor(h[:, k, :], h[:, k, :], vec[:, 0, :], ALU.mult).then_inc(skip, 1)
                    g.wait_ge(skip, i * 4 + 2 * k + 1)
                    g.tensor_tensor(h[:, k, :], h[:, k, :], vec[:, 1, :], ALU.add).then_inc(skip, 1)
                for k in range(2):
                    g.wait_ge(normed, i * 2 + k + 1)
                    g.tensor_tensor(h[:, k, :], h[:, k, :], vec[:, 2, :], ALU.mult).then_inc(h1_d, 1)
                    g.wait_ge(h1_d, i * 4 + 2 * k + 1)
                    g.tensor_tensor(h[:, k, :], h[:, k, :], vec[:, 3, :], ALU.add).then_inc(h1_d, 1)

        @block.vector
        def _(v):
            v.wait_ge(con_in, 16 * 6)
            with v.Fori(0, TT // 2) as i:
                for k in range(2):
                    t = i * 2 + k
                    v.wait_ge(mixed, t + 1)
                    v.wait_ge(skip, i * 4 + 2 * k + 2)
                    for f in range(2):
                        part = h[:, k, HALF * f:HALF * (f + 1)]
                        ins = v.scalar_tensor_tensor(part, bank[2 * k + f][:, :], 0.5, part, ALU.mult, ALU.add)
                    ins.then_inc(added, 1)
                    v.wait_ge(added, t + 1)
                    for f in range(2):
                        ins = v.bn_stats(stats[:, k, 6 * f:6 * f + 6], h[:, k, HALF * f:HALF * (f + 1)])
                    ins.then_inc(stat, 1)
                    meet(v, stat, t * 2 + 1, held)
                    v.bn_aggr(mv[:, k, 0:2], stats[:, k, :]).then_inc(stat, 1)
                    v.wait_ge(rstd, t * 2 + 2)
                    v.tensor_scalar(h[:, k, :], h[:, k, :], mv[:, k, 0:1], mv[:, k, 3:4], ALU.subtract, ALU.mult).then_inc(normed, 1)
                for k in range(2):
                    t = i * 2 + k
                    v.wait_ge(routed, t + 1)
                    v.tensor_tensor(lg[:, bass.ds(t, 1), :].rearrange("p a n -> p (a n)"), bank[6][:, 0:NL], br[:, :],
                                    ALU.add).then_inc(lg_d, 1)

        @block.scalar
        def _(act):
            with act.Fori(0, TT // 2) as i:
                for k in range(2):
                    t = i * 2 + k
                    act.wait_ge(stat, t * 2 + 2)
                    act.activation(mv[:, k, 2:3], mv[:, k, 1:2], ACT.Ln, bias=eps[:, 0:1]).then_inc(rstd, 1)
                    act.wait_ge(rstd, t * 2 + 1)
                    act.activation(mv[:, k, 3:4], mv[:, k, 2:3], ACT.Exp, scale=-0.5).then_inc(rstd, 1)
                for k in range(2):
                    t = i * 2 + k
                    act.wait_ge(turned, t + 1)
                    act.wait_ge(routed, i * 2)
                    for f in range(2):
                        ins = act.activation(hT1[:, k, 4 * f:4 * f + 4, :].rearrange("p c n -> p (c n)"), bank[4 + f][:, :], ACT.Copy)
                    ins.then_inc(hT_in, 1)


def route(nc, io, keep):
    con, lg, slot, wt, owner = keep["con"], keep["logits"], keep["slot"], keep["weight"], keep["owner"]
    C = lambda n: con[:, C_AT[n][0]:C_AT[n][1]]
    with ExitStack() as ctx:
        sb, ps, sem = makers(nc, ctx, "route")
        top = sb("top", [P, 4, TT])
        eq = sb("group_rank", [P, TT, NG])
        goh = sb("group_onehot", [P, TT, NG])
        gex = sb("group_exp", [P, TT, NG])
        gw = sb("group_weight", [P, TT])
        tmp = sb("picked", [P, TT, NG, EPG])
        sel = sb("expert_logits", [P, TT, EPG])
        rank = sb("expert_rank", [P, TT, EPG])
        oh = sb("expert_onehot", [P, 2, TT, EPG])
        hot = sb("onehot", [P, 3, TT, NE])
        dif = sb("logit_difference", [P, 2, TT])
        base = sb("tile_base", [P, TT + 1, NE])
        k128 = sb("block_edges", [P, TT])
        over = sb("over_edge", [P, NE, TT])
        nb = sb("expert_blocks", [P, NE])
        bend = sb("block_end", [P, NE])
        one = sb("one", [P, NE])
        dest = sb("dest", [P, TT, NE])
        own = sb("own", [1, NBLK, NE])
        ownf = sb("own_sum", [1, NBLK])
        sl = sb("slot_f", [P, 2, TT])
        ids = sb("token_ids", [P, TT], U32)
        zero = sb("zero", [P, NBLK], U32)
        pre = ps("prefix", [P, TT, NE])
        tot = ps("totals", [P, TT, NE])
        step, ex, pfx = sem("route_step"), sem("exp_done"), sem("prefix_done")
        cleared, table = sem("table_cleared"), sem("table_out")
        block = ctx.enter_context(nc.Block())
        MARK = 99.0
        count = {}

        @block.vector
        def _(v):
            n = [0]

            def link(ins, name=None):
                n[0] += 1
                ins.then_inc(step, 1)
                v.wait_ge(step, n[0])
                if name:
                    count[name] = n[0]

            last = lambda a, k: a.unsqueeze(a.ndim).to_broadcast(list(a.shape) + [k])
            G = lg[:, :, 0:NG]
            E = lg[:, :, NG:NG + NE].rearrange("p t (g e) -> p t g e", e=EPG)
            gidx = C("gidx").unsqueeze(1).to_broadcast([P, TT, NG])
            eidx = C("eidx")[:, 0:EPG].unsqueeze(1).to_broadcast([P, TT, EPG])
            link(v.memset(zero[:, :], 0))
            link(v.tensor_copy(ids[:, :], C("tok")), "ids")
            link(v.memset(one[:, :], 1.0))
            link(v.memset(base[:, 0, :], 0.0))
            link(v.tensor_reduce(top[:, 0, :], G, AX.X, ALU.max))
            link(v.tensor_tensor(eq[:, :, :], G, last(top[:, 0, :], NG), ALU.is_equal))
            link(v.scalar_tensor_tensor(eq[:, :, :], eq[:, :, :], -MARK, gidx, ALU.mult, ALU.add))
            link(v.tensor_reduce(top[:, 1, :], eq[:, :, :], AX.X, ALU.min))
            link(v.tensor_tensor(goh[:, :, :], eq[:, :, :], last(top[:, 1, :], NG), ALU.is_equal))
            link(v.tensor_tensor(gex[:, :, :], G, last(top[:, 0, :], NG), ALU.subtract), "group_shifted")
            link(v.tensor_tensor(tmp[:, :, :, :], E, last(goh[:, :, :], EPG), ALU.mult))
            link(v.tensor_reduce(sel[:, :, :], tmp[:, :, :, :].rearrange("p t g e -> p t e g"), AX.X, ALU.add))
            for k in range(2):
                link(v.tensor_reduce(top[:, 2 + k, :], sel[:, :, :], AX.X, ALU.max))
                link(v.tensor_tensor(rank[:, :, :], sel[:, :, :], last(top[:, 2 + k, :], EPG), ALU.is_equal))
                link(v.scalar_tensor_tensor(rank[:, :, :], rank[:, :, :], -MARK, eidx, ALU.mult, ALU.add))
                link(v.tensor_reduce(dif[:, 0, :], rank[:, :, :], AX.X, ALU.min))
                link(v.tensor_tensor(oh[:, k, :, :], rank[:, :, :], last(dif[:, 0, :], EPG), ALU.is_equal))
                if k == 0:
                    link(v.scalar_tensor_tensor(sel[:, :, :], oh[:, 0, :, :], -BIG, sel[:, :, :], ALU.mult, ALU.add))
            link(v.tensor_tensor(dif[:, 1, :], top[:, 3, :], top[:, 2, :], ALU.subtract), "pair_shifted")
            for k in range(2):
                link(v.tensor_tensor(hot[:, k, :, :].rearrange("p t (g e) -> p t g e", e=EPG), last(goh[:, :, :], EPG),
                                     oh[:, k, :, :].unsqueeze(2).to_broadcast([P, TT, NG, EPG]), ALU.mult))
            link(v.tensor_tensor(hot[:, 2, :, :], hot[:, 0, :, :], hot[:, 1, :, :], ALU.add), "hot")
            v.wait_ge(ex, 2)
            link(v.tensor_reduce(gw[:, :], gex[:, :, :], AX.X, ALU.add))
            link(v.tensor_scalar(top[:, 0, :], dif[:, 1, :], 1.0, None, ALU.add))
            link(v.tensor_tensor(gw[:, :], gw[:, :], top[:, 0, :], ALU.mult))
            link(v.reciprocal(wt[:, 0, :], gw[:, :]))
            link(v.tensor_tensor(wt[:, 1, :], wt[:, 0, :], dif[:, 1, :], ALU.mult))
            v.wait_ge(pfx, 2)
            for t in range(TT):
                link(v.tensor_tensor(base[:, t + 1, :], base[:, t, :], tot[:, t, :], ALU.add))
            link(v.tensor_scalar(k128[:, :], C("blk")[:, 0:TT], float(P), None, ALU.mult))
            link(v.tensor_tensor(over[:, :, :], last(base[:, TT, :], TT), k128[:, :].unsqueeze(1).to_broadcast([P, NE, TT]),
                                 ALU.is_gt))
            link(v.tensor_reduce(nb[:, :], over[:, :, :], AX.X, ALU.add))
            link(v.tensor_tensor_scan(bend[:, :], one[:, :], nb[:, :], 0.0, ALU.mult, ALU.add))
            link(v.tensor_tensor(nb[:, :], bend[:, :], nb[:, :], ALU.subtract))
            link(v.tensor_tensor(dest[:, :, :], pre[:, :, :], base[:, 0:TT, :], ALU.add))
            link(v.scalar_tensor_tensor(dest[:, :, :], nb[:, :].unsqueeze(1).to_broadcast([P, TT, NE]), float(P), dest[:, :, :],
                                        ALU.mult, ALU.add))
            for k in range(2):
                link(v.tensor_tensor(hot[:, k, :, :], hot[:, k, :, :], dest[:, :, :], ALU.mult))
                link(v.tensor_reduce(sl[:, k, :], hot[:, k, :, :], AX.X, ALU.add))
            link(v.tensor_copy(slot[:, :, :], sl[:, :, :]), "slot")
            link(v.tensor_tensor(own[:, :, :], bend[0:1, :].unsqueeze(1).to_broadcast([1, NBLK, NE]),
                                 last(C("blk")[0:1, :], NE), ALU.is_le))
            link(v.tensor_reduce(ownf[:, :], own[:, :, :], AX.X, ALU.add))
            link(v.tensor_scalar(owner[:, 0:NBLK], ownf[:, :], float(NE - 1), None, ALU.min))
            link(v.tensor_tensor(own[:, 0:NBLK // 2, 0], C("blk")[0:1, ::2], bend[0:1, NE - 1:NE].to_broadcast([1, NBLK // 2]),
                                 ALU.is_lt))
            link(v.tensor_reduce(ownf[:, 0:1], own[:, 0:NBLK // 2, 0], AX.X, ALU.add))
            link(v.tensor_copy(owner[:, NBLK:NBLK + 1], ownf[:, 0:1]))

        @block.scalar
        def _(act):
            act.wait_ge(step, count["group_shifted"])
            act.activation(gex[:, :, :], gex[:, :, :], ACT.Exp).then_inc(ex, 1)
            act.wait_ge(step, count["pair_shifted"])
            act.activation(dif[:, 1, :], dif[:, 1, :], ACT.Exp).then_inc(ex, 1)

        @block.tensor
        def _(pe):
            pe.wait_ge(step, count["hot"])
            for dst, tri in ((pre, "before"), (tot, "ones")):
                pe.matmul(dst[:, :, :], C(tri), hot[:, 2, :, :], start=True, stop=True).then_inc(pfx, 1)

        @block.gpsimd
        def _(g):
            g.wait_ge(step, count["ids"])
            g.dma_start(io["token_of"].rearrange("(p b) a -> p (b a)", p=P), zero[:, :]).then_inc(cleared, 16)
            g.wait_ge(cleared, 16)
            g.wait_ge(step, count["slot"])
            for k in range(2):
                for t in range(TT):
                    g.indirect_dma_start(out=io["token_of"], out_offset=bass.IndirectOffsetOnAxis(ap=slot[:, k, t:t + 1], axis=0),
                                         in_=ids[:, t:t + 1], in_offset=None).then_inc(table, 16)
            g.wait_ge(table, 16 * 2 * TT)


def experts(nc, io, keep):
    con, owner = keep["con"], keep["owner"]
    ident = con[:, C_AT["ident"][0]:C_AT["ident"][1]]
    FC = FE // P
    with ExitStack() as ctx:
        sb, ps, sem = makers(nc, ctx, "moe")
        wgu = sb("w_gate_up", [P, 2, DC, 2 * FE])
        wdn = sb("w_down", [P, 2, FC, D])
        idx = sb("token_index", [P, 2], U32)
        x = sb("x_rows", [P, 2, D])
        xT = sb("x_T", [P, 2, DC, P])
        th = sb("gate_tanh", [P, 2, FE])
        hid = sb("hidden", [P, 2, FE])
        hidT = sb("hidden_T", [P, 2, FC, P])
        y = sb("y_rows", [P, 2, D])
        bank = [ps(f"bank{k}", [P, HALF]) for k in range(8)]
        two = lambda n: [sem(f"{n}{k}") for k in range(2)]
        gu_in, dn_in, idx_in, x_in, y_out = two("gate_up_in"), two("down_in"), two("index_in"), two("x_in"), two("y_out")
        turned, gu, down = two("x_turned"), two("gate_up"), two("down_done")
        xT_a, xT_v, th_d = sem("x_T_low"), sem("x_T_high"), sem("tanh_done")
        hid_d, hid_t, hidT_in = sem("hidden_step"), sem("hidden_turned"), sem("hidden_T_in")
        y_a, y_v, met, met_g, met_a = sem("y_low"), sem("y_high"), sem("met"), sem("met_g"), sem("met_a")
        block = ctx.enter_context(nc.Block())

        @block.sync
        def _(sp):
            def pair(i):
                e = [sp.value_load(owner[0:1, bass.ds(2 * i + k, 1)], min_val=0, max_val=NE - 1) for k in range(2)]
                for wt, name, used, done in ((wgu, "w_gate_up", gu, gu_in), (wdn, "w_down", down, dn_in)):
                    for k in range(2):
                        meet(sp, used[k], i, met)
                        sp.dma_start(wt[:, k, :, :], io[name][bass.ds(e[k], 1), :, :, :]
                                     .rearrange("a p c n -> p (a c) n")).then_inc(done[k], 16)

            with sp.Fori(0, FULL // 2) as i:
                pair(i)
            pairs = sp.value_load(owner[0:1, NBLK:NBLK + 1], min_val=FULL // 2, max_val=NBLK // 2)
            with sp.Fori(FULL // 2, NBLK // 2) as i:
                with sp.If(i < pairs):
                    pair(i)

        @block.gpsimd
        def _(g):
            def pair(i):
                for k in range(2):
                    meet(g, x_in[k], i * 16, met_g)
                    g.dma_start(idx[:, k:k + 1], io["token_of"][bass.ds((2 * i + k) * P, P), :]).then_inc(idx_in[k], 16)
                for k in range(2):
                    meet(g, idx_in[k], i * 16 + 16, met_g)
                    meet(g, turned[k], i, met_g)
                    g.indirect_dma_start(out=x[:, k, :], out_offset=None, in_=io["h1"],
                                         in_offset=bass.IndirectOffsetOnAxis(ap=idx[:, k:k + 1], axis=0)).then_inc(x_in[k], 16)

            with g.Fori(0, FULL // 2) as i:
                pair(i)
            pairs = g.value_load(owner[0:1, NBLK:NBLK + 1], min_val=FULL // 2, max_val=NBLK // 2)
            with g.Fori(FULL // 2, NBLK // 2) as i:
                with g.If(i < pairs):
                    pair(i)

        @block.tensor
        def _(pe):
            def turn_x(i, k):
                b = i * 2 + k
                pe.wait_ge(x_in[k], i * 16 + 16)
                pe.wait_ge(xT_a, b)
                pe.wait_ge(xT_v, b)
                for c in range(DC):
                    ins = pe.transpose(bank[c // 4][:, P * (c % 4):P * (c % 4) + P], x[:, k, P * c:P * c + P], ident)
                ins.then_inc(turned[k], 1)

            def gate_up(i, k):
                b = i * 2 + k
                pe.wait_ge(gu_in[k], i * 16 + 16)
                pe.wait_ge(hid_d, i * 4)
                for c in range(DC):
                    if c == 0:
                        pe.wait_ge(xT_a, b + 1)
                    if c == 4:
                        pe.wait_ge(xT_v, b + 1)
                    ins = pe.matmul(bank[2 + k][:, :], xT[:, k, c, :], wgu[:, k, c, :], start=(c == 0), stop=(c == DC - 1))
                ins.then_inc(gu[k], 1)

            def turn_hidden(i, k):
                b = i * 2 + k
                pe.wait_ge(hid_d, i * 4 + 2 * k + 2)
                pe.wait_ge(hidT_in, b)
                for f in range(FC):
                    ins = pe.transpose(bank[4][:, P * f:P * f + P], hid[:, k, P * f:P * f + P], ident)
                ins.then_inc(hid_t, 1)

            def project_down(i, k):
                b = i * 2 + k
                pe.wait_ge(dn_in[k], i * 16 + 16)
                pe.wait_ge(hidT_in, b + 1)
                pe.wait_ge(y_a, b)
                pe.wait_ge(y_v, b)
                for half in range(2):
                    for f in range(FC):
                        ins = pe.matmul(bank[5 + half][:, :], hidT[:, k, f, :], wdn[:, k, f, HALF * half:HALF * (half + 1)],
                                        start=(f == 0), stop=(f == FC - 1))
                ins.then_inc(down[k], 1)

            def pair(i):
                turn_x(i, 0)
                gate_up(i, 0)
                turn_x(i, 1)
                turn_hidden(i, 0)
                gate_up(i, 1)
                project_down(i, 0)
                turn_hidden(i, 1)
                project_down(i, 1)

            with pe.Fori(0, FULL // 2) as i:
                pair(i)
            pairs = pe.value_load(owner[0:1, NBLK:NBLK + 1], min_val=FULL // 2, max_val=NBLK // 2)
            with pe.Fori(FULL // 2, NBLK // 2) as i:
                with pe.If(i < pairs):
                    pair(i)

        @block.scalar
        def _(act):
            def copy_x(i, k):
                act.wait_ge(turned[k], i + 1)
                act.wait_ge(gu[k], i)
                act.activation(xT[:, k, 0:4, :].rearrange("p c n -> p (c n)"), bank[0][:, :], ACT.Copy).then_inc(xT_a, 1)

            def tanh(i, k):
                act.wait_ge(gu[k], i + 1)
                act.wait_ge(hid_d, i * 4)
                act.activation(th[:, k, :], bank[2 + k][:, 0:FE], ACT.Tanh, scale=0.5).then_inc(th_d, 1)

            def copy_hidden(i, k):
                act.wait_ge(hid_t, i * 2 + k + 1)
                act.wait_ge(down[k], i)
                act.activation(hidT[:, k, :, :].rearrange("p f n -> p (f n)"), bank[4][:, 0:FE], ACT.Copy).then_inc(hidT_in, 1)

            def copy_y(i, k):
                act.wait_ge(down[k], i + 1)
                act.wait_ge(y_out[k], i * 16)
                act.activation(y[:, k, 0:HALF], bank[5][:, :], ACT.Copy).then_inc(y_a, 1)

            def store_y(i, k):
                b = i * 2 + k
                act.wait_ge(y_a, b + 1)
                act.wait_ge(y_v, b + 1)
                act.dma_start(io["y"][bass.ds(b * P, P), :], y[:, k, :]).then_inc(y_out[k], 16)

            def pair(i):
                copy_x(i, 0)
                tanh(i, 0)
                copy_x(i, 1)
                copy_hidden(i, 0)
                tanh(i, 1)
                copy_y(i, 0)
                copy_hidden(i, 1)
                store_y(i, 0)
                copy_y(i, 1)
                store_y(i, 1)

            with act.Fori(0, FULL // 2) as i:
                pair(i)
            pairs = act.value_load(owner[0:1, NBLK:NBLK + 1], min_val=FULL // 2, max_val=NBLK // 2)
            with act.Fori(FULL // 2, NBLK // 2) as i:
                with act.If(i < pairs):
                    pair(i)
            for k in range(2):
                meet(act, y_out[k], 16 * pairs, met_a)

        @block.vector
        def _(v):
            def pair(i):
                for k in range(2):
                    b = i * 2 + k
                    v.wait_ge(turned[k], i + 1)
                    v.wait_ge(gu[k], i)
                    v.tensor_copy(xT[:, k, 4:8, :].rearrange("p c n -> p (c n)"), bank[1][:, :]).then_inc(xT_v, 1)
                    v.wait_ge(th_d, b + 1)
                    v.wait_ge(hid_t, i * 2)
                    v.scalar_tensor_tensor(hid[:, k, :], th[:, k, :], 1.0, bank[2 + k][:, 0:FE], ALU.add, ALU.mult).then_inc(hid_d, 1)
                    v.wait_ge(hid_d, i * 4 + 2 * k + 1)
                    v.scalar_tensor_tensor(hid[:, k, :], hid[:, k, :], 0.5, bank[2 + k][:, FE:2 * FE], ALU.mult, ALU.mult).then_inc(hid_d, 1)
                for k in range(2):
                    b = i * 2 + k
                    v.wait_ge(down[k], i + 1)
                    v.wait_ge(y_out[k], i * 16)
                    v.tensor_copy(y[:, k, HALF:D], bank[6][:, :]).then_inc(y_v, 1)

            with v.Fori(0, FULL // 2) as i:
                pair(i)
            pairs = v.value_load(owner[0:1, NBLK:NBLK + 1], min_val=FULL // 2, max_val=NBLK // 2)
            with v.Fori(FULL // 2, NBLK // 2) as i:
                with v.If(i < pairs):
                    pair(i)


def last_norm(nc, io, keep):
    con, slot, wt = keep["con"], keep["slot"], keep["weight"]
    eps = con[:, C_AT["eps"][0]:C_AT["eps"][1]]
    B = 4
    with ExitStack() as ctx:
        sb, ps, sem = makers(nc, ctx, "norm2")
        vec = sb("norm_rows", [P, 2, D])
        pick = sb("slot_index", [P, B, 2], U32)
        pw = sb("slot_weight", [P, B, 2])
        y = sb("y_rows", [P, B, 2, D])
        h = sb("h_rows", [P, B, D])
        z = sb("out_rows", [P, B, D])
        stats = sb("stats", [P, B, 12])
        mv = sb("mean_var", [P, B, 4])
        each = range(B)
        many = lambda n: [sem(f"{n}{k}") for k in each]
        vec_in, h_in, y_in, out = sem("rows_in"), many("h_in"), many("y_in"), many("out_stored")
        picked, scaled, summed, stat, rstd = sem("picked"), sem("first_scaled"), sem("summed"), sem("stat"), sem("rstd")
        normed, fin = sem("normed"), sem("final")
        held, held_a, met, met_g = sem("held"), sem("held_a"), sem("met"), sem("met_g")
        block = ctx.enter_context(nc.Block())

        @block.sync
        def _(sp):
            def load(i, k):
                sp.dma_start(h[:, k, :], io["h1"][bass.ds((B * i + k) * P, P), :]).then_inc(h_in[k], 16)

            def store(i):
                for k in each:
                    meet(sp, fin, (B * i + k) * 2 + 2, met)
                    sp.dma_start(io["out"][bass.ds((B * i + k) * P, P), :], z[:, k, :]).then_inc(out[k], 16)

            for k in each:
                load(0, k)
            with sp.Fori(0, TT // B - 1) as i:
                for k in each:
                    meet(sp, summed, (B * i + k) * 2 + 2, met)
                    load(i + 1, k)
                store(i)
            store(TT // B - 1)
            for k in each:
                sp.wait_ge(out[k], 16 * (TT // B))

        @block.gpsimd
        def _(g):
            def gather(i, k, used=None):
                meet(g, picked, (B * i + k) * 2 + 2, met_g)
                if used is not None:
                    meet(g, summed, used, met_g)
                for e in range(2):
                    g.indirect_dma_start(out=y[:, k, e, :], out_offset=None, in_=io["y"],
                                         in_offset=bass.IndirectOffsetOnAxis(ap=pick[:, k, e:e + 1], axis=0)).then_inc(y_in[k], 16)

            for k in each:
                gather(0, k)
            for k, name in enumerate(("ln2_g", "ln2_b")):
                g.dma_start(vec[:, k, :], io[name].to_broadcast([P, D])).then_inc(vec_in, 16)

            def finish(i):
                for k in each:
                    t = B * i + k
                    g.wait_ge(normed, t + 1)
                    g.wait_ge(vec_in, 32)
                    g.tensor_tensor(z[:, k, :], z[:, k, :], vec[:, 0, :], ALU.mult).then_inc(fin, 1)
                    g.wait_ge(fin, t * 2 + 1)
                    g.tensor_tensor(z[:, k, :], z[:, k, :], vec[:, 1, :], ALU.add).then_inc(fin, 1)

            with g.Fori(0, TT // B - 1) as i:
                for k in each:
                    gather(i + 1, k, (B * i + k) * 2 + 2)
                finish(i)
            finish(TT // B - 1)

        @block.vector
        def _(v):
            def select(i, k):
                v.tensor_copy(pick[:, k, :], slot[:, :, bass.ds(B * i + k, 1)].rearrange("p e a -> p (e a)")).then_inc(picked, 1)
                v.tensor_copy(pw[:, k, :], wt[:, :, bass.ds(B * i + k, 1)].rearrange("p e a -> p (e a)")).then_inc(picked, 1)

            def tiles(i, more):
                for k in each:
                    t = B * i + k
                    v.wait_ge(scaled, t + 1)
                    v.wait_ge(picked, t * 2 + 2)
                    v.scalar_tensor_tensor(y[:, k, 0, :], y[:, k, 1, :], pw[:, k, 1:2], y[:, k, 0, :], ALU.mult, ALU.add).then_inc(summed, 1)
                    v.wait_ge(summed, t * 2 + 1)
                    if more:
                        select(i + 1, k)
                    v.wait_ge(h_in[k], i * 16 + 16)
                    v.wait_ge(out[k], i * 16)
                    v.scalar_tensor_tensor(z[:, k, :], h[:, k, :], ALPHA, y[:, k, 0, :], ALU.mult, ALU.add).then_inc(summed, 1)
                    v.wait_ge(summed, t * 2 + 2)
                    for f in range(2):
                        ins = v.bn_stats(stats[:, k, 6 * f:6 * f + 6], z[:, k, HALF * f:HALF * (f + 1)])
                    ins.then_inc(stat, 1)
                    meet(v, stat, t * 2 + 1, held)
                    v.bn_aggr(mv[:, k, 0:2], stats[:, k, :]).then_inc(stat, 1)
                    if k % 2 == 1:
                        for n in (k - 1, k):
                            v.wait_ge(rstd, (B * i + k - 1) * 2 + 4)
                            v.tensor_scalar(z[:, n, :], z[:, n, :], mv[:, n, 0:1], mv[:, n, 3:4], ALU.subtract, ALU.mult).then_inc(normed, 1)

            for k in each:
                select(0, k)
            with v.Fori(0, TT // B - 1) as i:
                tiles(i, True)
            tiles(TT // B - 1, False)

        @block.scalar
        def _(act):
            with act.Fori(0, TT // B) as i:
                for k in range(0, B, 2):
                    for n in (k, k + 1):
                        meet(act, y_in[n], i * 32 + 32, held_a)
                        act.wait_ge(picked, (B * i + n) * 2 + 2)
                        act.activation(y[:, n, 0, :], y[:, n, 0, :], ACT.Copy, scale=pw[:, n, 0:1]).then_inc(scaled, 1)
                    t = B * i + k
                    act.wait_ge(stat, t * 2 + 4)
                    act.activation(mv[:, k:k + 2, 2:3], mv[:, k:k + 2, 1:2], ACT.Ln, bias=eps[:, 0:1]).then_inc(rstd, 2)
                    act.wait_ge(rstd, t * 2 + 2)
                    act.activation(mv[:, k:k + 2, 3:4], mv[:, k:k + 2, 2:3], ACT.Exp, scale=-0.5).then_inc(rstd, 2)


def kernel(**inputs):
    from concourse import bacc
    from concourse.bass_utils import run_bass_kernel_spmd

    f = {k: np.asarray(v) for k, v in inputs.items()}
    for name in f:
        if f[name].shape[0] == 1 and name not in ("x", "meta_tokens"):
            f[name] = f[name][0]
    w = f["w_in"]
    rowsof = lambda a: a.reshape(-1, P, a.shape[-1]).transpose(1, 0, 2)
    at = 3 * NA_W + 4 * D
    wg = np.zeros((P, DC, P), w.dtype)
    for k in range(4):
        wg[:, :, 32 * k:32 * k + GH] = rowsof(w[:, at + GH * k:at + GH * k + GH])
    cols = np.zeros((P, V_W), w.dtype)

    def put(name, a, lo=0):
        cols[lo:lo + a.shape[0], V_AT[name][0]:V_AT[name][1]] = a

    put("ln0_g", f["ln0_g"].reshape(DC, P).T)
    put("ln0_b", f["ln0_b"].reshape(DC, P).T)
    for d in range(2):
        put("dt", f["gdn_dt_bias"][d][:, None], 32 * d)
        put("alog", f["gdn_a_log"][d][:, None], 32 * d)
    put("conv", f["gdn_conv_w"].reshape(5, 3, GH, P)[:, [1, 0, 2]].transpose(3, 2, 1, 0).reshape(P, -1))
    put("norm_w", f["gdn_norm_w"][:, None])
    at = 3 * NA_W
    w_gdn = np.stack([w[:, at + D * m:at + D * m + D].reshape(DC, P, GH, P) for m in (1, 0, 2, 3)], 3)
    w_gdn = w_gdn.transpose(2, 1, 3, 0, 4)
    w_na3 = np.stack([w[:, NA_W * m:NA_W * (m + 1)].reshape(DC, P, NPAIR, P) for m in range(3)], 3).transpose(2, 1, 0, 3, 4)
    col = np.arange(GRID_W)
    distance = np.clip(col[None, :] - col[:, None] + KC - 1, 0, 2 * KC - 2)
    bias = f["na_rpb"][:, :, distance].transpose(0, 2, 1, 3).reshape(NPAIR, P, DRS, GRID_W)
    at = 3 * NA_W + 4 * D + 4 * GH
    by_out = lambda a: a.reshape(a.shape[0] // P, P, DC, P).transpose(2, 1, 0, 3)
    w_merge = np.concatenate([by_out(w[:, at:at + D]), by_out(w[:, at + D:at + 2 * D]), by_out(f["w_branch_na"]),
                              by_out(f["w_branch_gdn"])], 2)
    w_router = np.concatenate([f["router_group_w"], f["router_expert_w"]], 1)
    b_router = np.concatenate([f["router_group_b"], f["router_expert_b"]])[None, :]
    w_gate_up = np.concatenate([f["expert_w_gate"], f["expert_w_up"]], 2).reshape(NE, DC, P, 2 * FE).transpose(0, 2, 1, 3)
    arrays = {
        "const": constants(), "scan": scan_masks(), "cols": cols, "w_gates": wg,
        "x": f["x"][0], "meta": f["meta_tokens"], "w_gdn": w_gdn, "w_na3": w_na3, "bias": bias,
        "w_merge": w_merge, "w_out": rowsof(f["w_out"]), "w_router": rowsof(w_router), "b_router": b_router,
        "w_gate_up": w_gate_up, "w_down": f["expert_w_down"].reshape(NE, FE // P, P, D).transpose(0, 2, 1, 3),
        **{n: f[n].reshape(1, D) for n in ("ln0_g", "ln0_b", "ln1_g", "ln1_b", "ln2_g", "ln2_b")},
    }
    nc = bacc.Bacc("TRN2", target_bir_lowering=False, num_devices=1)
    io = {}
    for name, a in arrays.items():
        arrays[name] = a = np.ascontiguousarray(a)
        io[name] = nc.dram_tensor(f"in_{name}", a.shape, mybir.dt.from_np(a.dtype), kind="ExternalInput").ap()
    for name, shape, dt in SCRATCH:
        io[name] = nc.dram_tensor(f"s_{name}", shape, dt, kind="Internal").ap()
    io["out"] = nc.dram_tensor("out", (SEQ, D), F32, kind="ExternalOutput").ap()
    program(nc, io)
    r = run_bass_kernel_spmd(nc, [{f"in_{n}": a for n, a in arrays.items()}], core_ids=[0])
    return r.results[0]["out"].reshape(1, SEQ, D)


SCRATCH = [
    ("xn", (SEQ, D), F32),
    ("rows", (GH // 2, STEPS, 2, 2, 2, P), F32),
    ("og", (GH, P, SEQ), F32),
    ("ona", (NPAIR, P, SEQ), F32),
    ("merged", (TT, P, DC, P), F32),
    ("h1", (SEQ, D), F32),
    ("token_of", (SLOTS, 1), U32),
    ("y", (SLOTS, D), F32),
]


def program(nc, io):
    with ExitStack() as ctx:
        keep = {
            "con": ctx.enter_context(nc.sbuf_tensor("con", [P, C_W], F32)),
            "colv": ctx.enter_context(nc.sbuf_tensor("colv", [P, V_W], F32)),
        }
        with nc.sbuf_tensor("hT", [P, DC, L], F32) as hT, \
                nc.sbuf_tensor("tab", [P, GH // 2, STEPS, 2, 2, 5], F32) as tab:
            keep["hT"], keep["tab"] = hT, tab
            input_norm(nc, io, keep)
            neighbourhood(nc, io, keep)
            deltanet(nc, io, keep)
            merge(nc, io, keep)
        with nc.sbuf_tensor("logits", [P, TT, NG + NE], F32) as logits, \
                nc.sbuf_tensor("slot", [P, 2, TT], U32) as slot, \
                nc.sbuf_tensor("weight", [P, 2, TT], F32) as weight, \
                nc.sbuf_tensor("owner", [1, NBLK + 1], I32) as owner:
            keep.update(logits=logits, slot=slot, weight=weight, owner=owner)
            first_norm(nc, io, keep)
            route(nc, io, keep)
            experts(nc, io, keep)
            last_norm(nc, io, keep)
```
